# Optimizing a Trainium2 kernel written in Bass

```python
import jax, jax.numpy as jnp
from jax import lax
import numpy as np

D_MODEL = 1024
BATCH = 1
SEQ = 512
DEPTH = 1

HEAD_DIM = 64
N_ATTN_HEADS = 8
ATTN_WIDTH = N_ATTN_HEADS * HEAD_DIM
N_SGU_GROUPS = 8
SGU_GROUP_DIM = 64
SGU_WIDTH = N_SGU_GROUPS * SGU_GROUP_DIM
MIX_WIDTH = ATTN_WIDTH + SGU_WIDTH
IN_WIDTH = 3 * ATTN_WIDTH + 2 * SGU_WIDTH
DILATION_PATTERNS = ((128, 1), (512, 4), (2048, 16))
SGU_CHUNK = 128
ROPE_THETA = 500000.0
ROT_DIM = HEAD_DIM // 4
N_GROUPS = 4
EXPERTS_PER_GROUP = 8
TOP_K = 2
EXPERT_FF = 256
LN_EPS = 1e-5
NEG_INF = -1e30
DEEPNORM_ALPHA = (2 * DEPTH) ** 0.25
DEEPNORM_BETA = (8 * DEPTH) ** -0.25


def layer_norm(x, g, b):
    xf = x.astype(jnp.float32)
    mu = jnp.mean(xf, -1, keepdims=True)
    xc = xf - mu
    var = jnp.mean(xc * xc, -1, keepdims=True)
    return xc * lax.rsqrt(var + LN_EPS) * g.astype(jnp.float32) + b.astype(jnp.float32)

def rope_tables(positions):
    inv = ROPE_THETA ** (-jnp.arange(0, ROT_DIM, 2, dtype=jnp.float32) / ROT_DIM)
    ang = positions.astype(jnp.float32)[..., None] * inv
    return jnp.cos(ang)[:, :, None, :], jnp.sin(ang)[:, :, None, :]

def apply_partial_rope(t, cos, sin):
    half = ROT_DIM // 2
    t1, t2 = t[..., :half], t[..., half:ROT_DIM]
    return jnp.concatenate([t1 * cos - t2 * sin, t2 * cos + t1 * sin, t[..., ROT_DIM:]], -1)

def dilated_window_attention(q, k, v, window, dilation):
    B, S, H, Dh = q.shape
    d = dilation
    L = S // d
    w_sub = window // d
    blk = min(w_sub, L)
    nb = -(-L // blk)
    Lp = nb * blk

    def to_blocks(t):
        t = t.reshape(B, L, d, H, Dh)
        t = jnp.pad(t, ((0, 0), (0, Lp - L), (0, 0), (0, 0), (0, 0)))
        return t.reshape(B, nb, blk, d, H, Dh)

    qb, kb, vb = to_blocks(q), to_blocks(k), to_blocks(v)

    def with_prev(t):
        prev = jnp.pad(t, ((0, 0), (1, 0), (0, 0), (0, 0), (0, 0), (0, 0)))[:, :nb]
        return jnp.concatenate([prev, t], axis=2)

    kk, vv = with_prev(kb), with_prev(vb)
    s = jnp.einsum('bnqrhe,bnkrhe->bnrhqk', qb, kk) * (Dh ** -0.5)
    qi = jnp.arange(blk)[:, None]
    kj = jnp.arange(2 * blk)[None, :]
    dist = qi + blk - kj
    key_pos = jnp.arange(nb)[:, None, None] * blk - blk + kj[None]
    valid = (dist >= 0) & (dist <= w_sub) & (key_pos >= 0)
    valid = valid[None, :, None, None]
    s = jnp.where(valid, s, NEG_INF)
    m = jnp.max(s, -1)
    p = jnp.where(valid, jnp.exp(s - m[..., None]), 0.0)
    l = jnp.sum(p, -1)
    m_t = jnp.moveaxis(m, -1, 2)
    l_t = jnp.moveaxis(l, -1, 2)
    o = jnp.einsum('bnrhqk,bnkrhe->bnqrhe', p, vv) / l_t[..., None]
    o = o.reshape(B, Lp, d, H, Dh)[:, :L].reshape(B, S, H, Dh)
    m_t = m_t.reshape(B, Lp, d, H)[:, :L].reshape(B, S, H)
    l_t = l_t.reshape(B, Lp, d, H)[:, :L].reshape(B, S, H)
    return o, m_t, l_t

def dilated_mixture_attention(q, k, v):
    res = [dilated_window_attention(q, k, v, w, d) for (w, d) in DILATION_PATTERNS]
    m_all = jnp.stack([r[1] for r in res], 0)
    l_all = jnp.stack([r[2] for r in res], 0)
    o_all = jnp.stack([r[0] for r in res], 0)
    wts = l_all * jnp.exp(m_all - jnp.max(m_all, 0, keepdims=True))
    o = jnp.sum(wts[..., None] * o_all, 0) / jnp.sum(wts, 0)[..., None]
    B, S, H, Dh = q.shape
    return o.reshape(B, S, H * Dh)

def spatial_gating(u, vs, ln_g, ln_b, w_spatial, b_spatial):
    B, S, _ = u.shape
    u = jax.nn.gelu(u.astype(jnp.float32), approximate=False)
    vs = layer_norm(jax.nn.gelu(vs.astype(jnp.float32), approximate=False), ln_g, ln_b)
    vc = vs.reshape(B, S // SGU_CHUNK, SGU_CHUNK, N_SGU_GROUPS, SGU_GROUP_DIM)
    causal = jnp.tril(jnp.ones((SGU_CHUNK, SGU_CHUNK), jnp.float32))
    w = w_spatial.astype(jnp.float32) * causal
    z = jnp.einsum('gts,bcsge->bctge', w, vc)
    z = z + b_spatial.astype(jnp.float32).T[None, None, :, :, None]
    return u * z.reshape(B, S, SGU_WIDTH)

def hierarchical_moe(h, w_group, b_group, w_expert, b_expert, w_gate_up, w_down):
    B, S, D = h.shape
    t = h.reshape(B * S, D)
    g_logits = (t @ w_group + b_group).astype(jnp.float32)
    p_group = jax.nn.softmax(g_logits, -1)
    g_onehot = jax.nn.one_hot(jnp.argmax(g_logits, -1), N_GROUPS, dtype=jnp.float32)
    p_sel = jnp.sum(p_group * g_onehot, -1)
    e_logits = (jnp.einsum('td,gde->tge', t, w_expert) + b_expert).astype(jnp.float32)
    e_sel = jnp.einsum('tge,tg->te', e_logits, g_onehot)
    top_vals, top_idx = lax.top_k(e_sel, TOP_K)
    top_w = jax.nn.softmax(top_vals, -1)
    e_gate = jnp.einsum('tk,tke->te', top_w,
                        jax.nn.one_hot(top_idx, EXPERTS_PER_GROUP, dtype=jnp.float32))
    gate = g_onehot[:, :, None] * e_gate[:, None, :] * p_sel[:, None, None]
    y = jnp.zeros((B * S, D), jnp.float32)
    for g in range(N_GROUPS):
        gu = jnp.einsum('td,edf->tef', t, w_gate_up[g]).astype(jnp.float32)
        a, b = gu[..., :EXPERT_FF], gu[..., EXPERT_FF:]
        act = jax.nn.silu(a) * b * gate[:, g, :, None]
        y = y + jnp.einsum('tef,efd->td', act, w_down[g].astype(jnp.float32))
    return y.reshape(B, S, D)

def first_inputs(seed: int = 0) -> dict:
    key = jax.random.key(seed)
    ks = jax.random.split(key, 18)
    f32 = jnp.float32
    x = jax.random.normal(ks[0], (BATCH, SEQ, D_MODEL), f32)
    positions = (jax.random.randint(ks[1], (BATCH, 1), 0, 4096, dtype=jnp.int32)
                 + jnp.arange(SEQ, dtype=jnp.int32)[None, :])
    col_scale = jnp.concatenate([jnp.ones((2 * ATTN_WIDTH,), f32),
                                 jnp.full((ATTN_WIDTH,), DEEPNORM_BETA, f32),
                                 jnp.ones((2 * SGU_WIDTH,), f32)])
    w_in = jax.random.normal(ks[2], (DEPTH, D_MODEL, IN_WIDTH), f32) * (D_MODEL ** -0.5) * col_scale
    sgu_ln_g = 1.0 + 0.1 * jax.random.normal(ks[3], (DEPTH, SGU_WIDTH), f32)
    sgu_ln_b = 0.02 * jax.random.normal(ks[4], (DEPTH, SGU_WIDTH), f32)
    w_spatial = jax.random.normal(ks[5], (DEPTH, N_SGU_GROUPS, SGU_CHUNK, SGU_CHUNK), f32) * (SGU_CHUNK ** -0.5)
    b_spatial = 1.0 + 0.1 * jax.random.normal(ks[6], (DEPTH, N_SGU_GROUPS, SGU_CHUNK), f32)
    w_out = jax.random.normal(ks[7], (DEPTH, MIX_WIDTH, D_MODEL), f32) * (MIX_WIDTH ** -0.5) * DEEPNORM_BETA
    ln1_g = 1.0 + 0.1 * jax.random.normal(ks[8], (DEPTH, D_MODEL), f32)
    ln1_b = 0.02 * jax.random.normal(ks[9], (DEPTH, D_MODEL), f32)
    w_group = jax.random.normal(ks[10], (DEPTH, D_MODEL, N_GROUPS), f32) * (D_MODEL ** -0.5)
    b_group = 0.01 * jax.random.normal(ks[11], (DEPTH, N_GROUPS), f32)
    w_expert = jax.random.normal(ks[12], (DEPTH, N_GROUPS, D_MODEL, EXPERTS_PER_GROUP), f32) * (D_MODEL ** -0.5)
    b_expert = 0.01 * jax.random.normal(ks[13], (DEPTH, N_GROUPS, EXPERTS_PER_GROUP), f32)
    w_gate_up = jax.random.normal(ks[14], (DEPTH, N_GROUPS, EXPERTS_PER_GROUP, D_MODEL, 2 * EXPERT_FF), f32) * (D_MODEL ** -0.5)
    w_down = jax.random.normal(ks[15], (DEPTH, N_GROUPS, EXPERTS_PER_GROUP, EXPERT_FF, D_MODEL), f32) * (EXPERT_FF ** -0.5) * DEEPNORM_BETA
    ln2_g = 1.0 + 0.1 * jax.random.normal(ks[16], (DEPTH, D_MODEL), f32)
    ln2_b = 0.02 * jax.random.normal(ks[17], (DEPTH, D_MODEL), f32)
    return {"x": x, "positions": positions, "w_in": w_in, "sgu_ln_g": sgu_ln_g,
            "sgu_ln_b": sgu_ln_b, "w_spatial": w_spatial, "b_spatial": b_spatial,
            "w_out": w_out, "ln1_g": ln1_g, "ln1_b": ln1_b, "w_group": w_group,
            "b_group": b_group, "w_expert": w_expert, "b_expert": b_expert,
            "w_gate_up": w_gate_up, "w_down": w_down, "ln2_g": ln2_g, "ln2_b": ln2_b}

def first_block(x, positions, w_in, sgu_ln_g, sgu_ln_b, w_spatial, b_spatial, w_out,
              ln1_g, ln1_b, w_group, b_group, w_expert, b_expert, w_gate_up, w_down,
              ln2_g, ln2_b):
    B, S, _ = x.shape
    cos, sin = rope_tables(positions)
    h = x.astype(jnp.float32)
    for layer in range(DEPTH):
        proj = h @ w_in[layer]
        a0 = ATTN_WIDTH
        q = proj[..., 0:a0].reshape(B, S, N_ATTN_HEADS, HEAD_DIM).astype(jnp.float32)
        k = proj[..., a0:2 * a0].reshape(B, S, N_ATTN_HEADS, HEAD_DIM).astype(jnp.float32)
        v = proj[..., 2 * a0:3 * a0].reshape(B, S, N_ATTN_HEADS, HEAD_DIM).astype(jnp.float32)
        u = proj[..., 3 * a0:3 * a0 + SGU_WIDTH]
        vs = proj[..., 3 * a0 + SGU_WIDTH:]
        q = apply_partial_rope(q, cos, sin)
        k = apply_partial_rope(k, cos, sin)
        attn_out = dilated_mixture_attention(q, k, v)
        sgu_out = spatial_gating(u, vs, sgu_ln_g[layer], sgu_ln_b[layer],
                                 w_spatial[layer], b_spatial[layer])
        mix = jnp.concatenate([attn_out, sgu_out], -1) @ w_out[layer].astype(jnp.float32)
        h = layer_norm(DEEPNORM_ALPHA * h + mix, ln1_g[layer], ln1_b[layer])
        moe = hierarchical_moe(h, w_group[layer], b_group[layer], w_expert[layer],
                               b_expert[layer], w_gate_up[layer], w_down[layer])
        h = layer_norm(DEEPNORM_ALPHA * h + moe, ln2_g[layer], ln2_b[layer])
    return h.astype(x.dtype)


DEPTH_2 = 2

GRID_W = 64
NA_HEADS = D_MODEL // (4 * HEAD_DIM)
NA_WIN_H = 8
NA_WIN_W = 16
MLA_HEADS = 3 * D_MODEL // (8 * HEAD_DIM)
MLA_Q_LORA = D_MODEL // 4
MLA_KV_LORA = D_MODEL // 8
MLA_NOPE = 64
MLA_ROPE = 32
MLA_V = 64
MLA_BLOCK = 128
SWA_HEADS = 3 * D_MODEL // (8 * HEAD_DIM)
SWA_KV_HEADS = 2
SWA_WINDOW = 128
SWA_BLOCK = 128
ROPE_THETA_2 = 10000.0
N_EXPERTS = 16
EC_CAPACITY = 2
D_EXPERT = D_MODEL
RMS_EPS = 1e-6
NEG_INF_2 = -1e30

A_W = NA_HEADS * HEAD_DIM
B_W = MLA_HEADS * MLA_V
C_W = SWA_HEADS * HEAD_DIM
D_MIX = A_W + B_W + C_W
IN_WIDTHS = (A_W, A_W, A_W,
             MLA_Q_LORA, MLA_KV_LORA, MLA_ROPE,
             SWA_HEADS * HEAD_DIM, SWA_KV_HEADS * HEAD_DIM, SWA_KV_HEADS * HEAD_DIM)
IN_COLS = sum(IN_WIDTHS)
IN_OFFSETS = tuple(int(v) for v in np.cumsum(IN_WIDTHS)[:-1])


def rms_norm(x, g):
    x32 = x.astype(jnp.float32)
    y = x32 * lax.rsqrt(jnp.mean(x32 * x32, axis=-1, keepdims=True) + RMS_EPS)
    return (y * g.astype(jnp.float32)).astype(x.dtype)

def rope_tables_2(seq, dim, dtype):
    inv = 1.0 / (ROPE_THETA_2 ** (jnp.arange(0, dim, 2, dtype=jnp.float32) / dim))
    ang = jnp.arange(seq, dtype=jnp.float32)[:, None] * inv[None, :]
    return jnp.cos(ang).astype(dtype), jnp.sin(ang).astype(dtype)

def apply_rope(x, cos, sin):
    x1, x2 = jnp.split(x, 2, axis=-1)
    c = cos[None, :, None, :]
    s = sin[None, :, None, :]
    return jnp.concatenate([x1 * c - x2 * s, x2 * c + x1 * s], axis=-1)

def neighbourhood_attention(q, k, v, rpb):
    B, S, _ = q.shape
    rows = S // GRID_W
    wh = min(NA_WIN_H, rows)
    ww = NA_WIN_W
    shp = (B, rows, GRID_W, NA_HEADS, HEAD_DIM)
    qg, kg, vg = q.reshape(shp), k.reshape(shp), v.reshape(shp)
    cols = jnp.arange(GRID_W)
    col_start = jnp.clip(cols - ww // 2, 0, GRID_W - ww)
    col_idx = col_start[:, None] + jnp.arange(ww)[None, :]
    dc = col_idx - cols[:, None] + (NA_WIN_W - 1)
    scale = HEAD_DIM ** -0.5

    def one_row(args):
        r, q_row = args
        rs = jnp.clip(r - wh // 2, 0, rows - wh)
        k_rows = lax.dynamic_slice_in_dim(kg, rs, wh, axis=1)
        v_rows = lax.dynamic_slice_in_dim(vg, rs, wh, axis=1)
        k_win = k_rows[:, :, col_idx]
        v_win = v_rows[:, :, col_idx]
        dr = rs + jnp.arange(wh) - r + (NA_WIN_H - 1)
        bias = rpb[:, dr][:, :, dc].transpose(0, 2, 1, 3)
        s = jnp.einsum('bchd,brcjhd->bhcrj', q_row, k_win).astype(jnp.float32) * scale
        s = s + bias[None].astype(jnp.float32)
        p = jax.nn.softmax(s.reshape(B, NA_HEADS, GRID_W, wh * ww), axis=-1)
        p = p.reshape(s.shape).astype(v.dtype)
        return jnp.einsum('bhcrj,brcjhd->bchd', p, v_win)

    out = lax.map(one_row, (jnp.arange(rows), qg.swapaxes(0, 1)))
    return out.swapaxes(0, 1).reshape(B, S, NA_HEADS * HEAD_DIM)

def latent_attention(c_q, c_kv, k_rope, q_norm, w_uq, kv_norm, w_ukv, cos_r, sin_r):
    B, S, _ = c_q.shape
    q = (rms_norm(c_q, q_norm) @ w_uq).reshape(B, S, MLA_HEADS, MLA_NOPE + MLA_ROPE)
    q_nope = q[..., :MLA_NOPE]
    q_pe = apply_rope(q[..., MLA_NOPE:], cos_r, sin_r)
    kv = (rms_norm(c_kv, kv_norm) @ w_ukv).reshape(B, S, MLA_HEADS, MLA_NOPE + MLA_V)
    k_nope = kv[..., :MLA_NOPE]
    v = kv[..., MLA_NOPE:]
    k_pe = apply_rope(k_rope[:, :, None, :], cos_r, sin_r)[:, :, 0]
    nb = S // MLA_BLOCK
    scale = (MLA_NOPE + MLA_ROPE) ** -0.5

    def to_blocks(t):
        return t.reshape(B, nb, MLA_BLOCK, *t.shape[2:]).swapaxes(0, 1)

    def one_block(args):
        qn, qp = args
        s = (jnp.einsum('bqhd,bkhd->bhqk', qn, k_nope)
             + jnp.einsum('bqhd,bkd->bhqk', qp, k_pe)).astype(jnp.float32) * scale
        p = jax.nn.softmax(s, axis=-1).astype(v.dtype)
        return jnp.einsum('bhqk,bkhd->bqhd', p, v)

    o = lax.map(one_block, (to_blocks(q_nope), to_blocks(q_pe)))
    return o.swapaxes(0, 1).reshape(B, S, MLA_HEADS * MLA_V)

def window_gqa(q, k, v, sink, cos, sin):
    B, S, _ = q.shape
    G = SWA_HEADS // SWA_KV_HEADS
    q = apply_rope(q.reshape(B, S, SWA_HEADS, HEAD_DIM), cos, sin)
    k = apply_rope(k.reshape(B, S, SWA_KV_HEADS, HEAD_DIM), cos, sin)
    v = v.reshape(B, S, SWA_KV_HEADS, HEAD_DIM)
    nb = S // SWA_BLOCK
    n_side = -(-SWA_WINDOW // SWA_BLOCK)
    pad = n_side * SWA_BLOCK
    n_keys = (2 * n_side + 1) * SWA_BLOCK

    def band(t):
        tp = jnp.pad(t, ((0, 0), (pad, pad), (0, 0), (0, 0)))
        tp = tp.reshape(B, nb + 2 * n_side, SWA_BLOCK, SWA_KV_HEADS, HEAD_DIM)
        return jnp.concatenate([tp[:, i:i + nb] for i in range(2 * n_side + 1)], axis=2)

    kb, vb = band(k), band(v)
    qb = q.reshape(B, nb, SWA_BLOCK, SWA_KV_HEADS, G, HEAD_DIM)
    s = jnp.einsum('bnqkgd,bnjkd->bnkgqj', qb, kb).astype(jnp.float32) * (HEAD_DIM ** -0.5)
    blk = jnp.arange(nb)[:, None, None] * SWA_BLOCK
    qpos = blk + jnp.arange(SWA_BLOCK)[None, :, None]
    kpos = blk - pad + jnp.arange(n_keys)[None, None, :]
    valid = (jnp.abs(qpos - kpos) <= SWA_WINDOW) & (kpos >= 0) & (kpos < S)
    s = jnp.where(valid[None, :, None, None], s, NEG_INF_2)
    sink_logit = jnp.broadcast_to(sink.astype(jnp.float32).reshape(1, 1, SWA_KV_HEADS, G, 1, 1),
                                  s.shape[:-1] + (1,))
    p = jax.nn.softmax(jnp.concatenate([s, sink_logit], axis=-1), axis=-1)[..., :-1].astype(v.dtype)
    o = jnp.einsum('bnkgqj,bnjkd->bnqkgd', p, vb)
    return o.reshape(B, S, SWA_HEADS * HEAD_DIM)

def expert_choice_ffn(xn, w_router, w_gate, w_up, w_down):
    B, S, D = xn.shape
    cap = EC_CAPACITY * S // N_EXPERTS
    aff = jax.nn.softmax((xn @ w_router).astype(jnp.float32), axis=-1)
    g, idx = lax.top_k(aff.swapaxes(1, 2), cap)
    bidx = jnp.arange(B)[:, None, None]
    xs = xn[bidx, idx]
    hid = jax.nn.silu(jnp.einsum('becd,edf->becf', xs, w_gate)) * jnp.einsum('becd,edf->becf', xs, w_up)
    y = jnp.einsum('becf,efd->becd', hid, w_down) * g[..., None].astype(xn.dtype)
    return jnp.zeros_like(xn).at[bidx, idx].add(y)

def second_inputs(seed: int = 0) -> dict:
    key = jax.random.key(seed)
    ks = jax.random.split(key, 17)
    f32 = jnp.float32

    def nrm(k, shape, scale):
        return jax.random.normal(k, shape, f32) * scale

    def gain(k, shape):
        return 1.0 + 0.05 * jax.random.normal(k, shape, f32)

    return {
        'x': nrm(ks[0], (BATCH, SEQ, D_MODEL), 1.0),
        'attn_norm': gain(ks[1], (DEPTH_2, D_MODEL)),
        'w_in': nrm(ks[2], (DEPTH_2, D_MODEL, IN_COLS), D_MODEL ** -0.5),
        'na_rpb': nrm(ks[3], (DEPTH_2, NA_HEADS, 2 * NA_WIN_H - 1, 2 * NA_WIN_W - 1), 0.1),
        'mla_q_norm': gain(ks[4], (DEPTH_2, MLA_Q_LORA)),
        'mla_w_uq': nrm(ks[5], (DEPTH_2, MLA_Q_LORA, MLA_HEADS * (MLA_NOPE + MLA_ROPE)), MLA_Q_LORA ** -0.5),
        'mla_kv_norm': gain(ks[6], (DEPTH_2, MLA_KV_LORA)),
        'mla_w_ukv': nrm(ks[7], (DEPTH_2, MLA_KV_LORA, MLA_HEADS * (MLA_NOPE + MLA_V)), MLA_KV_LORA ** -0.5),
        'swa_sink': nrm(ks[8], (DEPTH_2, SWA_HEADS), 1.0),
        'group_norm': gain(ks[9], (DEPTH_2, D_MIX)),
        'w_out': nrm(ks[10], (DEPTH_2, D_MIX, D_MODEL), D_MIX ** -0.5),
        'ffn_norm': gain(ks[11], (DEPTH_2, D_MODEL)),
        'w_router': nrm(ks[12], (DEPTH_2, D_MODEL, N_EXPERTS), D_MODEL ** -0.5),
        'w_gate': nrm(ks[13], (DEPTH_2, N_EXPERTS, D_MODEL, D_EXPERT), D_MODEL ** -0.5),
        'w_up': nrm(ks[14], (DEPTH_2, N_EXPERTS, D_MODEL, D_EXPERT), D_MODEL ** -0.5),
        'w_down': nrm(ks[15], (DEPTH_2, N_EXPERTS, D_EXPERT, D_MODEL), D_EXPERT ** -0.5),
        'final_norm': gain(ks[16], (D_MODEL,)),
    }

def second_block(x, attn_norm, w_in, na_rpb, mla_q_norm, mla_w_uq, mla_kv_norm, mla_w_ukv, swa_sink,
              group_norm, w_out, ffn_norm, w_router, w_gate, w_up, w_down, final_norm):
    B, S, _ = x.shape
    cos, sin = rope_tables_2(S, HEAD_DIM, x.dtype)
    cos_r, sin_r = rope_tables_2(S, MLA_ROPE, x.dtype)
    h = x
    for l in range(DEPTH_2):
        xn = rms_norm(h, attn_norm[l])
        proj = xn @ w_in[l]
        a_q, a_k, a_v, b_cq, b_ckv, b_kr, c_q, c_k, c_v = jnp.split(proj, IN_OFFSETS, axis=-1)
        o_a = neighbourhood_attention(a_q, a_k, a_v, na_rpb[l])
        o_b = latent_attention(b_cq, b_ckv, b_kr, mla_q_norm[l], mla_w_uq[l],
                               mla_kv_norm[l], mla_w_ukv[l], cos_r, sin_r)
        o_c = window_gqa(c_q, c_k, c_v, swa_sink[l], cos, sin)
        gn = group_norm[l]
        o = jnp.concatenate([rms_norm(o_a, gn[:A_W]),
                             rms_norm(o_b, gn[A_W:A_W + B_W]),
                             rms_norm(o_c, gn[A_W + B_W:])], axis=-1)
        h = h + o @ w_out[l]
        h = h + expert_choice_ffn(rms_norm(h, ffn_norm[l]), w_router[l], w_gate[l], w_up[l], w_down[l])
    return rms_norm(h, final_norm)


def setup_inputs(seed=0):
    out = dict(first_inputs(seed))
    for name, value in second_inputs(seed + 1).items():
        if name != "x":
            out[name + "_2"] = value
    return out


def reference(
    x, positions, w_in, sgu_ln_g, sgu_ln_b, w_spatial, b_spatial, w_out, ln1_g, ln1_b, w_group,
    b_group, w_expert, b_expert, w_gate_up, w_down, ln2_g, ln2_b, attn_norm_2, w_in_2, na_rpb_2,
    mla_q_norm_2, mla_w_uq_2, mla_kv_norm_2, mla_w_ukv_2, swa_sink_2, group_norm_2, w_out_2,
    ffn_norm_2, w_router_2, w_gate_2, w_up_2, w_down_2, final_norm_2,
):
    x = first_block(
        x, positions, w_in, sgu_ln_g, sgu_ln_b, w_spatial, b_spatial, w_out, ln1_g, ln1_b,
        w_group, b_group, w_expert, b_expert, w_gate_up, w_down, ln2_g, ln2_b,
    )
    return second_block(
        x, attn_norm_2, w_in_2, na_rpb_2, mla_q_norm_2, mla_w_uq_2, mla_kv_norm_2, mla_w_ukv_2,
        swa_sink_2, group_norm_2, w_out_2, ffn_norm_2, w_router_2, w_gate_2, w_up_2, w_down_2,
        final_norm_2,
    )


_drawn_inputs = setup_inputs


def setup_inputs(seed=0):
    import zlib

    import numpy as np

    out = dict(_drawn_inputs(seed))
    spreads = {}
    factors = {'sgu_ln_b': 6.145,
     'b_group': 6.335,
     'b_expert': 6.827,
     'mla_q_norm_2': 3.256,
     'swa_sink_2': 8.0}
    for name, (base, spread) in spreads.items():
        noise = np.random.default_rng([zlib.crc32(name.encode()), seed]).standard_normal(out[name].shape)
        drawn = base * np.exp(spread * noise) if base else spread * noise
        out[name] = __import__('jax').numpy.asarray(drawn.astype(out[name].dtype))
    for name, factor in factors.items():
        out[name] = (out[name] * factor).astype(out[name].dtype)
    return out
```

```python
from contextlib import ExitStack

import concourse.bass as bass
import numpy as np
from concourse import mybir

ALU = mybir.AluOpType
ACT = mybir.ActivationFunctionType
F32 = mybir.dt.float32
I32 = mybir.dt.int32
AX_X = mybir.AxisListType.X

P = 128
S = 512
T = S // P
D = 1024
K = D // P
HD = 64
BIG = 1e30
HUGE = 3e38
LN_EPS = 1e-5
RMS_EPS = 1e-6
ALPHA = 2 ** 0.25
C = 64

RING = 6
SLOT_COLS = K * 512

H1 = 8
G1, E1, F1 = 4, 8, 256
NE1 = G1 * E1
LAYERS = 2
NE2 = 16
F2 = D
CAP2 = 2 * S // NE2
MLA_H, MLA_D, MLA_ROPE = 6, 96, 32
NA_H, SWA_H = 4, 6
GW = 64
GH = S // GW
RPB_ROW, RPB_COLS = 31, 15 * 31
RPB_PAD = 64
RPB_LEN = NA_H * RPB_COLS + 2 * RPB_PAD
BT_ROWS = 2 * GH - 2

BASE_COLS = dict(ident=P, ones=P, upto=P, iota=C, rank=8)
FIRST_COLS = dict(logcount=S, rot=P, inv=1)
SECOND_COLS = dict(rot=P, rot_mla=MLA_ROPE, cos=S, sin=S, cos_mla=S, sin_mla=S, band=3 * P, window=GW)


def places(cols):
    at, out = 0, {}
    for name, n in cols.items():
        out[name] = (at, at + n)
        at += n
    return out, at


BASE_AT, BASE_N = places(BASE_COLS)
FIRST_AT, FIRST_N = places(FIRST_COLS)
SECOND_AT, SECOND_N = places(SECOND_COLS)


def rotation(half, width):
    m = np.zeros((P, P), np.float32)
    for h in range(0, P, width):
        for i in range(half):
            m[h + half + i, h + i] = -1.0
            m[h + i, h + half + i] = 1.0
    return m


def rope_table(dim, rows):
    inv = np.float32(1.0) / (np.float32(10000.0) ** (np.arange(0, dim, 2, dtype=np.float32) / np.float32(dim)))
    ang = np.arange(S, dtype=np.float32)[None, :] * inv.astype(np.float32)[:, None]
    reps = rows // (dim // 2)
    return np.tile(np.cos(ang), (reps, 1)).astype(np.float32), np.tile(np.sin(ang), (reps, 1)).astype(np.float32)


def shape_constants():
    p = np.arange(P)[:, None]
    base = np.zeros((P, BASE_N), np.float32)
    put = lambda a, at, name, v: a.__setitem__((slice(None), slice(*at[name])), v)
    put(base, BASE_AT, "ident", np.eye(P))
    put(base, BASE_AT, "ones", 1.0)
    put(base, BASE_AT, "upto", p <= np.arange(P)[None, :])
    put(base, BASE_AT, "iota", np.arange(1, C + 1)[None, :])
    put(base, BASE_AT, "rank", np.arange(8, 0, -1)[None, :])

    first = np.zeros((P, FIRST_N), np.float32)
    dist = p + (T - 1) * P - np.arange(S)[None, :]
    n = (dist <= 128) * 1 + (dist % 4 == 0) * 1 + (dist % 16 == 0) * 1
    put(first, FIRST_AT, "logcount", np.where((dist >= 0) & (n > 0), -np.log(np.maximum(n, 1)), BIG))
    put(first, FIRST_AT, "rot", rotation(8, HD))
    inv = (np.float32(500000.0) ** (-np.arange(0, 16, 2, dtype=np.float32) / np.float32(16))).astype(np.float32)
    d = np.arange(P) % HD
    put(first, FIRST_AT, "inv", np.where(d < 16, inv[d % 8], 0.0)[:, None])

    second = np.zeros((P, SECOND_N), np.float32)
    put(second, SECOND_AT, "rot", rotation(HD // 2, HD))
    put(second, SECOND_AT, "rot_mla", rotation(MLA_ROPE // 2, MLA_ROPE)[:, HD:HD + MLA_ROPE])
    c, s = rope_table(HD, P)
    put(second, SECOND_AT, "cos", c)
    put(second, SECOND_AT, "sin", s)
    c, s = rope_table(MLA_ROPE, P)
    put(second, SECOND_AT, "cos_mla", c)
    put(second, SECOND_AT, "sin_mla", s)
    put(second, SECOND_AT, "band", np.where(np.abs(p + P - np.arange(3 * P)[None, :]) <= P, 0.0, BIG))
    col, key = np.arange(P)[:, None] % GW, np.arange(GW)[None, :]
    start = np.clip(col - 8, 0, GW - 16)
    put(second, SECOND_AT, "window", np.where((key >= start) & (key < start + 16), 0.0, BIG)[:, ::-1])
    return base, first, second


PROJ1 = [("qk", 0)]
for _c in range(1, 8):
    PROJ1 += [("qk", _c), ("rot", _c - 1)]
PROJ1 += [("v", 0), ("rot", 7)] + [("v", t) for t in range(1, T)]
PROJ1 += [("u", c) for c in range(4)] + [("gate", t) for t in range(T)]
PROJ1_ACT = ("qk", "u", "gate")

PROJ2 = [("cq", 0), ("cq", 1), ("ckv", 0), ("kr", 0), ("ssq", 0), ("na", 0), ("ssq", 1), ("krrot", 0), ("na", 1)]
PROJ2 += [("uq", h) for h in range(MLA_H)] + [("na", 2)] + [("uqrot", h) for h in range(MLA_H)]
PROJ2 += [("na", 3)] + [("uk", h) for h in range(MLA_H)] + [("swa", 0)] + [("uv", t) for t in range(T)]
PROJ2 += [("swa", 1), ("swarot", 0), ("swa", 2), ("swarot", 1), ("swa", 3), ("swarot", 2), ("va", 0), ("swarot", 3)]
PROJ2 += [("va", t) for t in range(1, T)]
PROJ2_ACT = ("cq", "ckv", "kr", "na", "ssq", "uq", "uv", "swa")

HEADS1 = [("dilated", h) for h in range(H1)]
HEADS2 = [("mla", h) for h in range(MLA_H)] + [("swa", h) for h in range(SWA_H)] + [("na", h) for h in range(NA_H)]


def first_key(kind, t):
    return max(t - 1, 0) if kind == "swa" else 0


def end_key(kind, t):
    return {"dilated": t + 1, "swa": min(t + 2, T)}.get(kind, T)


def nth(plan, takers, i):
    mine = plan[i][0] in takers
    return sum((w in takers) == mine for w, _ in plan[:i + 1])


IN2 = [(1024, 416), (0, 512), (512, 512), (1440, 384)]
SLOT_OF2 = {0: ("cq", "ckv", "kr"), 1: ("na",), 2: ("swa",), 3: ("va",)}
GROUPS2 = ((0, 256), (256, 640), (640, 1024))
TWO_PI_PARTS = (6.28125, 0.0019340515136718750, float(2 * np.pi - 6.28125 - 0.0019340515136718750))
PI_BELOW = 3.1415925
DVE2 = 60


def last_of(plan, what, i):
    return plan.index((what, i))


class Signal:

    def __init__(self, sem, per=0, first=0):
        self.sem, self.per, self.first = sem, per, first

    def at(self, n, l=0):
        return l * self.per + (self.first + n)


class Steps:

    def __init__(self, sem, base=0):
        self.sem, self.base, self.n = sem, base, 0

    def next(self):
        self.n += 1
        return self.base + self.n


def build(nc, a, out):
    with ExitStack() as ctx:
        def sb(name, cols, dt=F32):
            return ctx.enter_context(nc.sbuf_tensor(name, [P, cols], dt))

        def sem(name):
            return ctx.enter_context(nc.semaphore(name))

        def sig(name, per=0):
            return Signal(sem(name), per)

        def split(ap, **n):
            (name, count), = n.items()
            return ap.rearrange(f"p ({name} x) -> p {name} x", **{name: count})

        def spread(ap, axis, n):
            v = ap.unsqueeze(axis)
            shape = list(v.shape)
            shape[axis] = n
            return v.to_broadcast(shape)

        h_sb = sb("h", T * D)
        x_sb = sb("xT_or_o", K * S)
        arena = sb("arena", 14848)
        tables = sb("tables", SECOND_N)
        probs = sb("probs", 4 * S)
        base = sb("base", BASE_N)
        small = sb("small", 320 + 33 * LAYERS)
        rounds_i = sb("rounds", 1, I32)
        ring = sb("ring", RING * SLOT_COLS)
        bank = [ctx.enter_context(nc.psum_tensor(f"bank{i}", [P, 512], F32)) for i in range(8)]

        h = split(h_sb[:, :], t=T)
        xT = split(x_sb[:, :], k=K)
        slot = [split(ring[:, i * SLOT_COLS:(i + 1) * SLOT_COLS], k=K) for i in range(RING)]
        ident, ones, upto, iota, rank = (base[:, slice(*BASE_AT[n])] for n in ("ident", "ones", "upto", "iota", "rank"))

        def area(start, n, **parts):
            v = arena[:, start:start + n]
            return split(v, **parts) if parts else v

        def tab(at, name):
            return tables[:, slice(*at[name])]

        qk1 = area(0, 4096, k=8)
        v1 = area(4096, 2048, t=T)
        u1 = area(6144, 2048, k=4)
        g1 = area(8192, 2048, t=T)
        mix1 = area(10240, 4096, k=8)
        ln1g, ln1b = area(6144, 1024), area(7168, 1024)
        ang, turns, sin_arg, cos_arg = (area(8192 + 512 * i, 512) for i in range(4))
        turns_i = area(10240, 512).bitcast(I32)
        over = area(10752, 512)
        pos_i = area(11264, 512).bitcast(I32)
        o = FIRST_N + 7 & ~7
        cos1, sin1 = tables[:, o:o + 512], tables[:, o + 512:o + 1024]
        bsp = split(tables[:, o + 1024:o + 1536], c=4)
        o1 = split(x_sb[:, 0:2048], t=T)
        wsT = split(x_sb[:, 2048:3072], g=8)
        sgu_g, sgu_b = probs[:, 0:512], probs[:, 512:1024]
        rot_tmp = probs[:, 1024:1536]
        ln2g, ln2b = probs[:, 0:1024], probs[:, 1024:2048]

        qk2 = area(0, 10240, k=20)
        va = area(10240, 1536, t=T)
        vm = area(11776, 1536, t=T)
        cq = area(13312, 1536, k=3)
        sq = area(11776, 1536, k=3)
        rs = area(10240, 1024, k=2)
        wuq = area(2048, 1152, k=2)
        wukv = area(3200, 768)
        kr_raw, kr_new = probs[:, 0:512], probs[:, 512:1024]
        o2 = split(x_sb[:, :], t=T)
        oT2 = area(0, 4096, k=8)
        junk = area(4096, 4096, t=T)
        bt = [tables[:, SECOND_AT[n][0]:SECOND_AT[n][0] + BT_ROWS * GW] for n in ("cos", "cos_mla")]
        fin_g = area(8192, 1024)
        fin_o = area(0, 4096, t=T)

        prob = [probs[:, 0:512], probs[:, 512:1024]]
        probT = [probs[:, 1024:1536], probs[:, 1536:2048]]

        xn = area(0, 4096, t=T)
        sel = area(4096, 512, t=T)
        selg = area(4608, 512, t=T)
        selgT = area(5120, 512)
        xs = area(5632, 1024, k=K)
        silu = area(6656, 512)
        hid = area(7168, 512)
        hidT = area(7680, 512)
        ys = area(8192, 1024)
        place = area(10752, 128)
        gate = area(10880, 128)
        rt = 11008
        logits = area(rt, 144, t=T)
        pick = [area(rt + 144 * (i + 1), 144) for i in range(3)]
        mask_s = area(rt + 576, 128)
        affT, workT, maskT = (area(rt + 704 + 512 * i, 512) for i in range(3))
        top8 = area(rt + 2240, 8)
        mask1_w = workT[:, 0:128]
        router1_w = area(13264, K * 36, k=K)
        router2_w = area(13264, K * NE2, k=K)

        negmax, total = small[:, 0:64], small[:, 64:128]
        ss, std, rstd = small[:, 128:140], small[:, 140:152], small[:, 152:164]
        layer_cols = small[:, 164:197]
        gains = split(small[:, 164:188], k=3)
        lat_g = small[:, 188:191]
        all_cols = small[:, 320:320 + 33 * LAYERS]
        sink, nsink, esink = small[:, 191:197], small[:, 197:203], small[:, 203:207]
        rtotal = small[:, 207:211]
        eps_ln, eps_rms = small[:, 211:212], small[:, 212:213]
        bias36 = small[:, 213:249]
        bn = small[:, 249:261]
        mv = small[:, 261:269]
        col = [small[:, 269 + 4 * i:273 + 4 * i] for i in range(12)]


        def view1(kind, i):
            keys = mix1[:, i // 2, :] if i % 2 else qk1[:, 4 + i // 2, :]
            return qk1[:, i // 2, :], keys, lambda c: v1[:, c, i // 2 * P:i // 2 * P + P]

        def view2(kind, i):
            if kind == "mla":
                return qk2[0:MLA_D, 8 + i, :], qk2[0:MLA_D, 14 + i, :], lambda c: vm[:, c, i // 2 * P:i // 2 * P + P]
            if kind == "swa":
                return qk2[:, 4 + i % 3, :], cq[:, 2, :] if i // 3 else qk2[:, 7, :], lambda c: va[:, c, 256:384]
            keys = cq[:, i // 2, :] if i % 2 else qk2[:, 2 + i // 2, :]
            return qk2[:, i // 2, :], keys, lambda c: va[:, c, i // 2 * P:i // 2 * P + P]

        def second_of_two(kind, i):
            return i // 3 if kind == "swa" else i % 2

        def table1(kind, i, t):
            return tab(FIRST_AT, "logcount")[:, (T - 1 - t) * P:]

        def table2(kind, i, t):
            if kind == "swa":
                y = (first_key(kind, t) - t + 1) * P
                return tab(SECOND_AT, "band")[:, y:y + (end_key(kind, t) - first_key(kind, t)) * P]
            b = bt[i % 2]
            return bass.AP(b.tensor, b.offset + (GH - 2 - 2 * t) * GW + GW - 1, [list(b.ap[0]), [GW, GH], [-1, GW]])

        def place2(kind, i):
            c0 = {"na": 0, "mla": 256, "swa": 640}[kind] + i * HD
            return o2[:, :, c0:c0 + HD]

        def mask_of(n):
            return split(mask_s[:, 0:T * n], t=T)

        landed1 = [sem(f"landed1_{i}") for i in range(RING)]
        landed2 = [sem(f"landed2_{i}") for i in range(RING)]
        x_in, h_in, base_in, first_in, pos_in = (sig(n) for n in ("x_in", "h_in", "base_in", "first_in", "pos_in"))
        sgu_in, ws_in, bsp_in, ln1_in, ln2_in, rt1_in = (
            sig(n) for n in ("sgu_in", "ws_in", "bsp_in", "ln1_in", "ln2_in", "rt1_in"))
        sin_args, rope1, dve1 = (sig(n) for n in ("sin_args", "rope1", "dve1"))
        proj1, took1_a, took1_v, qk1_ready, padded1 = (
            sig(n) for n in ("proj1", "took1_a", "took1_v", "qk1_ready", "padded1"))
        g1_var, g1_std, g1_ready = (sig(n) for n in ("g1_var", "g1_std", "g1_ready"))

        def attention_signals(n, heads):
            m = T * len(heads) if n == 2 else 0
            return {name: sig(f"{name}{n}", m // div) for name, div in dict(
                score=1, shifted=1, prob=1, turned=1, probT_v=2, probT_a=2, pv=1, head_out=4).items()}

        att1, att2 = attention_signals(1, HEADS1), attention_signals(2, HEADS2)
        sunk = sig("sunk", SWA_H)
        oT_mm, oT_a, oT_v, sgu_mm, sgu_ok, ws_masked = (
            sig(n) for n in ("oT_mm", "oT_a", "oT_v", "sgu_mm", "sgu_ok", "ws_masked"))
        wo1_mm, h1_sum, h1_var, h1_std, h1_ready = (
            sig(n) for n in ("wo1_mm", "h1_sum", "h1_var", "h1_std", "h1_ready"))
        r1_mm, r1_a, r1_v, lg1_mm, ex1_in, ex1_out, mask1, cum1_mm, places1 = (
            sig(n) for n in ("r1_mm", "r1_a", "r1_v", "lg1_mm", "ex1_in", "ex1_out", "mask1", "cum1_mm", "places1"))

        def expert_signals(n):
            return {name: sig(f"{name}{n}") for name in (
                "sel", "selg", "gath", "xs", "gu", "silu", "hid", "hT", "hT_ok", "dn", "selgT", "selgT_ok", "ys",
                "scat", "added")}

        ex1, ex2 = expert_signals(1), expert_signals(2)
        next_round = sig("next_round")
        h2_var, h2_std = sig("h2_var"), sig("h2_std")
        layer_done = sig("layer_done", 1)
        cols_ready = sig("cols_ready", 1)
        second_in, ukv_in, gains_in, rt2_in = sig("second_in", 16), sig("ukv_in", 32), sig("gains_in"), sig("rt2_in", 16)
        bias_in, bias_ready = [sig("bias_in0", 64), sig("bias_in1", 64)], sig("bias_ready", NA_H)

        norm_sems = {name: sem(f"norm_{name}") for name in ("ss", "std", "x", "mm", "a", "v")}

        def norm_signals(stage):
            return {name: Signal(norm_sems[name], 3 * m, stage * m) for name, m in dict(
                ss=1, std=1, x=T, mm=K, a=K // 2, v=K // 2).items()}

        nrm, gnm, fnm = (norm_signals(stage) for stage in range(3))
        fin = {"ss": sig("fin_ss"), "std": sig("fin_std")}
        proj2 = sig("proj2", len(PROJ2))
        took2_a = sig("took2_a", sum(w in PROJ2_ACT for w, _ in PROJ2))
        took2_v = sig("took2_v", sum(w not in PROJ2_ACT for w, _ in PROJ2))
        lat_ready, kpe_ready, keys_set, rope2 = (sig(n, p) for n, p in (
            ("lat_ready", 3), ("kpe_ready", 1), ("keys_set", MLA_H + 3), ("rope2", MLA_H + 4)))
        wo2_mm, h2_sum = sig("wo2_mm", 2 * T), sig("h2_sum", 2 * T)
        lg2_mm, ex2_in, ex2_out, aff_ready, affT_mm, maskT_ready, mask_mm, mask2, cum2_mm, places2 = (
            sig(n, 1) for n in ("lg2_mm", "ex2_in", "ex2_out", "aff_ready", "affT_mm", "maskT_ready", "mask_mm",
                                "mask2", "cum2_mm", "places2"))
        fin_in, fin_ready, stored = (sig(n) for n in ("fin_in", "fin_ready", "stored"))
        dve2 = sem("dve2")

        block = ctx.enter_context(nc.Block())

        w_in1 = a["w_in"][0].rearrange("(k p) f -> p k f", p=P)
        w_out1 = a["w_out"][0].rearrange("(k p) f -> p k f", p=P)
        w_gu1 = a["w_gate_up"][0].rearrange("g e (k p) f -> p (g e) k f", p=P)
        w_dn1 = a["w_down"][0].rearrange("g e (c p) d -> p (g e c) d", p=P)
        w_in2 = a["w_in_2"].rearrange("l (k p) f -> p l k f", p=P)
        w_out2 = a["w_out_2"].rearrange("l (k p) f -> p l k f", p=P)
        w_gate2, w_up2, w_down2 = (a[n].rearrange("l e (k p) f -> p (l e) k f", p=P)
                                   for n in ("w_gate_2", "w_up_2", "w_down_2"))

        SET1 = ((1, "gu", 0), (2, "gu", 1), (3, "dn", 0), (4, "gu", 2), (0, "gu", 3), (5, "dn", 2))
        SET1_OF = {s: kind for s, kind, _ in SET1}
        RUNS1 = NE1 // 4
        BEFORE1 = {s: 2 if s == 0 else 1 for s in range(RING)}
        PER_SLOT2 = 1 + NE2

        @block.sync
        def _(sp):
            for half in range(2):
                sp.dma_start(xT[:, 4 * half:4 * half + 4], a["xT"].rearrange("(k p) s -> p k s", p=P)
                             [:, 4 * half:4 * half + 4]).then_inc(x_in.sem, 16)
            for i in range(5):
                sp.dma_start(slot[i], w_in1[:, :, 512 * i:512 * i + 512]).then_inc(landed1[i], 16)
            sp.dma_start(h, a["x"][0].rearrange("(t p) d -> p t d", p=P)).then_inc(h_in.sem, 16)
            sp.dma_start(slot[5], w_out1[:, :, 0:512]).then_inc(landed1[5], 16)
            sp.wait_ge(proj1.sem, 1 + last_of(PROJ1, "qk", 3))
            sp.dma_start(slot[0], w_out1[:, :, 512:1024]).then_inc(landed1[0], 16)

            def load(s, kind, e, e4):
                if kind == "gu":
                    sp.dma_start(slot[s], w_gu1[:, e4 * 4 + e]).then_inc(landed1[s], 16)
                else:
                    sp.dma_start(ring[:, s * SLOT_COLS:(s + 1) * SLOT_COLS].rearrange("p (c d) -> p c d", d=D),
                                 w_dn1[:, bass.ds((e4 * 4 + e) * 2, 4)]).then_inc(landed1[s], 16)

            sp.wait_ge(proj1.sem, len(PROJ1))
            for s, kind, e in SET1[:4]:
                load(s, kind, e, 0)
            sp.wait_ge(wo1_mm.sem, 2 * T)
            for s, kind, e in SET1[4:]:
                load(s, kind, e, 0)

            def next_set(run, e4):
                for s, kind, e in SET1:
                    if kind == "gu":
                        sp.wait_ge(ex1["gu"].sem, ex1["gu"].at((run - 1) * 2 + (e // 2 + 1)))
                    else:
                        sp.wait_ge(ex1["dn"].sem, ex1["dn"].at((run - 1) * 4 + (e + 2)))
                    load(s, kind, e, e4)

            with sp.Fori(1, RUNS1) as e4:
                next_set(e4, e4)
            sp.wait_ge(places1.sem, 1)
            n_rounds = sp.value_load(rounds_i[0:1, 0:1], min_val=1, max_val=S // C)
            with sp.If(n_rounds > 1):
                with sp.Fori(1, n_rounds) as r:
                    with sp.Fori(0, RUNS1) as e4:
                        next_set(r * RUNS1 + e4, e4)

            def load2(s, w, i, half, n=512):
                sp.dma_start(slot[s][:, :, 0:n], w[:, i, :, half:half + n]).then_inc(landed2[s], 16)

            for s, w, (c0, n) in [(i, w_in2, c) for i, c in enumerate(IN2)] + [(4, w_out2, (0, 512)),
                                                                               (5, w_out2, (512, 512))]:
                if SET1_OF[s] == "gu":
                    sp.wait_ge(ex1["gu"].sem, ex1["gu"].at(n_rounds * (RUNS1 * 2)))
                else:
                    sp.wait_ge(ex1["dn"].sem, ex1["dn"].at(n_rounds * (RUNS1 * 4)))
                load2(s, w, 0, c0, n)

            EXPERT = ((w_gate2, 0), (w_gate2, 512), (w_up2, 0), (w_up2, 512), (w_down2, 0), (w_down2, 512))

            def released(s, e):
                if s < 4:
                    sp.wait_ge(ex2["gu"].sem, ex2["gu"].at((e - 1) * 2 + (s // 2 + 1)))
                else:
                    sp.wait_ge(ex2["dn"].sem, ex2["dn"].at(e))

            def layer(l):
                for s, (w, half) in enumerate(EXPERT):
                    if s < 4:
                        sp.wait_ge(proj2.sem, proj2.at(1 + max(i for i, g in enumerate(PROJ2) if g[0] in SLOT_OF2[s]), l))
                    else:
                        sp.wait_ge(wo2_mm.sem, wo2_mm.at(2 * T, l))
                    load2(s, w, l * NE2, half)
                with sp.Fori(1, NE2) as e:
                    for s, (w, half) in enumerate(EXPERT):
                        released(s, l * NE2 + e)
                        load2(s, w, l * NE2 + e, half)

            with sp.Fori(0, LAYERS - 1) as l:
                layer(l)
                for s, (c0, n) in enumerate(IN2):
                    released(s, (l + 1) * NE2)
                    load2(s, w_in2, l + 1, c0, n)
                for s in (4, 5):
                    released(s, (l + 1) * NE2)
                    load2(s, w_out2, l + 1, 512 * (s - 4))
            layer(LAYERS - 1)
            for t in range(T):
                sp.wait_ge(fin_ready.sem, t + 1)
                sp.dma_start(out[0, t * P:(t + 1) * P, :], fin_o[:, t, :]).then_inc(stored.sem, 16)
            sp.wait_ge(stored.sem, 16 * T)

        @block.gpsimd
        def _(pool):
            pool.dma_start(pos_i, a["positions"].rearrange("a s -> (a s)").partition_broadcast(P))\
                .then_inc(pos_in.sem, 16)
            pool.dma_start(tables[:, 0:FIRST_N], a["first_const"]).then_inc(first_in.sem, 16)
            pool.dma_start(base[:, :], a["base_const"]).then_inc(base_in.sem, 16)
            pool.dma_start(sgu_g, a["sgu_ln_g"][0].partition_broadcast(P)).then_inc(sgu_in.sem, 16)
            pool.dma_start(sgu_b, a["sgu_ln_b"][0].partition_broadcast(P)).then_inc(sgu_in.sem, 16)
            for i in range(LAYERS):
                pool.dma_start(all_cols[:, 33 * i:33 * i + 27], a["gains"][i]).then_inc(gains_in.sem, 16)
                pool.dma_start(all_cols[:, 33 * i + 27:33 * i + 33], a["swa_sink_2"][i].partition_broadcast(P))\
                    .then_inc(gains_in.sem, 16)
            for g in range(8):
                pool.dma_start(bsp[HD * (g % 2):HD * (g % 2) + HD, g // 2, :],
                               a["b_spatial"][0, g].partition_broadcast(HD)).then_inc(bsp_in.sem, 16)
            pool.dma_start(bias36[:, 0:G1], a["b_group"][0].partition_broadcast(P)).then_inc(rt1_in.sem, 16)
            pool.dma_start(bias36[:, G1:G1 + NE1], a["b_expert"][0].rearrange("g e -> (g e)").partition_broadcast(P))\
                .then_inc(rt1_in.sem, 16)
            pool.wait_ge(qk1_ready.sem, 1)
            pool.memset(mix1[0:HD, 0:4, :], 0.0).then_inc(padded1.sem, 1)
            pool.wait_ge(padded1.sem, 1)
            pool.wait_ge(qk1_ready.sem, 8)
            pool.memset(qk1[HD:P, 4:8, :], 0.0).then_inc(padded1.sem, 1)
            pool.wait_ge(padded1.sem, 2)
            pool.wait_ge(proj1.sem, len(PROJ1))
            pool.dma_start(wsT, a["w_spatialT"].rearrange("g s t -> s g t")).then_inc(ws_in.sem, 16)
            pool.wait_ge(ws_in.sem, 16)
            pool.wait_ge(base_in.sem, 16)
            for g in range(8):
                pool.tensor_tensor(wsT[:, g, :], wsT[:, g, :], upto, ALU.mult).then_inc(ws_masked.sem, 1)
            pool.wait_ge(sgu_ok.sem, 4)
            pool.dma_start(ln1g, a["ln1_g"][0].partition_broadcast(P)).then_inc(ln1_in.sem, 16)
            pool.dma_start(ln1b, a["ln1_b"][0].partition_broadcast(P)).then_inc(ln1_in.sem, 16)
            pool.wait_ge(wo1_mm.sem, 2 * T)
            pool.dma_start(router1_w, a["w_router1"].rearrange("(k p) e -> p k e", p=P)).then_inc(rt1_in.sem, 16)
            pool.dma_start(ln2g, a["ln2_g"][0].partition_broadcast(P)).then_inc(ln2_in.sem, 16)
            pool.dma_start(ln2b, a["ln2_b"][0].partition_broadcast(P)).then_inc(ln2_in.sem, 16)

            pool.dma_start(tables[:, 0:SECOND_N], a["second_const"]).then_inc(second_in.sem, 16)
            with pool.Fori(0, LAYERS) as l:
                pool.wait_ge(nrm["mm"].sem, nrm["mm"].at(K, l))
                pool.nop(nofuse=True)
                pool.dma_start(wuq, a["mla_w_uq_2"][l].rearrange("(k p) f -> p k f", p=P)).then_inc(ukv_in.sem, 16)
                pool.dma_start(wukv, a["w_ukv"][l]).then_inc(ukv_in.sem, 16)
                pool.wait_ge(kpe_ready.sem, kpe_ready.at(1, l))
                pool.nop(nofuse=True)
                for i in range(MLA_H):
                    pool.tensor_copy(qk2[HD:MLA_D, 14 + i, :], kr_new[HD:MLA_D, :]).then_inc(keys_set.sem, 1)
                pool.wait_ge(keys_set.sem, keys_set.at(MLA_H, l))
                pool.nop(nofuse=True)
                pool.memset(qk2[HD:P, 2:4, :], 0.0).then_inc(keys_set.sem, 1)
                pool.wait_ge(keys_set.sem, keys_set.at(MLA_H + 1, l))
                pool.nop(nofuse=True)
                pool.wait_ge(proj2.sem, proj2.at(1 + last_of(PROJ2, "uv", T - 1), l))
                pool.nop(nofuse=True)
                pool.memset(cq[0:HD, :, :], 0.0).then_inc(keys_set.sem, 1)
                pool.wait_ge(keys_set.sem, keys_set.at(MLA_H + 2, l))
                pool.nop(nofuse=True)
                pool.wait_ge(rope2.sem, rope2.at(rope2.per, l))
                pool.nop(nofuse=True)
                pool.memset(qk2[HD:P, 7, :], 0.0).then_inc(keys_set.sem, 1)
                for i in range(NA_H):
                    if i == 0:
                        pool.wait_ge(took2_a.sem, took2_a.at(took2_a.per, l))
                        pool.wait_ge(took2_v.sem, took2_v.at(took2_v.per, l))
                        pool.wait_ge(rope2.sem, rope2.at(rope2.per, l))
                        pool.nop(nofuse=True)
                    if i >= 2:
                        pool.wait_ge(att2["shifted"].sem, att2["shifted"].at(T * (len(HEADS2) - NA_H + i - 1), l))
                        pool.nop(nofuse=True)
                    for r in range(2):
                        src = bass.AP(a["rpb"].tensor,
                                      l * RPB_LEN + (RPB_PAD + i * RPB_COLS + (1 - r) * RPB_ROW + 15 - (GW - 1)),
                                      [[1, GW], [RPB_ROW, BT_ROWS], [1, GW]])
                        pool.dma_start(split(bt[i % 2][GW * r:GW * r + GW, :], j=BT_ROWS), src)\
                            .then_inc(bias_in[i % 2].sem, 16)
                pool.wait_ge(wo2_mm.sem, wo2_mm.at(2 * T, l))
                pool.nop(nofuse=True)
                pool.dma_start(router2_w, a["w_router_2"][l].rearrange("(k p) e -> p k e", p=P))\
                    .then_inc(rt2_in.sem, 16)
                pool.dma_start(tables[:, 0:SECOND_N], a["second_const"]).then_inc(second_in.sem, 16)
            pool.wait_ge(layer_done.sem, 1 + LAYERS)
            pool.dma_start(fin_g, a["final_norm_2"].partition_broadcast(P)).then_inc(fin_in.sem, 16)

        @block.tensor
        def _(pe):
            def product(o, pairs):
                for i, (lhs, rhs) in enumerate(pairs):
                    mm = pe.matmul(o, lhs, rhs, start=(i == 0), stop=(i == len(pairs) - 1))
                return mm

            def turn(src, chunks, sg, l=0, b0=0):
                for c in range(chunks):
                    for t in range(T):
                        mm = pe.transpose(bank[b0 + c][:, t * P:(t + 1) * P], src[:, t, c * P:(c + 1) * P], ident)
                    mm.then_inc(sg.sem, 1)

            def attention(heads, sg, view, l=0):
                units = [(n, kind, i, t) for n, (kind, i) in enumerate(heads) for t in range(T)]
                for u in range(len(units) + 2):
                    if u < len(units):
                        n, kind, i, t = units[u]
                        q, k, _ = view(kind, i)
                        k0, k1 = first_key(kind, t) * P, end_key(kind, t) * P
                        pe.matmul(bank[u % 2][:, 0:k1 - k0], q[:, t * P:(t + 1) * P], k[:, k0:k1], start=True,
                                  stop=True).then_inc(sg["score"].sem, 1)
                    if 1 <= u <= len(units):
                        n, kind, i, t = units[u - 1]
                        pe.wait_ge(sg["prob"].sem, sg["prob"].at(u, l))
                        for c in range(end_key(kind, t) - first_key(kind, t)):
                            mm = pe.transpose(bank[2 + (u - 1) % 2][:, c * P:(c + 1) * P],
                                              prob[(u - 1) % 2][:, c * P:(c + 1) * P], ident)
                        mm.then_inc(sg["turned"].sem, 1)
                    if u >= 2:
                        w = u - 2
                        n, kind, i, t = units[w]
                        _, _, v = view(kind, i)
                        pe.wait_ge(sg["probT_a" if w % 2 else "probT_v"].sem, sg["probT_a" if w % 2 else "probT_v"].at(w // 2 + 1, l))
                        if t == 0 and n >= 2:
                            pe.wait_ge(sg["head_out"].sem, sg["head_out"].at(n - 1, l))
                        k0 = first_key(kind, t)
                        product(bank[4 + n % 2][:, t * P:(t + 1) * P],
                                [(probT[w % 2][:, (c - k0) * P:(c - k0 + 1) * P], v(c))
                                 for c in range(k0, end_key(kind, t))]).then_inc(sg["pv"].sem, 1)

            def columns(o, halves):
                for i in range(len(halves[0])):
                    for n, pairs in enumerate(halves):
                        lhs, rhs = pairs[i]
                        mm = pe.matmul(o[C * n:C * n + C, :], lhs, rhs, start=(i == 0), stop=(i == len(pairs) - 1))
                return mm

            def gather(X, it):
                pe.wait_ge(X["sel"].sem, X["sel"].at(it + 1))
                for c in range(K):
                    mm = product(bank[c // 4][:, c % 4 * P:c % 4 * P + P],
                                 [(xn[:, t, c * P:(c + 1) * P], sel[:, t, :]) for t in range(T)])
                mm.then_inc(X["gath"].sem, 1)

            def turn_hidden(X, n, chunks):
                pe.wait_ge(X["hid"].sem, X["hid"].at(n + 1))
                for c in range(chunks):
                    mm = pe.transpose(bank[2][:, c * P:(c + 1) * P], hid[:, c * P:(c + 1) * P], ident)
                mm.then_inc(X["hT"].sem, 1)

            def turn_gates(X, it):
                pe.wait_ge(X["selg"].sem, X["selg"].at(it + 1))
                for t in range(T):
                    mm = pe.transpose(bank[3][:, t * P:(t + 1) * P], selg[:, t, :], ident)
                mm.then_inc(X["selgT"].sem, 1)

            def scatter(X, it):
                pe.wait_ge(X["selgT_ok"].sem, X["selgT_ok"].at(it + 1))
                pe.wait_ge(X["ys"].sem, X["ys"].at(it * 2 + 2))
                for g in range(2 * T):
                    if g >= 2:
                        pe.wait_ge(X["added"].sem, X["added"].at(it * 8 + g - 1))
                    t, half = divmod(g, 2)
                    pe.matmul(bank[6 + g % 2][:, :], selgT[:, t * P:(t + 1) * P], ys[:, half * 512:(half + 1) * 512],
                              start=True, stop=True).then_inc(X["scat"].sem, 1)

            def places(n, sg):
                for t in range(T):
                    mm = product(bank[3][:, t * n:(t + 1) * n],
                                 [(ones, mask_of(n)[:, s, :]) for s in range(t)] + [(upto, mask_of(n)[:, t, :])])
                if n == NE1:
                    mm = product(bank[3][:, T * n:(T + 1) * n], [(ones, mask_of(n)[:, t, :]) for t in range(T)])
                mm.then_inc(sg.sem, 1)

            pe.wait_ge(base_in.sem, 16)
            pe.wait_ge(first_in.sem, 16)
            pe.wait_ge(x_in.sem, 32)
            for n, (w, i) in enumerate(PROJ1):
                b = bank[n % 8][:, :]
                if n >= 8:
                    mine = PROJ1[n - 8][0] in PROJ1_ACT
                    pe.wait_ge((took1_a if mine else took1_v).sem, nth(PROJ1, PROJ1_ACT, n - 8))
                if w == "qk":
                    pe.wait_ge(landed1[i // 4], 16)
                    mm = product(b, [(slot[i // 4][:, k, i % 4 * P:i % 4 * P + P], xT[:, k, :]) for k in range(K)])
                elif w == "rot":
                    pe.wait_ge(took1_a.sem, nth(PROJ1, PROJ1_ACT, PROJ1.index(("qk", i))))
                    mm = product(b, [(tab(FIRST_AT, "rot"), qk1[:, i, :])])
                elif w == "v":
                    pe.wait_ge(landed1[2], 16)
                    mm = product(b, [(xT[:, k, i * P:(i + 1) * P], slot[2][:, k, :]) for k in range(K)])
                elif w == "u":
                    pe.wait_ge(landed1[3], 16)
                    mm = product(b, [(slot[3][:, k, i * P:(i + 1) * P], xT[:, k, :]) for k in range(K)])
                else:
                    pe.wait_ge(landed1[4], 16)
                    mm = product(b, [(xT[:, k, i * P:(i + 1) * P], slot[4][:, k, :]) for k in range(K)])
                mm.then_inc(proj1.sem, 1)
            pe.wait_ge(took1_a.sem, sum(w in PROJ1_ACT for w, _ in PROJ1))
            pe.wait_ge(took1_v.sem, sum(w not in PROJ1_ACT for w, _ in PROJ1))
            pe.wait_ge(qk1_ready.sem, 8)
            pe.wait_ge(padded1.sem, 2)
            attention(HEADS1, att1, view1)
            pe.wait_ge(att1["head_out"].sem, att1["head_out"].at(H1))
            turn(o1, 4, oT_mm)
            pe.wait_ge(ws_masked.sem, 8)
            pe.wait_ge(g1_ready.sem, T)
            for c in range(4):
                for g in range(2):
                    for t in range(T):
                        mm = pe.matmul(bank[4 + c][HD * g:HD * g + HD, t * P:(t + 1) * P],
                                       g1[:, t, (2 * c + g) * HD:(2 * c + g + 1) * HD], wsT[:, 2 * c + g, :],
                                       start=True, stop=True)
                mm.then_inc(sgu_mm.sem, 1)
            pe.wait_ge(oT_a.sem, 2)
            pe.wait_ge(oT_v.sem, 2)
            pe.wait_ge(sgu_ok.sem, 4)
            pe.wait_ge(landed1[5], 16)
            pe.wait_ge(landed1[0], 32)
            for n in range(2 * T):
                t, half = divmod(n, 2)
                w = slot[5 if half == 0 else 0]
                product(bank[n][:, :], [(mix1[:, k, t * P:(t + 1) * P], w[:, k, :]) for k in range(K)])\
                    .then_inc(wo1_mm.sem, 1)
            pe.wait_ge(h1_ready.sem, T)
            turn(xn, K, r1_mm)
            pe.wait_ge(rt1_in.sem, 48)
            pe.wait_ge(r1_a.sem, K // 2)
            pe.wait_ge(r1_v.sem, K // 2)
            for t in range(T):
                mm = product(bank[0][:, t * 36:(t + 1) * 36],
                             [(xT[:, k, t * P:(t + 1) * P], router1_w[:, k, :]) for k in range(K)])
            mm.then_inc(lg1_mm.sem, 1)
            pe.wait_ge(mask1.sem, G1)
            places(NE1, cum1_mm)

            def pair1(it, slots, landed, more):
                s_gu, s_dn = slots
                X = ex1
                pe.wait_ge(X["xs"].sem, X["xs"].at(it + 1))
                for s in s_gu:
                    landed(s)
                columns(bank[2], [[(xs[:, k, C * j:C * j + C], slot[s_gu[j]][:, k, :]) for k in range(K)]
                                  for j in range(2)]).then_inc(X["gu"].sem, 1)
                if more:
                    gather(X, it + 1)
                turn_hidden(X, it, 2)
                turn_gates(X, it)
                landed(s_dn)
                pe.wait_ge(X["hT_ok"].sem, X["hT_ok"].at(it + 1))
                for half in range(2):
                    columns(bank[4 + half], [[(hidT[:, c * P + C * j:c * P + C * j + C],
                                               ring[:, s_dn * SLOT_COLS + (2 * j + c) * D + 512 * half:][:, 0:512])
                                              for c in range(2)] for j in range(2)]).then_inc(X["dn"].sem, 1)
                scatter(X, it)

            def four_experts(run, last):
                def landed(s):
                    pe.wait_ge(landed1[s], (run + (BEFORE1[s] + 1)) * 16)

                for q in range(2):
                    gu0, gu1, dn = (SET1[3 * q + i][0] for i in range(3))
                    pair1(run * 2 + q, ((gu0, gu1), dn), landed, not (last and q))

            def round1(run0):
                gather(ex1, run0 * 2)
                with pe.Fori(0, RUNS1 - 1) as e4:
                    four_experts(run0 + e4, False)
                four_experts(run0 + (RUNS1 - 1), True)

            round1(0)
            pe.wait_ge(places1.sem, 1)
            n_rounds = pe.value_load(rounds_i[0:1, 0:1], min_val=1, max_val=S // C)
            with pe.If(n_rounds > 1):
                with pe.Fori(1, n_rounds) as r:
                    round1(r * RUNS1)

            def rows(w, i):
                return slice(HD, MLA_D) if w in ("kr", "krrot", "uqrot") else slice(0, {"uq": MLA_D, "uk": HD}.get(w, P))

            with pe.Fori(0, LAYERS) as l:
                pe.wait_ge(nrm["x"].sem, nrm["x"].at(T, l))
                turn(xn, K, nrm["mm"])
                pe.wait_ge(nrm["a"].sem, nrm["a"].at(K // 2, l))
                pe.wait_ge(nrm["v"].sem, nrm["v"].at(K // 2, l))
                pe.wait_ge(second_in.sem, second_in.at(16, l))
                for n, (w, i) in enumerate(PROJ2):
                    b = bank[n % 8]
                    if n >= 8:
                        mine = PROJ2[n - 8][0] in PROJ2_ACT
                        pe.wait_ge((took2_a if mine else took2_v).sem, (took2_a if mine else took2_v).at(nth(PROJ2, PROJ2_ACT, n - 8), l))
                    s = {"cq": 0, "ckv": 0, "kr": 0, "na": 1, "swa": 2, "va": 3}.get(w)
                    if s is not None:
                        pe.wait_ge(landed2[s], l * (16 * PER_SLOT2) + 16)
                    if w in ("cq", "ckv", "kr", "na", "swa"):
                        c0 = {"ckv": 2 * P, "kr": 3 * P}.get(w, i * P)
                        c1 = c0 + (MLA_ROPE if w == "kr" else P)
                        mm = product(b[rows(w, i), :], [(slot[s][:, k, c0:c1], xT[:, k, :]) for k in range(K)])
                    elif w == "va":
                        mm = product(b[:, 0:384], [(xT[:, k, i * P:(i + 1) * P], slot[3][:, k, 0:384]) for k in range(K)])
                    elif w == "ssq":
                        pe.wait_ge(took2_a.sem, took2_a.at(nth(PROJ2, PROJ2_ACT, PROJ2.index(("ckv", 0) if i else ("cq", 1))), l))
                        mm = product(b[:, :], [(ones, sq[:, c, :]) for c in ((2,) if i else (0, 1))])
                    elif w == "krrot":
                        pe.wait_ge(took2_a.sem, took2_a.at(nth(PROJ2, PROJ2_ACT, PROJ2.index(("kr", 0))), l))
                        pe.nop(nofuse=True)
                        mm = product(b[HD:MLA_D, :], [(tab(SECOND_AT, "rot_mla")[HD:MLA_D, :], kr_raw[HD:MLA_D, :])])
                    elif w == "uq":
                        pe.wait_ge(ukv_in.sem, ukv_in.at(32, l))
                        pe.wait_ge(lat_ready.sem, lat_ready.at(2, l))
                        mm = product(b[0:MLA_D, :], [(wuq[:, c, i * MLA_D:(i + 1) * MLA_D], cq[:, c, :]) for c in range(2)])
                    elif w == "uqrot":
                        pe.wait_ge(took2_a.sem, took2_a.at(nth(PROJ2, PROJ2_ACT, PROJ2.index(("uq", i))), l))
                        pe.nop(nofuse=True)
                        mm = product(b[HD:MLA_D, :], [(tab(SECOND_AT, "rot_mla")[HD:MLA_D, :], qk2[HD:MLA_D, 8 + i, :])])
                    elif w == "uk":
                        pe.wait_ge(lat_ready.sem, lat_ready.at(3, l))
                        mm = product(b[0:HD, :], [(wukv[:, i * HD:(i + 1) * HD], cq[:, 2, :])])
                    elif w == "uv":
                        mm = product(b[:, 0:384], [(cq[:, 2, i * P:(i + 1) * P], wukv[:, 384:768])])
                    else:
                        pe.wait_ge(took2_a.sem, took2_a.at(nth(PROJ2, PROJ2_ACT, PROJ2.index(("swa", i))), l))
                        mm = product(b[:, :], [(tab(SECOND_AT, "rot"), qk2[:, 4 + i, :])])
                    mm.then_inc(proj2.sem, 1)
                pe.wait_ge(took2_a.sem, took2_a.at(took2_a.per, l))
                pe.wait_ge(took2_v.sem, took2_v.at(took2_v.per, l))
                pe.wait_ge(rope2.sem, rope2.at(rope2.per, l))
                pe.wait_ge(keys_set.sem, keys_set.at(MLA_H + 3, l))
                attention(HEADS2, att2, view2, l)
                pe.wait_ge(gnm["x"].sem, gnm["x"].at(T, l))
                turn(o2, K, gnm["mm"])
                pe.wait_ge(gnm["a"].sem, gnm["a"].at(K // 2, l))
                pe.wait_ge(gnm["v"].sem, gnm["v"].at(K // 2, l))
                pe.wait_ge(landed2[4], l * (16 * PER_SLOT2) + 16)
                pe.wait_ge(landed2[5], l * (16 * PER_SLOT2) + 16)
                for n in range(2 * T):
                    t, half = divmod(n, 2)
                    product(bank[n][:, :], [(oT2[:, k, t * P:(t + 1) * P], slot[4 + half][:, k, :]) for k in range(K)])\
                        .then_inc(wo2_mm.sem, 1)
                pe.wait_ge(fnm["x"].sem, fnm["x"].at(T, l))
                turn(xn, K, fnm["mm"])
                pe.wait_ge(fnm["a"].sem, fnm["a"].at(K // 2, l))
                pe.wait_ge(fnm["v"].sem, fnm["v"].at(K // 2, l))
                pe.wait_ge(rt2_in.sem, rt2_in.at(16, l))
                for t in range(T):
                    mm = product(bank[0][:, t * NE2:(t + 1) * NE2],
                                 [(xT[:, k, t * P:(t + 1) * P], router2_w[:, k, :]) for k in range(K)])
                mm.then_inc(lg2_mm.sem, 1)
                pe.wait_ge(aff_ready.sem, aff_ready.at(1, l))
                for t in range(T):
                    mm = pe.transpose(bank[1][0:NE2, t * P:(t + 1) * P], pick[2][:, t * NE2:(t + 1) * NE2], ident)
                mm.then_inc(affT_mm.sem, 1)
                pe.wait_ge(maskT_ready.sem, maskT_ready.at(1, l))
                pe.nop(nofuse=True)
                for t in range(T):
                    mm = pe.transpose(bank[2][:, t * NE2:(t + 1) * NE2], maskT[0:NE2, t * P:(t + 1) * P],
                                      ident[0:NE2, 0:NE2])
                mm.then_inc(mask_mm.sem, 1)
                pe.wait_ge(mask2.sem, mask2.at(1, l))
                places(NE2, cum2_mm)

                def pair2(pair, last):
                    X = ex2
                    it = l * (NE2 // 2) + pair
                    pe.wait_ge(X["xs"].sem, X["xs"].at(it + 1))
                    for j in range(2):
                        def landed(s, j=j):
                            pe.wait_ge(landed2[s], (l * PER_SLOT2 + pair * 2 + (j + 2)) * 16)

                        for which in range(2):
                            landed(2 * which)
                            landed(2 * which + 1)
                            columns(bank[2 + which], [[(xs[:, k, C * j:C * j + C], slot[2 * which + half][:, k, :])
                                                       for k in range(K)] for half in range(2)])\
                                .then_inc(X["gu"].sem, 1)
                        if j and not last:
                            gather(X, it + 1)
                        turn_hidden(X, it * 2 + j, 4)
                        if j:
                            turn_gates(X, it)
                        landed(4)
                        landed(5)
                        pe.wait_ge(X["hT_ok"].sem, X["hT_ok"].at(it * 2 + (j + 1)))
                        columns(bank[4 + j], [[(hidT[:, c * P + C * fh:c * P + C * fh + C], slot[4 + half][:, 4 * fh + c, :])
                                               for fh in range(2) for c in range(4)] for half in range(2)])\
                            .then_inc(X["dn"].sem, 1)
                    scatter(X, it)

                gather(ex2, l * (NE2 // 2))
                with pe.Fori(0, NE2 // 2 - 1) as pair:
                    pair2(pair, False)
                pair2(NE2 // 2 - 1, True)

        @block.scalar
        def _(act):
            def take_chunks(sg, dst, chunks, gain=None, l=0, b0=0):
                for n, c in enumerate(range(0, chunks, 2)):
                    act.wait_ge(sg["mm"].sem, sg["mm"].at(c + 1, l))
                    act.activation(dst[:, c, :], bank[b0 + c][:, :], ACT.Copy,
                                   scale=1.0 if gain is None else gain[:, c:c + 1]).then_inc(sg["a"].sem, 1)

            def attention(heads, sg, l=0):
                units = [(n, kind, i, t) for n, (kind, i) in enumerate(heads) for t in range(T)]
                swa_seen = 0
                for u in range(len(units) + 1):
                    if u < len(units):
                        n, kind, i, t = units[u]
                        w = (end_key(kind, t) - first_key(kind, t)) * P
                        p = prob[u % 2][:, 0:w]
                        act.wait_ge(sg["shifted"].sem, sg["shifted"].at(u + 1, l))
                        if kind == "mla":
                            if u >= 2:
                                act.wait_ge(sg["turned"].sem, sg["turned"].at(u - 1, l))
                            act.activation(p, bank[u % 2][:, 0:w], ACT.Exp, bias=negmax[:, u:u + 1],
                                           accum_out=total[:, u:u + 1]).then_inc(sg["prob"].sem, 1)
                        else:
                            act.activation(p, p, ACT.Exp, bias=negmax[:, u:u + 1], scale=-1.0,
                                           accum_out=total[:, u:u + 1]).then_inc(sg["prob"].sem, 1)
                        if kind == "swa" and t == T - 1:
                            act.activation(esink, negmax[:, u - T + 1:u + 1], ACT.Exp, bias=sink[:, i:i + 1])\
                               .then_inc(sunk.sem, 1)
                    v = u - 1
                    if v >= 0 and v % 2:
                        n, kind, i, t = units[v]
                        w = (end_key(kind, t) - first_key(kind, t)) * P
                        act.wait_ge(sg["turned"].sem, sg["turned"].at(v + 1, l))
                        if v >= 2:
                            act.wait_ge(sg["pv"].sem, sg["pv"].at(v - 1, l))
                        act.activation(probT[1][:, 0:w], bank[3][:, 0:w], ACT.Copy).then_inc(sg["probT_a"].sem, 1)

            def hidden(X, n, per, w):
                act.wait_ge(X["gu"].sem, X["gu"].at(n * per + 1))
                act.activation(silu[:, 0:w], bank[2][:, 0:w], ACT.Silu).then_inc(X["silu"].sem, 1)
                act.wait_ge(X["hT"].sem, X["hT"].at(n + 1))
                act.activation(hidT[:, 0:w], bank[2][:, 0:w], ACT.Copy).then_inc(X["hT_ok"].sem, 1)

            def gates(X, it):
                act.wait_ge(X["selgT"].sem, X["selgT"].at(it + 1))
                act.activation(selgT, bank[3][:, :], ACT.Copy).then_inc(X["selgT_ok"].sem, 1)

            def pair1(it):
                hidden(ex1, it, 1, F1)
                gates(ex1, it)
                for half in range(2):
                    act.wait_ge(ex1["dn"].sem, ex1["dn"].at(it * 2 + (half + 1)))
                    act.activation(ys[:, half * 512:(half + 1) * 512], bank[4 + half][:, :], ACT.Copy)\
                       .then_inc(ex1["ys"].sem, 1)

            def pair2(it):
                for j in range(2):
                    hidden(ex2, it * 2 + j, 2, 512)
                    if j:
                        gates(ex2, it)
                    act.wait_ge(ex2["dn"].sem, ex2["dn"].at(it * 2 + (j + 1)))
                    for half in range(2):
                        ins = act.activation(ys[C * j:C * j + C, half * 512:(half + 1) * 512],
                                             bank[4 + j][C * half:C * half + C, :], ACT.Copy)
                    ins.then_inc(ex2["ys"].sem, 1)

            def squares(src, sg, eps_n, l=0):
                for t in range(T):
                    ins = act.activation(junk[:, t, :], src[:, t, :], ACT.Square, accum_out=ss[:, t:t + 1])
                ins.then_inc(sg["ss"].sem, 1)
                act.wait_ge(sg["ss"].sem, sg["ss"].at(1, l))
                act.activation(std[:, 0:T], ss[:, 0:T], ACT.Sqrt, bias=eps_rms, scale=1.0 / D)\
                   .then_inc(sg["std"].sem, 1)

            act.wait_ge(sin_args.sem, 2)
            act.activation(sin1, sin_arg, ACT.Sin).then_inc(rope1.sem, 1)
            act.activation(cos1, cos_arg, ACT.Sin).then_inc(rope1.sem, 1)
            for n, (w, i) in enumerate(PROJ1):
                if w in PROJ1_ACT:
                    act.wait_ge(proj1.sem, n + 1)
                    b = bank[n % 8][:, :]
                    if w == "qk":
                        act.activation(qk1[:, i, :], b, ACT.Copy, scale=-HD ** -0.5 if i < 4 else 1.0)\
                           .then_inc(took1_a.sem, 1)
                    else:
                        act.activation((u1 if w == "u" else g1)[:, i, :], b, ACT.Gelu).then_inc(took1_a.sem, 1)
            act.wait_ge(g1_var.sem, T)
            act.activation(std[:, 0:T], mv[:, 1:8:2], ACT.Sqrt, bias=eps_ln).then_inc(g1_std.sem, 1)
            attention(HEADS1, att1)
            take_chunks({"mm": oT_mm, "a": oT_a}, mix1, 4)
            act.wait_ge(h1_var.sem, T)
            act.activation(std[:, 0:T], mv[:, 1:8:2], ACT.Sqrt, bias=eps_ln).then_inc(h1_std.sem, 1)
            take_chunks({"mm": r1_mm, "a": r1_a}, xT, K)
            for i, n in enumerate((T * G1, T)):
                act.wait_ge(ex1_in.sem, i + 1)
                act.activation(pick[1][:, 0:n], pick[0][:, 0:n], ACT.Exp).then_inc(ex1_out.sem, 1)
            with act.Fori(0, NE1 // 2) as pair:
                pair1(pair)
            act.wait_ge(places1.sem, 1)
            n_rounds = act.value_load(rounds_i[0:1, 0:1], min_val=1, max_val=S // C)
            with act.If(n_rounds > 1):
                with act.Fori(1, n_rounds) as r:
                    with act.Fori(0, NE1 // 2) as pair:
                        pair1(r * (NE1 // 2) + pair)
            act.wait_ge(h2_var.sem, T)
            act.activation(std[:, 0:T], mv[:, 1:8:2], ACT.Sqrt, bias=eps_ln).then_inc(h2_std.sem, 1)

            with act.Fori(0, LAYERS) as l:
                act.wait_ge(layer_done.sem, layer_done.at(1, l))
                squares(h, nrm, D, l)
                act.wait_ge(cols_ready.sem, cols_ready.at(1, l))
                take_chunks(nrm, xT, K, gains[:, 0, :], l)
                for n, (w, i) in enumerate(PROJ2):
                    if w not in PROJ2_ACT:
                        continue
                    b = bank[n % 8]
                    act.wait_ge(proj2.sem, proj2.at(n + 1, l))
                    if w in ("cq", "ckv"):
                        c = 2 if w == "ckv" else i
                        act.activation(cq[:, c, :], b[:, :], ACT.Copy)
                        ins = act.activation(sq[:, c, :], b[:, :], ACT.Square)
                    elif w == "kr":
                        ins = act.activation(kr_raw[HD:MLA_D, :], b[HD:MLA_D, :], ACT.Copy)
                    elif w == "na" and i < 2:
                        ins = act.activation(qk2[:, i, :], b[:, :], ACT.Copy, scale=-HD ** -0.5)
                    elif w == "na":
                        act.activation(qk2[0:HD, i, :], b[0:HD, :], ACT.Copy)
                        ins = act.activation(cq[HD:P, i - 2, :], b[HD:P, :], ACT.Copy)
                    elif w == "swa":
                        ins = act.activation(qk2[:, 4 + i, :], b[:, :], ACT.Copy, scale=-HD ** -0.5 if i < 3 else 1.0)
                    elif w == "ssq":
                        ins = act.activation(rs[:, i, :], b[:, :], ACT.Sqrt, bias=eps_rms, scale=1.0 / (P if i else 2 * P))
                    elif w == "uq":
                        ins = act.activation(qk2[0:MLA_D, 8 + i, :], b[0:MLA_D, :], ACT.Copy, scale=MLA_D ** -0.5)
                    else:
                        ins = act.activation(vm[:, i, :], b[:, 0:384], ACT.Copy)
                    ins.then_inc(took2_a.sem, 1)
                attention(HEADS2, att2, l)
                act.wait_ge(att2["head_out"].sem, att2["head_out"].at(len(HEADS2), l))
                for g, (c0, c1) in enumerate(GROUPS2):
                    for t in range(T):
                        ins = act.activation(junk[:, t, c0:c1], o2[:, t, c0:c1], ACT.Square,
                                             accum_out=ss[:, g * T + t:g * T + t + 1])
                ins.then_inc(gnm["ss"].sem, 1)
                act.wait_ge(gnm["ss"].sem, gnm["ss"].at(1, l))
                act.activation(std[:, 0:T], ss[:, 0:T], ACT.Sqrt, bias=eps_rms, scale=1.0 / 256)
                act.activation(std[:, T:3 * T], ss[:, T:3 * T], ACT.Sqrt, bias=eps_rms, scale=1.0 / 384)\
                   .then_inc(gnm["std"].sem, 1)
                take_chunks(gnm, oT2, K, gains[:, 1, :], l)
                act.wait_ge(h2_sum.sem, h2_sum.at(2 * T, l))
                squares(h, fnm, D, l)
                take_chunks(fnm, xT, K, gains[:, 2, :], l)
                act.wait_ge(ex2_in.sem, ex2_in.at(1, l))
                act.activation(pick[1][:, 0:T * NE2], pick[0][:, 0:T * NE2], ACT.Exp).then_inc(ex2_out.sem, 1)
                with act.Fori(0, NE2 // 2) as pair:
                    pair2(l * (NE2 // 2) + pair)
            act.wait_ge(layer_done.sem, 1 + LAYERS)
            squares(h, fin, D)

        @block.vector
        def _(dve):
            v = dve

            def take_chunks(sg, dst, chunks, gain=None, l=0, b0=0):
                for c in range(1, chunks, 2):
                    v.wait_ge(sg["mm"].sem, sg["mm"].at(c + 1, l))
                    if gain is None:
                        ins = v.tensor_copy(dst[:, c, :], bank[b0 + c][:, :])
                    else:
                        ins = v.tensor_scalar(dst[:, c, :], bank[b0 + c][:, :], gain[:, c:c + 1], None, ALU.mult)
                    ins.then_inc(sg["v"].sem, 1)

            def attention(heads, sg, table, place_of, chain, l=0):
                units = [(n, kind, i, t) for n, (kind, i) in enumerate(heads) for t in range(T)]
                for u in range(len(units) + 2):
                    if u < len(units):
                        n, kind, i, t = units[u]
                        k0, k1 = first_key(kind, t), end_key(kind, t)
                        w = (k1 - k0) * P
                        if kind == "na" and t == 0:
                            v.wait_ge(bias_in[i % 2].sem, bias_in[i % 2].at(32 * (i // 2 + 1), l))
                            b = split(bt[i % 2], j=BT_ROWS)
                            v.scalar_tensor_tensor(out=b, in0=b, scalar=-1.0,
                                                   in1=spread(tab(SECOND_AT, "window"), 1, BT_ROWS),
                                                   op0=ALU.mult, op1=ALU.add).then_inc(bias_ready.sem, 1)
                            v.wait_ge(bias_ready.sem, bias_ready.at(i + 1, l))
                        v.wait_ge(sg["score"].sem, sg["score"].at(u + 1, l))
                        if kind != "mla":
                            v.nop(nofuse=True)
                        s = bank[u % 2][:, 0:w]
                        if kind == "mla":
                            v.tensor_reduce(negmax[:, u:u + 1], s, AX_X, ALU.max, negate=True)\
                             .then_inc(sg["shifted"].sem, 1)
                        else:
                            if u >= 2:
                                v.wait_ge(sg["turned"].sem, sg["turned"].at(u - 1, l))
                                v.nop(nofuse=True)
                            rows = (lambda x: split(x, r=GH)) if kind == "na" else (lambda x: x)
                            v.tensor_tensor_reduce(out=rows(prob[u % 2][:, 0:w]), in0=rows(s), in1=table(kind, i, t), scale=1.0,
                                                   scalar=nsink[:, i:i + 1] if kind == "swa" else HUGE,
                                                   op0=ALU.add, op1=ALU.min, accum_out=negmax[:, u:u + 1])\
                             .then_inc(sg["shifted"].sem, 1)
                    w1 = u - 1
                    if 0 <= w1 < len(units) and w1 % 2 == 0:
                        n, kind, i, t = units[w1]
                        w = (end_key(kind, t) - first_key(kind, t)) * P
                        v.wait_ge(sg["turned"].sem, sg["turned"].at(w1 + 1, l))
                        if w1 >= 2:
                            v.wait_ge(sg["pv"].sem, sg["pv"].at(w1 - 1, l))
                        v.tensor_copy(probT[0][:, 0:w], bank[2][:, 0:w]).then_inc(sg["probT_v"].sem, 1)
                    if u >= 2 and (u - 2) % T == T - 1:
                        n, kind, i, t = units[u - 2]
                        v.wait_ge(sg["pv"].sem, sg["pv"].at(u - 1, l))
                        sums = total[:, n * T:(n + 1) * T]
                        if kind == "swa":
                            v.wait_ge(sunk.sem, sunk.at(i + 1, l))
                            v.tensor_tensor(sums, sums, esink, ALU.add).then_inc(chain.sem, 1)
                            v.wait_ge(chain.sem, chain.next())
                        v.reciprocal(rtotal, sums).then_inc(chain.sem, 1)
                        v.wait_ge(chain.sem, chain.next())
                        own = HD * second_of_two(kind, i)
                        v.tensor_tensor(place_of(kind, i), split(bank[4 + n % 2][:, :], t=T)[:, :, own:own + HD],
                                        spread(rtotal, 2, HD), ALU.mult).then_inc(sg["head_out"].sem, 1)

            def moments(t, width, src, chain):
                m = width // 512
                for i in range(m):
                    ins = v.bn_stats(bn[:, 6 * i:6 * i + 6], src[:, t, 512 * i:512 * (i + 1)])
                ins.then_inc(chain.sem, 1)
                v.wait_ge(chain.sem, chain.next())
                return v.bn_aggr(mv[:, 2 * t:2 * t + 2], bn[:, 0:6 * m])

            def layer_norm(src, dst, g, b, t, chain):
                v.tensor_scalar(src, src, mv[:, 2 * t:2 * t + 1], rstd[:, t:t + 1], ALU.subtract, ALU.mult)\
                 .then_inc(chain.sem, 1)
                v.wait_ge(chain.sem, chain.next())
                v.tensor_tensor(src, src, g, ALU.mult).then_inc(chain.sem, 1)
                v.wait_ge(chain.sem, chain.next())
                return v.tensor_tensor(dst, src, b, ALU.add)

            def first_max(values, n, groups, m, eq, chain):
                v.tensor_reduce(m, values, AX_X, ALU.max).then_inc(chain.sem, 1)
                v.wait_ge(chain.sem, chain.next())
                v.tensor_tensor(eq, values, spread(m, 2, n), ALU.is_equal).then_inc(chain.sem, 1)
                v.wait_ge(chain.sem, chain.next())
                v.tensor_tensor(eq, eq, spread(rank[:, 0:n], 1, groups), ALU.mult).then_inc(chain.sem, 1)
                v.wait_ge(chain.sem, chain.next())
                v.tensor_reduce(col[0], eq, AX_X, ALU.max).then_inc(chain.sem, 1)
                v.wait_ge(chain.sem, chain.next())
                v.tensor_tensor(eq, eq, spread(col[0], 2, n), ALU.is_equal).then_inc(chain.sem, 1)
                v.wait_ge(chain.sem, chain.next())

            def set_places(n, mm, l=0):
                v.wait_ge(mm.sem, mm.at(1, l))
                return v.tensor_tensor(place[:, 0:n * T].rearrange("p (e t) -> p t e", t=T), mask_of(n),
                                       split(bank[3][:, 0:n * T], t=T), ALU.mult)

            def by_place(table, e):
                return spread(split(table[:, bass.ds(e * T, 2 * T)], j=2).rearrange("p j t -> p t j"), 3, C)

            def pairs_of(x):
                return x.rearrange("p t (j c) -> p t j c", j=2)

            def choose(X, it, e):
                v.tensor_tensor(pairs_of(sel), spread(spread(iota, 1, 2), 1, T), by_place(place, e), ALU.is_equal)\
                 .then_inc(X["sel"].sem, 1)

            def take_tokens(X, it, gain):
                v.wait_ge(X["gath"].sem, X["gath"].at(it + 1))
                for half in range(2):
                    dst = xs[:, 4 * half:4 * half + 4, :]
                    if gain is None:
                        ins = v.tensor_copy(dst, split(bank[half][:, :], k=4))
                    else:
                        ins = v.tensor_tensor(dst, split(bank[half][:, :], k=4),
                                              spread(gain[:, 4 * half:4 * half + 4], 2, P), ALU.mult)
                ins.then_inc(X["xs"].sem, 1)

            def first_pair(X, it, gain):
                choose(X, it, 0)
                take_tokens(X, it, gain)

            def expert_pair(X, it, e, gain, w, last):
                v.wait_ge(X["sel"].sem, X["sel"].at(it + 1))
                v.tensor_tensor(pairs_of(selg), pairs_of(sel), by_place(gate, e), ALU.mult).then_inc(X["selg"].sem, 1)
                if not last:
                    v.wait_ge(X["selg"].sem, X["selg"].at(it + 1))
                    choose(X, it + 1, e + 2)
                one_by_one = w == 512
                for j in range(2 if one_by_one else 1):
                    n = it * 2 + j if one_by_one else it
                    v.wait_ge(X["gu"].sem, X["gu"].at((n + 1) * 2 if one_by_one else n + 1))
                    v.wait_ge(X["silu"].sem, X["silu"].at(n + 1))
                    up = bank[3][:, :] if one_by_one else bank[2][:, w:2 * w]
                    v.tensor_tensor(hid[:, 0:w], silu[:, 0:w], up, ALU.mult).then_inc(X["hid"].sem, 1)
                if not last:
                    take_tokens(X, it + 1, gain)
                for g in range(2 * T):
                    t, half = divmod(g, 2)
                    v.wait_ge(X["scat"].sem, X["scat"].at(it * 8 + g + 1))
                    hs = h[:, t, half * 512:(half + 1) * 512]
                    v.tensor_tensor(hs, hs, bank[6 + g % 2][:, :], ALU.add).then_inc(X["added"].sem, 1)

            def expert_round(X, it0, pairs, gain, w):
                first_pair(X, it0, gain)
                with v.Fori(0, pairs - 1) as pair:
                    expert_pair(X, it0 + pair, pair * 2, gain, w, False)
                expert_pair(X, it0 + (pairs - 1), 2 * (pairs - 1), gain, w, True)

            c1 = Steps(dve1.sem)
            v.memset(eps_ln, LN_EPS).then_inc(c1.sem, 1)
            v.wait_ge(c1.sem, c1.next())
            v.memset(eps_rms, RMS_EPS).then_inc(c1.sem, 1)
            v.wait_ge(c1.sem, c1.next())
            v.wait_ge(pos_in.sem, 16)
            v.wait_ge(first_in.sem, 16)
            v.tensor_copy(ang, pos_i).then_inc(c1.sem, 1)
            v.wait_ge(c1.sem, c1.next())
            v.tensor_scalar(ang, ang, tab(FIRST_AT, "inv"), None, ALU.mult).then_inc(c1.sem, 1)
            v.wait_ge(c1.sem, c1.next())
            v.tensor_scalar(turns, ang, 1.0 / (2 * np.pi), None, ALU.mult).then_inc(c1.sem, 1)
            v.wait_ge(c1.sem, c1.next())
            v.tensor_copy(turns_i, turns).then_inc(c1.sem, 1)
            v.wait_ge(c1.sem, c1.next())
            v.tensor_copy(turns, turns_i).then_inc(c1.sem, 1)
            v.wait_ge(c1.sem, c1.next())
            for n, part in enumerate(TWO_PI_PARTS):
                v.scalar_tensor_tensor(out=sin_arg, in0=turns, scalar=-part, in1=sin_arg if n else ang,
                                       op0=ALU.mult, op1=ALU.add).then_inc(c1.sem, 1)
                v.wait_ge(c1.sem, c1.next())

            def wrap(x, side):
                v.tensor_scalar(over, x, side * np.pi, -side * 2 * np.pi, ALU.is_gt if side > 0 else ALU.is_lt,
                                ALU.mult).then_inc(c1.sem, 1)
                v.wait_ge(c1.sem, c1.next())
                v.tensor_tensor(x, x, over, ALU.add).then_inc(c1.sem, 1)
                v.wait_ge(c1.sem, c1.next())

            wrap(sin_arg, 1)
            wrap(sin_arg, -1)
            v.tensor_scalar(cos_arg, sin_arg, np.pi / 2, None, ALU.add).then_inc(c1.sem, 1)
            v.wait_ge(c1.sem, c1.next())
            wrap(cos_arg, 1)
            for x in (sin_arg, cos_arg):
                v.tensor_scalar(x, x, PI_BELOW, -PI_BELOW, ALU.min, ALU.max).then_inc(sin_args.sem, 1)

            v.wait_ge(rope1.sem, 2)
            for n, (w, i) in enumerate(PROJ1):
                if w in PROJ1_ACT:
                    continue
                v.wait_ge(proj1.sem, n + 1)
                b = bank[n % 8][:, :]
                if w == "v":
                    v.tensor_copy(v1[:, i, :], b).then_inc(took1_v.sem, 1)
                else:
                    v.tensor_tensor(rot_tmp, b, sin1, ALU.mult).then_inc(took1_v.sem, 1)
                    v.tensor_tensor(qk1[:, i, :], qk1[:, i, :], cos1, ALU.mult).then_inc(c1.sem, 1)
                    v.wait_ge(c1.sem, c1.next())
                    v.wait_ge(took1_v.sem, nth(PROJ1, PROJ1_ACT, n))
                    if i >= 4:
                        v.tensor_tensor(mix1[HD:P, i - 4, :], qk1[HD:P, i, :], rot_tmp[HD:P, :], ALU.add)
                    own = slice(0, HD if i >= 4 else P)
                    v.tensor_tensor(qk1[own, i, :], qk1[own, i, :], rot_tmp[own, :], ALU.add)\
                     .then_inc(qk1_ready.sem, 1)
                    v.wait_ge(qk1_ready.sem, i + 1)
            v.wait_ge(sgu_in.sem, 32)
            for t in range(T):
                v.wait_ge(took1_a.sem, nth(PROJ1, PROJ1_ACT, PROJ1.index(("gate", t))))
                moments(t, 512, g1, c1).then_inc(g1_var.sem, 1)
                v.wait_ge(g1_var.sem, t + 1)
            v.wait_ge(g1_std.sem, 1)
            v.reciprocal(rstd[:, 0:T], std[:, 0:T]).then_inc(c1.sem, 1)
            v.wait_ge(c1.sem, c1.next())
            for t in range(T):
                layer_norm(g1[:, t, :], g1[:, t, :], sgu_g, sgu_b, t, c1).then_inc(g1_ready.sem, 1)
            v.wait_ge(g1_ready.sem, T)
            attention(HEADS1, att1, table1, lambda kind, i: o1[:, :, i * HD:(i + 1) * HD], c1)
            take_chunks({"mm": oT_mm, "v": oT_v}, mix1, 4)
            v.wait_ge(bsp_in.sem, 128)
            for c in range(4):
                v.wait_ge(sgu_mm.sem, c + 1)
                v.tensor_tensor(split(rot_tmp, t=T), split(bank[4 + c][:, :], t=T), spread(bsp[:, c, :], 1, T),
                                ALU.add).then_inc(c1.sem, 1)
                v.wait_ge(c1.sem, c1.next())
                v.tensor_tensor(mix1[:, 4 + c, :], u1[:, c, :], rot_tmp, ALU.mult).then_inc(sgu_ok.sem, 1)
                v.wait_ge(sgu_ok.sem, c + 1)
            v.wait_ge(h_in.sem, 16)
            for n in range(2 * T):
                t, half = divmod(n, 2)
                hs = h[:, t, half * 512:(half + 1) * 512]
                v.wait_ge(wo1_mm.sem, n + 1)
                v.scalar_tensor_tensor(out=hs, in0=hs, scalar=ALPHA, in1=bank[n][:, :], op0=ALU.mult, op1=ALU.add)\
                 .then_inc(h1_sum.sem, 1)
                if half:
                    v.wait_ge(h1_sum.sem, n + 1)
                    moments(t, D, h, c1).then_inc(h1_var.sem, 1)
                    v.wait_ge(h1_var.sem, t + 1)
            v.wait_ge(h1_std.sem, 1)
            v.reciprocal(rstd[:, 0:T], std[:, 0:T]).then_inc(c1.sem, 1)
            v.wait_ge(c1.sem, c1.next())
            v.wait_ge(ln1_in.sem, 32)
            for t in range(T):
                layer_norm(h[:, t, :], xn[:, t, :], ln1g, ln1b, t, c1).then_inc(h1_ready.sem, 1)
            v.wait_ge(h1_ready.sem, T)
            for t in range(T):
                ins = v.tensor_scalar(h[:, t, :], xn[:, t, :], ALPHA, None, ALU.mult)
            ins.then_inc(c1.sem, 1)
            v.wait_ge(c1.sem, c1.next())
            take_chunks({"mm": r1_mm, "v": r1_v}, xT, K)

            v.wait_ge(lg1_mm.sem, 1)
            v.wait_ge(rt1_in.sem, 48)
            v.tensor_tensor(logits, split(bank[0][:, 0:T * 36], t=T), spread(bias36, 1, T), ALU.add).then_inc(c1.sem, 1)
            v.wait_ge(c1.sem, c1.next())
            gl, el = logits[:, :, 0:G1], logits[:, :, G1:G1 + NE1]
            gm, psel, e1, e2, w1, w2 = col[1], col[2], col[3], col[4], col[5], col[6]
            gone = split(pick[2][:, 0:T * G1], t=T)
            first_max(gl, G1, T, gm, gone, c1)
            v.tensor_tensor(split(pick[0][:, 0:T * G1], t=T), gl, spread(gm, 2, G1), ALU.subtract)\
             .then_inc(ex1_in.sem, 1)
            v.wait_ge(ex1_out.sem, 1)
            v.tensor_reduce(psel, split(pick[1][:, 0:T * G1], t=T), AX_X, ALU.add).then_inc(c1.sem, 1)
            v.wait_ge(c1.sem, c1.next())
            v.reciprocal(psel, psel).then_inc(c1.sem, 1)
            v.wait_ge(c1.sem, c1.next())
            by_group = mask1_w.rearrange("p (t g e) -> p t g e", t=T, g=G1)
            v.tensor_tensor(by_group, el.rearrange("p t (g e) -> p t g e", g=G1), spread(gone, 3, E1), ALU.mult)\
             .then_inc(c1.sem, 1)
            v.wait_ge(c1.sem, c1.next())
            es = split(pick[0][:, 16:16 + T * E1], t=T)
            v.tensor_reduce(es, by_group.rearrange("p t g e -> p t e g"), AX_X, ALU.add).then_inc(c1.sem, 1)
            v.wait_ge(c1.sem, c1.next())
            one = [split(pick[2][:, 16 + T * E1 * i:16 + T * E1 * (i + 1)], t=T) for i in range(2)]
            first_max(es, E1, T, e1, one[0], c1)
            v.scalar_tensor_tensor(out=es, in0=one[0], scalar=-HUGE, in1=es, op0=ALU.mult, op1=ALU.add)\
             .then_inc(c1.sem, 1)
            v.wait_ge(c1.sem, c1.next())
            first_max(es, E1, T, e2, one[1], c1)
            v.tensor_tensor(pick[0][:, 0:T], e2, e1, ALU.subtract).then_inc(ex1_in.sem, 1)
            v.wait_ge(ex1_out.sem, 2)
            v.tensor_scalar(w1, pick[1][:, 0:T], 1.0, None, ALU.add).then_inc(c1.sem, 1)
            v.wait_ge(c1.sem, c1.next())
            v.reciprocal(w1, w1).then_inc(c1.sem, 1)
            v.wait_ge(c1.sem, c1.next())
            v.tensor_tensor(w2, pick[1][:, 0:T], w1, ALU.mult).then_inc(c1.sem, 1)
            v.wait_ge(c1.sem, c1.next())
            v.tensor_tensor(w1, w1, psel, ALU.mult).then_inc(c1.sem, 1)
            v.wait_ge(c1.sem, c1.next())
            v.tensor_tensor(w2, w2, psel, ALU.mult).then_inc(c1.sem, 1)
            v.wait_ge(c1.sem, c1.next())
            both = split(pick[0][:, 48:48 + T * E1], t=T)
            tmp = split(pick[0][:, 80:80 + T * E1], t=T)
            v.tensor_tensor(both, one[0], one[1], ALU.add).then_inc(c1.sem, 1)
            v.wait_ge(c1.sem, c1.next())
            v.tensor_tensor(one[0], one[0], spread(w1, 2, E1), ALU.mult).then_inc(c1.sem, 1)
            v.wait_ge(c1.sem, c1.next())
            v.tensor_tensor(tmp, one[1], spread(w2, 2, E1), ALU.mult).then_inc(c1.sem, 1)
            v.wait_ge(c1.sem, c1.next())
            v.tensor_tensor(one[0], one[0], tmp, ALU.add).then_inc(c1.sem, 1)
            v.wait_ge(c1.sem, c1.next())
            for g in range(G1):
                v.tensor_tensor(mask_of(NE1)[:, :, g * E1:(g + 1) * E1], both, spread(gone[:, :, g], 2, E1), ALU.mult)\
                 .then_inc(mask1.sem, 1)
                v.tensor_tensor(gate[:, g * E1 * T:(g + 1) * E1 * T].rearrange("p (e t) -> p t e", t=T), one[0],
                                spread(gone[:, :, g], 2, E1), ALU.mult).then_inc(c1.sem, 1)
                v.wait_ge(c1.sem, c1.next())
            v.wait_ge(mask1.sem, G1)
            set_places(NE1, cum1_mm).then_inc(c1.sem, 1)
            v.wait_ge(c1.sem, c1.next())
            most, more = col[7][:, 0:1], small[:, 313:320]
            v.tensor_reduce(most, bank[3][:, T * NE1:(T + 1) * NE1], AX_X, ALU.max).then_inc(c1.sem, 1)
            v.wait_ge(c1.sem, c1.next())
            v.tensor_scalar(more, iota[:, 0:7], float(C), None, ALU.mult).then_inc(c1.sem, 1)
            v.wait_ge(c1.sem, c1.next())
            v.tensor_scalar(more, more, most, None, ALU.is_lt).then_inc(c1.sem, 1)
            v.wait_ge(c1.sem, c1.next())
            v.tensor_reduce(most, more, AX_X, ALU.add).then_inc(c1.sem, 1)
            v.wait_ge(c1.sem, c1.next())
            v.tensor_scalar(rounds_i[:, :], most, 1.0, None, ALU.add).then_inc(places1.sem, 1)
            v.wait_ge(places1.sem, 1)
            expert_round(ex1, 0, NE1 // 2, None, F1)
            n_rounds = v.value_load(rounds_i[0:1, 0:1], min_val=1, max_val=S // C)
            with v.If(n_rounds > 1):
                with v.Fori(1, n_rounds) as r:
                    v.tensor_scalar(place[:, 0:NE1 * T], place[:, 0:NE1 * T], -float(C), None, ALU.add)\
                     .then_inc(next_round.sem, 1)
                    v.wait_ge(next_round.sem, r)
                    v.nop(nofuse=True)
                    expert_round(ex1, r * (NE1 // 2), NE1 // 2, None, F1)
            c2 = Steps(sem("dve_h2"))
            for t in range(T):
                moments(t, D, h, c2).then_inc(h2_var.sem, 1)
                v.wait_ge(h2_var.sem, t + 1)
            v.wait_ge(h2_std.sem, 1)
            v.reciprocal(rstd[:, 0:T], std[:, 0:T]).then_inc(c2.sem, 1)
            v.wait_ge(c2.sem, c2.next())
            v.wait_ge(ln2_in.sem, 32)
            for t in range(T):
                ins = layer_norm(h[:, t, :], h[:, t, :], ln2g, ln2b, t, c2)
                if t < T - 1:
                    ins.then_inc(c2.sem, 1)
                    v.wait_ge(c2.sem, c2.next())
            ins.then_inc(layer_done.sem, 1)
            v.wait_ge(layer_done.sem, 1)

            v.wait_ge(gains_in.sem, 32 * LAYERS)
            with v.Fori(0, LAYERS) as l:
                c = Steps(dve2, l * DVE2)

                def scaled(sg, dst, l=l):
                    v.wait_ge(sg["std"].sem, sg["std"].at(1, l))
                    v.reciprocal(rstd[:, 0:T], std[:, 0:T]).then_inc(c.sem, 1)
                    v.wait_ge(c.sem, c.next())
                    for t in range(T):
                        v.tensor_scalar(dst[:, t, :], h[:, t, :], rstd[:, t:t + 1], None, ALU.mult)\
                         .then_inc(sg["x"].sem, 1)

                v.tensor_copy(layer_cols, all_cols[:, bass.ds(l * 33, 33)]).then_inc(cols_ready.sem, 1)
                v.wait_ge(cols_ready.sem, cols_ready.at(1, l))
                v.tensor_scalar(nsink, sink, -1.0, None, ALU.mult).then_inc(c.sem, 1)
                v.wait_ge(c.sem, c.next())
                scaled(nrm, xn)
                take_chunks(nrm, xT, K, gains[:, 0, :], l)
                v.wait_ge(second_in.sem, second_in.at(16, l))

                def rotate(n, x, dst, cos, sin, done, count, part=slice(0, P), apart=None):
                    v.tensor_tensor(rot_tmp[part, :], bank[n % 8][part, :], tab(SECOND_AT, sin)[part, :], ALU.mult)\
                     .then_inc(took2_v.sem, 1)
                    v.tensor_tensor(dst, x, tab(SECOND_AT, cos)[part, :], ALU.mult).then_inc(c.sem, 1)
                    v.wait_ge(c.sem, c.next())
                    v.wait_ge(took2_v.sem, took2_v.at(nth(PROJ2, PROJ2_ACT, n), l))
                    own = part
                    if apart is not None:
                        v.tensor_tensor(apart, dst[HD:P, :], rot_tmp[HD:P, :], ALU.add)
                        own, dst = slice(0, HD), dst[0:HD, :]
                    v.tensor_tensor(dst, dst, rot_tmp[own, :], ALU.add).then_inc(done.sem, 1)
                    v.wait_ge(done.sem, done.at(count, l))

                low = slice(HD, MLA_D)
                roped = 0
                for n, (w, i) in enumerate(PROJ2):
                    if w == "ssq":
                        v.wait_ge(took2_a.sem, took2_a.at(nth(PROJ2, PROJ2_ACT, n), l))
                        v.reciprocal(rs[:, i, :], rs[:, i, :]).then_inc(c.sem, 1)
                        v.wait_ge(c.sem, c.next())
                        for k in (2,) if i else (0, 1):
                            v.scalar_tensor_tensor(out=cq[:, k, :], in0=cq[:, k, :], scalar=lat_g[:, k:k + 1],
                                                   in1=rs[:, i, :], op0=ALU.mult, op1=ALU.mult)\
                             .then_inc(lat_ready.sem, 1)
                    if w in PROJ2_ACT:
                        continue
                    v.wait_ge(proj2.sem, proj2.at(n + 1, l))
                    b = bank[n % 8]
                    if w == "krrot":
                        rotate(n, kr_raw[low, :], kr_new[low, :], "cos_mla", "sin_mla", kpe_ready, 1, low)
                    elif w in ("uqrot", "swarot"):
                        roped += 1
                        x, names, part = ((qk2[low, 8 + i, :], ("cos_mla", "sin_mla"), low) if w == "uqrot" else
                                          (qk2[:, 4 + i, :], ("cos", "sin"), slice(0, P)))
                        rotate(n, x, x, *names, rope2, roped, part, cq[HD:P, 2, :] if (w, i) == ("swarot", 3) else None)
                    elif w == "uk":
                        v.tensor_copy(qk2[0:HD, 14 + i, :], b[0:HD, :]).then_inc(took2_v.sem, 1)
                    else:
                        v.tensor_copy(va[:, i, :], b[:, 0:384]).then_inc(took2_v.sem, 1)
                attention(HEADS2, att2, table2, place2, c, l)

                v.wait_ge(gnm["std"].sem, gnm["std"].at(1, l))
                v.reciprocal(rstd, std).then_inc(c.sem, 1)
                v.wait_ge(c.sem, c.next())
                for t in range(T):
                    for g, (c0, c1_) in enumerate(GROUPS2):
                        ins = v.tensor_scalar(o2[:, t, c0:c1_], o2[:, t, c0:c1_], rstd[:, g * T + t:g * T + t + 1], None,
                                              ALU.mult)
                    ins.then_inc(gnm["x"].sem, 1)
                take_chunks(gnm, oT2, K, gains[:, 1, :], l)
                for n in range(2 * T):
                    t, half = divmod(n, 2)
                    hs = h[:, t, half * 512:(half + 1) * 512]
                    v.wait_ge(wo2_mm.sem, wo2_mm.at(n + 1, l))
                    v.tensor_tensor(hs, hs, bank[n][:, :], ALU.add).then_inc(h2_sum.sem, 1)
                v.wait_ge(h2_sum.sem, h2_sum.at(2 * T, l))
                scaled(fnm, xn)
                take_chunks(fnm, xT, K, gains[:, 2, :], l)

                v.wait_ge(lg2_mm.sem, lg2_mm.at(1, l))
                lg = split(bank[0][:, 0:T * NE2], t=T)
                low_, ex, aff = (split(pick[i][:, 0:T * NE2], t=T) for i in range(3))
                v.tensor_reduce(col[0], lg, AX_X, ALU.max).then_inc(c.sem, 1)
                v.wait_ge(c.sem, c.next())
                v.tensor_tensor(low_, lg, spread(col[0], 2, NE2), ALU.subtract).then_inc(ex2_in.sem, 1)
                v.wait_ge(ex2_out.sem, ex2_out.at(1, l))
                v.tensor_reduce(col[1], ex, AX_X, ALU.add).then_inc(c.sem, 1)
                v.wait_ge(c.sem, c.next())
                v.reciprocal(col[1], col[1]).then_inc(c.sem, 1)
                v.wait_ge(c.sem, c.next())
                v.tensor_tensor(aff, ex, spread(col[1], 2, NE2), ALU.mult).then_inc(aff_ready.sem, 1)
                v.wait_ge(aff_ready.sem, aff_ready.at(1, l))
                v.tensor_copy(gate[:, 0:NE2 * T].rearrange("p (e t) -> p t e", t=T), aff).then_inc(c.sem, 1)
                v.wait_ge(c.sem, c.next())
                v.wait_ge(affT_mm.sem, affT_mm.at(1, l))
                v.tensor_copy(affT[0:NE2, :], bank[1][0:NE2, :]).then_inc(c.sem, 1)
                v.wait_ge(c.sem, c.next())
                v.nop(nofuse=True)
                for i in range(CAP2 // 8):
                    src = workT if i else affT
                    v.max(top8[0:NE2, :], src[0:NE2, :]).then_inc(c.sem, 1)
                    v.wait_ge(c.sem, c.next())
                    v.nop(nofuse=True)
                    v.match_replace(workT[0:NE2, :], top8[0:NE2, :], src[0:NE2, :], -1.0).then_inc(c.sem, 1)
                    v.wait_ge(c.sem, c.next())
                    v.nop(nofuse=True)
                v.tensor_scalar(maskT[0:NE2, :], workT[0:NE2, :], 0.0, None, ALU.is_lt).then_inc(maskT_ready.sem, 1)
                v.wait_ge(mask_mm.sem, mask_mm.at(1, l))
                v.tensor_copy(mask_of(NE2), split(bank[2][:, 0:T * NE2], t=T)).then_inc(mask2.sem, 1)
                set_places(NE2, cum2_mm, l).then_inc(places2.sem, 1)
                v.wait_ge(places2.sem, places2.at(1, l))
                v.nop(nofuse=True)
                expert_round(ex2, l * (NE2 // 2), NE2 // 2, gains[:, 2, :], 512)
                v.wait_ge(ex2["added"].sem, ex2["added"].at((l + 1) * (NE2 // 2 * 8)))
                v.memset(col[11], 0.0).then_inc(layer_done.sem, 1)
            assert c.n == DVE2, c.n

            v.wait_ge(fin["std"].sem, fin["std"].at(1))
            c3 = Steps(sem("dve_fin"))
            v.reciprocal(rstd[:, 0:T], std[:, 0:T]).then_inc(c3.sem, 1)
            v.wait_ge(c3.sem, c3.next())
            v.wait_ge(fin_in.sem, 16)
            for t in range(T):
                v.tensor_scalar(fin_o[:, t, :], h[:, t, :], rstd[:, t:t + 1], None, ALU.mult).then_inc(c3.sem, 1)
                v.wait_ge(c3.sem, c3.next())
                v.tensor_tensor(fin_o[:, t, :], fin_o[:, t, :], fin_g, ALU.mult).then_inc(fin_ready.sem, 1)
    return nc


def _laid_out(i):
    np_ = {n: np.asarray(v) for n, v in i.items()}
    same = ("x", "positions", "w_in", "sgu_ln_g", "sgu_ln_b", "b_spatial", "w_out", "ln1_g", "ln1_b", "b_group",
            "b_expert", "w_gate_up", "w_down", "ln2_g", "ln2_b", "mla_w_uq_2", "swa_sink_2", "w_out_2", "w_router_2",
            "w_gate_2", "w_up_2", "w_down_2", "final_norm_2")
    o = {n: np_[n] for n in same}
    o["xT"] = np_["x"][0].T
    o["w_spatialT"] = np_["w_spatial"][0].transpose(0, 2, 1)
    o["w_router1"] = np.concatenate([np_["w_group"][0], np_["w_expert"][0].transpose(1, 0, 2).reshape(D, NE1)], 1)
    w = np_["w_in_2"]
    aq, ak, av, bq, bkv, kr, cq, ck, cv = np.split(w, (256, 512, 768, 1024, 1152, 1184, 1568, 1696), axis=-1)
    cq = cq.reshape(LAYERS, D, 2, 3, HD).transpose(0, 1, 3, 2, 4).reshape(LAYERS, D, 6 * HD)
    o["w_in_2"] = np.concatenate([aq, ak, cq, ck, bq, bkv, kr, av, cv], -1)
    u = np_["mla_w_ukv_2"].reshape(LAYERS, P, MLA_H, 2, HD).transpose(0, 1, 3, 2, 4)
    o["w_ukv"] = u.reshape(LAYERS, P, 2 * MLA_H * HD)
    o["gains"] = np.concatenate([np_[n].reshape(LAYERS, -1, P).transpose(0, 2, 1) for n in (
        "attn_norm_2", "group_norm_2", "ffn_norm_2", "mla_q_norm_2", "mla_kv_norm_2")], -1)
    o["rpb"] = np.pad(np_["na_rpb_2"][..., ::-1].reshape(LAYERS, -1), ((0, 0), (RPB_PAD, RPB_PAD))).reshape(-1)
    o["base_const"], o["first_const"], o["second_const"] = shape_constants()
    return {n: np.ascontiguousarray(v) for n, v in o.items()}


def kernel(**inputs):
    import concourse.bacc as bacc
    from concourse.bass_utils import run_bass_kernel_spmd

    arrays = _laid_out(inputs)
    nc = bacc.Bacc("TRN2", target_bir_lowering=False, num_devices=1)
    aps = {n: nc.dram_tensor(f"in_{n}", v.shape, mybir.dt.from_np(v.dtype), kind="ExternalInput").ap()
           for n, v in arrays.items()}
    out = nc.dram_tensor("out_0", (1, S, D), F32, kind="ExternalOutput").ap()
    build(nc, aps, out)
    r = run_bass_kernel_spmd(nc, [{f"in_{n}": v for n, v in arrays.items()}], core_ids=[0])
    return r.results[0]["out_0"]
```

```python
from contextlib import ExitStack

import concourse.bass as bass
import numpy as np
from concourse import mybir

ALU = mybir.AluOpType
ACT = mybir.ActivationFunctionType
F32 = mybir.dt.float32
I32 = mybir.dt.int32
BF16 = mybir.dt.bfloat16
AX_X = mybir.AxisListType.X

P = 128
S = 512
T = S // P
D = 1024
K = D // P
HD = 64
BIG = 1e30
HUGE = 3e38
LN_EPS = 1e-5
RMS_EPS = 1e-6
ALPHA = 2 ** 0.25
C = 64

RING = 6
SLOT_COLS = K * 512

H1 = 8
G1, E1, F1 = 4, 8, 256
NE1 = G1 * E1
NR1 = G1 + NE1
LAYERS = 2
NE2 = 16
F2 = D
CAP2 = 2 * S // NE2
MLA_H, MLA_D, MLA_ROPE = 6, 96, 32
NA_H, SWA_H = 4, 6
GW = 64
GH = S // GW
RPB_ROW, RPB_COLS = 31, 15 * 31
RPB_PAD = 64
RPB_LEN = NA_H * RPB_COLS + 2 * RPB_PAD
BT_ROWS = 2 * GH - 2

BASE_COLS = dict(ident=P, ones=P, upto=P, iota=C, rank=8)
FIRST_COLS = dict(logcount=S, rot=P, inv=1)
SECOND_COLS = dict(rot=P, rot_mla=MLA_ROPE, cos=S, sin=S, cos_mla=S, sin_mla=S, band=3 * P, window=GW)


def places(cols):
    at, out = 0, {}
    for name, n in cols.items():
        out[name] = (at, at + n)
        at += n
    return out, at


BASE_AT, BASE_N = places(BASE_COLS)
FIRST_AT, FIRST_N = places(FIRST_COLS)
SECOND_AT, SECOND_N = places(SECOND_COLS)


def rotation(half, width):
    m = np.zeros((P, P), np.float32)
    for h in range(0, P, width):
        for i in range(half):
            m[h + half + i, h + i] = -1.0
            m[h + i, h + half + i] = 1.0
    return m


def rope_table(dim, rows):
    inv = np.float32(1.0) / (np.float32(10000.0) ** (np.arange(0, dim, 2, dtype=np.float32) / np.float32(dim)))
    ang = np.arange(S, dtype=np.float32)[None, :] * inv.astype(np.float32)[:, None]
    reps = rows // (dim // 2)
    return np.tile(np.cos(ang), (reps, 1)).astype(np.float32), np.tile(np.sin(ang), (reps, 1)).astype(np.float32)


def shape_constants():
    p = np.arange(P)[:, None]
    base = np.zeros((P, BASE_N), np.float32)
    put = lambda a, at, name, v: a.__setitem__((slice(None), slice(*at[name])), v)
    put(base, BASE_AT, "ident", np.eye(P))
    put(base, BASE_AT, "ones", 1.0)
    put(base, BASE_AT, "upto", p <= np.arange(P)[None, :])
    put(base, BASE_AT, "iota", np.arange(1, C + 1)[None, :])
    put(base, BASE_AT, "rank", np.arange(8, 0, -1)[None, :])

    first = np.zeros((P, FIRST_N), np.float32)
    dist = p + (T - 1) * P - np.arange(S)[None, :]
    n = (dist <= 128) * 1 + (dist % 4 == 0) * 1 + (dist % 16 == 0) * 1
    put(first, FIRST_AT, "logcount", np.where((dist >= 0) & (n > 0), -np.log(np.maximum(n, 1)), BIG))
    put(first, FIRST_AT, "rot", rotation(8, HD))
    inv = (np.float32(500000.0) ** (-np.arange(0, 16, 2, dtype=np.float32) / np.float32(16))).astype(np.float32)
    d = np.arange(P) % HD
    put(first, FIRST_AT, "inv", np.where(d < 16, inv[d % 8], 0.0)[:, None])

    second = np.zeros((P, SECOND_N), np.float32)
    put(second, SECOND_AT, "rot", rotation(HD // 2, HD))
    put(second, SECOND_AT, "rot_mla", np.where(p >= HD, rotation(MLA_ROPE // 2, MLA_ROPE)[:, HD:HD + MLA_ROPE], 0.0))
    c, s = rope_table(HD, P)
    put(second, SECOND_AT, "cos", c)
    put(second, SECOND_AT, "sin", s)
    c, s = rope_table(MLA_ROPE, P)
    put(second, SECOND_AT, "cos_mla", c)
    put(second, SECOND_AT, "sin_mla", s)
    put(second, SECOND_AT, "band", np.where(np.abs(p + P - np.arange(3 * P)[None, :]) <= P, 0.0, BIG))
    col, key = np.arange(P)[:, None] % GW, np.arange(GW)[None, :]
    start = np.clip(col - 8, 0, GW - 16)
    put(second, SECOND_AT, "window", np.where((key >= start) & (key < start + 16), 0.0, BIG)[:, ::-1])
    return base, first, second


PROJ1 = [("qk", 0)]
for _c in range(1, 8):
    PROJ1 += [("qk", _c), ("rot", _c - 1)]
PROJ1 += [("v", 0), ("rot", 7)] + [("v", t) for t in range(1, T)]
PROJ1 += [("u", c) for c in range(4)] + [("gate", t) for t in range(T)]
PROJ1_ACT = ("qk", "u", "gate")

PROJ2 = [("cq", 0), ("cq", 1), ("ckv", 0), ("kr", 0), ("ssq", 0), ("na", 0), ("ssq", 1), ("krrot", 0), ("na", 1)]
PROJ2 += [("uq", h) for h in range(MLA_H)] + [("na", 2)] + [("uqrot", h) for h in range(MLA_H)]
PROJ2 += [("na", 3)] + [("uk", c) for c in range(MLA_H // 2)] + [("swa", 0)] + [("uv", t) for t in range(T)]
PROJ2 += [("swa", 1), ("swarot", 0), ("swa", 2), ("swarot", 1), ("swa", 3), ("swarot", 2), ("va", 0), ("swarot", 3)]
PROJ2 += [("va", t) for t in range(1, T)]
PROJ2_ACT = ("cq", "ckv", "kr", "na", "ssq", "uq", "uv", "swa")

HEADS1 = [("dilated", h) for h in range(H1)]
HEADS2 = [("mla", h) for h in range(MLA_H)] + [("swa", h) for h in range(SWA_H)] + [("na", h) for h in range(NA_H)]


def first_key(kind, t):
    return max(t - 1, 0) if kind == "swa" else 0


def end_key(kind, t):
    return {"dilated": t + 1, "swa": min(t + 2, T)}.get(kind, T)


def nth(plan, takers, i):
    mine = plan[i][0] in takers
    return sum((w in takers) == mine for w, _ in plan[:i + 1])


IN2 = [(1024, 416), (0, 512), (512, 512), (1440, 384)]
SLOT_OF2 = {0: ("cq", "ckv", "kr"), 1: ("na",), 2: ("swa",), 3: ("va",)}
GROUPS2 = ((0, 256), (256, 640), (640, 1024))
TWO_PI_PARTS = (6.28125, 0.0019340515136718750, float(2 * np.pi - 6.28125 - 0.0019340515136718750))
PI_BELOW = 3.1415925
GATE_STD = 12
DVE2 = 63


def last_of(plan, what, i):
    return plan.index((what, i))


class Signal:

    def __init__(self, sem, per=0, first=0):
        self.sem, self.per, self.first = sem, per, first

    def at(self, n, l=0):
        return l * self.per + (self.first + n)


class Steps:

    def __init__(self, sem, base=0):
        self.sem, self.base, self.n = sem, base, 0

    def next(self):
        self.n += 1
        return self.base + self.n


def build(nc, a, out):
    with ExitStack() as ctx:
        def sb(name, cols, dt=F32):
            return ctx.enter_context(nc.sbuf_tensor(name, [P, cols], dt))

        def sem(name):
            return ctx.enter_context(nc.semaphore(name))

        def sig(name, per=0):
            return Signal(sem(name), per)

        def split(ap, **n):
            (name, count), = n.items()
            return ap.rearrange(f"p ({name} x) -> p {name} x", **{name: count})

        def spread(ap, axis, n):
            v = ap.unsqueeze(axis)
            shape = list(v.shape)
            shape[axis] = n
            return v.to_broadcast(shape)

        h_sb = sb("h", T * D)
        x_sb = sb("xT_or_o", K * S)
        arena = sb("arena", 14848)
        tables = sb("tables", SECOND_N)
        probs = sb("probs", 4 * S)
        base = sb("base", BASE_N)
        small = sb("small", 321 + 33 * LAYERS)
        rounds_i = sb("rounds", 1, I32)
        ring = sb("ring", RING * SLOT_COLS)
        bank = [ctx.enter_context(nc.psum_tensor(f"bank{i}", [P, 512], F32)) for i in range(8)]

        h = split(h_sb[:, :], t=T)
        xT = split(x_sb[:, :], k=K)
        slot = [split(ring[:, i * SLOT_COLS:(i + 1) * SLOT_COLS], k=K) for i in range(RING)]
        ident, ones, upto, iota, rank = (base[:, slice(*BASE_AT[n])] for n in ("ident", "ones", "upto", "iota", "rank"))

        def area(start, n, **parts):
            v = arena[:, start:start + n]
            return split(v, **parts) if parts else v

        def tab(at, name):
            return tables[:, slice(*at[name])]

        qk1 = area(0, 4096, k=8)
        v1 = area(4096, 2048, t=T)
        u1 = area(6144, 2048, k=4)
        g1 = area(8192, 2048, t=T)
        mix1 = area(10240, 4096, k=8)
        ln1g, ln1b = area(6144, 1024), area(7168, 1024)
        ang, turns, sin_arg, cos_arg = (area(8192 + 512 * i, 512) for i in range(4))
        turns_i = area(10240, 512).bitcast(I32)
        over = area(10752, 512)
        pos_i = area(11264, 512).bitcast(I32)
        o = FIRST_N + 7 & ~7
        cos1, sin1 = tables[:, o:o + 512], tables[:, o + 512:o + 1024]
        bsp = split(tables[:, o + 1024:o + 1536], c=4)
        o1 = split(x_sb[:, 0:2048], t=T)
        wsT = split(x_sb[:, 2048:3072], g=8)
        sgu_g, sgu_b = x_sb[:, 3072:3584], x_sb[:, 3584:4096]
        rot_tmp = probs[:, 1024:1536]
        ln2g, ln2b = probs[:, 0:1024], probs[:, 1024:2048]

        qk2 = area(0, 10240, k=20)
        va = area(10240, 1536, t=T)
        vm = area(11776, 1536, t=T)
        cq = area(13312, 1536, k=3)
        sq = area(11776, 1536, k=3)
        rs = area(10240, 1024, k=2)
        wuq = area(2048, 1152, k=2)
        wukv = area(3200, 768)
        kr_raw, kr_new = probs[:, 0:512], probs[:, 512:1024]
        o2 = split(x_sb[:, :], t=T)
        oT2 = area(8192, 4096, k=8)
        junk = area(4096, 4096, t=T)
        bt = [tables[:, SECOND_AT[n][0]:SECOND_AT[n][0] + BT_ROWS * GW] for n in ("cos", "cos_mla")]
        fin_g = area(8192, 1024)
        fin_o = area(0, 4096, t=T)

        prob = [probs[:, 0:512], probs[:, 512:1024]]
        probT = [probs[:, 1024:1536], probs[:, 1536:2048]]

        xn = area(0, 4096, t=T)
        sel = area(4096, 512, t=T)
        selg = area(4608, 512, t=T)
        selgT = area(5120, 512)
        xs = area(5632, 1024, k=K)
        silu = area(6656, 512)
        hid = area(7168, 512)
        hidT = area(7680, 512)
        ys = area(8192, 1024)
        x_part = [split(v.bitcast(BF16), t=T) for v in (x_sb[:, 0:2048], x_sb[:, 2048:4096], tables[:, 0:2048])]
        sels = [sel, selg]
        sel_b = split(area(10240, 256).bitcast(BF16), t=T)
        selT_b = area(10496, 256).bitcast(BF16)
        xg = area(9216, 1024)
        y_part = [area(13264 + 512 * i, 512).bitcast(BF16) for i in range(3)]
        place_gate = small[:, 386:387]
        place = area(10752, 128)
        gate = area(10880, 128)
        rt = 11008
        logits = area(rt, 144, t=T)
        pick = [area(rt + 144 * (i + 1), 144) for i in range(3)]
        mask_s = area(rt + 576, 128)
        affT, workT, maskT = (area(rt + 704 + 512 * i, 512) for i in range(3))
        top8 = area(rt + 2240, 8)
        mask1_w = workT[:, 0:128]
        lgT = workT
        router1_w = area(4096, K * NR1, k=K)
        router2_w = area(13264, K * NE2, k=K)

        negmax, total = small[:, 0:64], small[:, 64:128]
        ss, std, rstd = small[:, 128:140], small[:, 140:152], small[:, 152:164]
        layer_cols = small[:, 164:197]
        gains = split(small[:, 164:188], k=3)
        lat_g = small[:, 188:191]
        all_cols = small[:, 320:320 + 33 * LAYERS]
        sink, nsink, esink = small[:, 191:197], small[:, 197:203], small[:, 203:207]
        rtotal = small[:, 207:211]
        eps_ln, eps_rms = small[:, 211:212], small[:, 212:213]
        bias_r = small[:, 213:249]
        bn = small[:, 249:261]
        mv = small[:, 261:269]
        col = [small[:, 269 + 4 * i:273 + 4 * i] for i in range(12)]


        def view1(kind, i):
            keys = mix1[:, i // 2, :] if i % 2 else qk1[:, 4 + i // 2, :]
            return qk1[:, i // 2, :], keys, lambda c: v1[:, c, i // 2 * P:i // 2 * P + P]

        def view2(kind, i):
            if kind == "mla":
                return qk2[0:MLA_D, 8 + i, :], qk2[0:MLA_D, 14 + i, :], lambda c: vm[:, c, i // 2 * P:i // 2 * P + P]
            if kind == "swa":
                return qk2[:, 4 + i % 3, :], cq[:, 2, :] if i // 3 else qk2[:, 7, :], lambda c: va[:, c, 256:384]
            keys = cq[:, i // 2, :] if i % 2 else qk2[:, 2 + i // 2, :]
            return qk2[:, i // 2, :], keys, lambda c: va[:, c, i // 2 * P:i // 2 * P + P]

        def second_of_two(kind, i):
            return i // 3 if kind == "swa" else i % 2

        def table1(kind, i, t):
            return tab(FIRST_AT, "logcount")[:, (T - 1 - t) * P:]

        def table2(kind, i, t):
            if kind == "swa":
                y = (first_key(kind, t) - t + 1) * P
                return tab(SECOND_AT, "band")[:, y:y + (end_key(kind, t) - first_key(kind, t)) * P]
            b = bt[i % 2]
            return bass.AP(b.tensor, b.offset + (GH - 2 - 2 * t) * GW + GW - 1, [list(b.ap[0]), [GW, GH], [-1, GW]])

        def place2(kind, i):
            c0 = {"na": 0, "mla": 256, "swa": 640}[kind] + i * HD
            return o2[:, :, c0:c0 + HD]

        def mask_of(n):
            return split(mask_s[:, 0:T * n], t=T)

        landed1 = [sem(f"landed1_{i}") for i in range(RING)]
        landed2 = [sem(f"landed2_{i}") for i in range(RING)]
        x_in = [sig("x_in0"), sig("x_in1")]
        h_in, base_in, first_in, pos_in = (sig(n) for n in ("h_in", "base_in", "first_in", "pos_in"))
        sgu_in, ws_in, bsp_in, ln1_in, ln2_in, rt1_in = (
            sig(n) for n in ("sgu_in", "ws_in", "bsp_in", "ln1_in", "ln2_in", "rt1_in"))
        sin_args, rope1, dve1 = (sig(n) for n in ("sin_args", "rope1", "dve1"))
        proj1, took1_a, took1_v, qk1_ready, padded1 = (
            sig(n) for n in ("proj1", "took1_a", "took1_v", "qk1_ready", "padded1"))
        g1_var, g1_std, g1_ready = (sig(n) for n in ("g1_var", "g1_std", "g1_ready"))

        def attention_signals(n, heads):
            m = T * len(heads) if n == 2 else 0
            return {name: sig(f"{name}{n}", m // div) for name, div in dict(
                score=1, shifted=1, prob=1, turned=1, probT_v=2, probT_a=2, pv=1, head_out=4).items()}

        att1, att2 = attention_signals(1, HEADS1), attention_signals(2, HEADS2)
        sunk = sig("sunk", SWA_H)
        oT_mm, oT_a, oT_v, sgu_mm, sgu_ok, ws_masked = (
            sig(n) for n in ("oT_mm", "oT_a", "oT_v", "sgu_mm", "sgu_ok", "ws_masked"))
        wo1_mm, h1_sum, h1_var, h1_std, h1_ready = (
            sig(n) for n in ("wo1_mm", "h1_sum", "h1_var", "h1_std", "h1_ready"))
        r1_mm, r1_a, r1_v, lg1_mm, ex1_in, ex1_out, mask1, cum1_mm, places1 = (
            sig(n) for n in ("r1_mm", "r1_a", "r1_v", "lg1_mm", "ex1_in", "ex1_out", "mask1", "cum1_mm", "places1"))

        def expert_signals(n):
            return {name: sig(f"{name}{n}") for name in (
                "sel", "selg", "gath", "xs", "gu", "silu", "hid", "hT", "hT_ok", "dn", "selgT", "selgT_ok", "ys",
                "scat", "added") if (name, n) != ("selg", 1)}

        ex1, ex2 = expert_signals(1), expert_signals(2)
        x_rounded, x_parts, xg_ready, turned_x, ys_parts, sel_ok = (
            sig(n) for n in ("x_rounded", "x_parts", "xg_ready", "turned_x", "ys_parts", "sel_ok"))
        next_round = sig("next_round")
        h2_var, h2_std = Signal(h1_var.sem, 0, T), Signal(h1_std.sem, 0, T)
        layer_done = sig("layer_done", 1)
        cols_ready = sig("cols_ready", 1)
        second_in, ukv_in = sig("second_in", 16), sig("ukv_in", 32)
        gains_in, rt2_in = sig("gains_in"), sig("rt2_in", 16)
        bias_in, bias_ready = [sig("bias_in0", 64), sig("bias_in1", 64)], sig("bias_ready", NA_H)

        norm_sems = {name: sem(f"norm_{name}") for name in ("ss", "std", "x", "mm", "a", "v")}

        def norm_signals(stage):
            return {name: Signal(norm_sems[name], (2 if name in ("ss", "std") else 3) * m, stage * m)
                    for name, m in dict(ss=1, std=1, x=T, mm=K, a=K // 2, v=K // 2).items()}

        nrm, gnm, fnm = (norm_signals(stage) for stage in range(3))
        lgT1_mm, lgT1_ok, lgT2_mm, lgT2_ok = sig("lgT1_mm"), sig("lgT1_ok"), sig("lgT2_mm", 1), sig("lgT2_ok", 1)
        fnm_ss, fnm_std = sig("fnm_ss", T), sig("fnm_std", T)
        h_tiles = sig("h_tiles")
        proj2 = sig("proj2", len(PROJ2))
        took2_a = sig("took2_a", sum(w in PROJ2_ACT for w, _ in PROJ2))
        took2_v = sig("took2_v", sum(w not in PROJ2_ACT for w, _ in PROJ2))
        lat_ready, kpe_ready, keys_set, rope2 = (sig(n, p) for n, p in (
            ("lat_ready", 3), ("kpe_ready", 1), ("keys_set", MLA_H + 3), ("rope2", MLA_H + 4)))
        wo2_mm, h2_sum = sig("wo2_mm", 2 * T), sig("h2_sum", 2 * T)
        lg2_mm, ex2_in, ex2_out, aff_ready, affT_mm, maskT_ready, mask_mm, mask2, cum2_mm, places2 = (
            sig(n, 1) for n in ("lg2_mm", "ex2_in", "ex2_out", "aff_ready", "affT_mm", "maskT_ready", "mask_mm",
                                "mask2", "cum2_mm", "places2"))
        fin_in, fin_ready, stored = (sig(n) for n in ("fin_in", "fin_ready", "stored"))
        dve2 = sem("dve2")

        block = ctx.enter_context(nc.Block())

        w_in1 = a["w_in"][0].rearrange("(k p) f -> p k f", p=P)
        w_out1 = a["w_out"][0].rearrange("(k p) f -> p k f", p=P)
        w_gu1 = a["w_gate_up"][0].rearrange("g e (k p) f -> p (g e) k f", p=P)
        w_dn1 = a["w_down"][0].rearrange("g e (c p) d -> p (g e c) d", p=P)
        w_in2 = a["w_in_2"].rearrange("l (k p) f -> p l k f", p=P)
        w_out2 = a["w_out_2"].rearrange("l (k p) f -> p l k f", p=P)
        w_gate2, w_up2, w_down2 = (a[n].rearrange("l e (k p) f -> p (l e) k f", p=P)
                                   for n in ("w_gate_2", "w_up_2", "w_down_2"))

        SET1 = ((1, "gu", 0), (2, "gu", 1), (3, "dn", 0), (4, "gu", 2), (0, "gu", 3), (5, "dn", 2))
        SET1_OF = {s: kind for s, kind, _ in SET1}
        RUNS1 = NE1 // 4
        SCATTER1 = (6, 7, 4, 5)
        BEFORE1 = {s: 1 for s in range(RING)}
        PER_SLOT2 = 1 + NE2

        @block.sync
        def _(sp):
            for half in range(2):
                ks = slice(4 * half, 4 * half + 4)
                sp.dma_start(xT[:, ks], a["xT"].rearrange("(k p) s -> p k s", p=P)[:, ks]).then_inc(x_in[half].sem, 16)
                sp.dma_start(slot[0][:, ks], w_in1[:, ks, 0:512]).then_inc(x_in[half].sem, 16)
            for i in range(1, 5):
                sp.dma_start(slot[i], w_in1[:, :, 512 * i:512 * i + 512]).then_inc(landed1[i], 16)
            sp.dma_start(h, a["x"][0].rearrange("(t p) d -> p t d", p=P)).then_inc(h_in.sem, 16)
            sp.dma_start(slot[5], w_out1[:, :, 0:512]).then_inc(landed1[5], 16)
            sp.wait_ge(proj1.sem, 1 + last_of(PROJ1, "qk", 3))
            sp.dma_start(slot[0], w_out1[:, :, 512:1024]).then_inc(landed1[0], 16)

            def load(s, kind, e, e4):
                if kind == "gu":
                    sp.dma_start(slot[s], w_gu1[:, e4 * 4 + e]).then_inc(landed1[s], 16)
                else:
                    sp.dma_start(ring[:, s * SLOT_COLS:(s + 1) * SLOT_COLS].rearrange("p (c d) -> p c d", d=D),
                                 w_dn1[:, bass.ds((e4 * 4 + e) * 2, 4)]).then_inc(landed1[s], 16)

            sp.wait_ge(proj1.sem, len(PROJ1))
            for s, kind, e in SET1[:4]:
                load(s, kind, e, 0)
            sp.wait_ge(wo1_mm.sem, 2 * T)
            for s, kind, e in SET1[4:]:
                load(s, kind, e, 0)

            def next_set(run, e4):
                for s, kind, e in SET1:
                    if kind == "gu":
                        sp.wait_ge(ex1["gu"].sem, ex1["gu"].at((run - 1) * 2 + (e // 2 + 1)))
                    else:
                        sp.wait_ge(ex1["dn"].sem, ex1["dn"].at((run - 1) * 4 + (e + 2)))
                    load(s, kind, e, e4)

            with sp.Fori(1, RUNS1) as e4:
                next_set(e4, e4)
            sp.wait_ge(places1.sem, 1)
            n_rounds = sp.value_load(rounds_i[0:1, 0:1], min_val=1, max_val=S // C)
            with sp.If(n_rounds > 1):
                with sp.Fori(1, n_rounds) as r:
                    with sp.Fori(0, RUNS1) as e4:
                        next_set(r * RUNS1 + e4, e4)

            def load2(s, w, i, half, n=512):
                sp.dma_start(slot[s][:, :, 0:n], w[:, i, :, half:half + n]).then_inc(landed2[s], 16)

            for s, w, (c0, n) in [(i, w_in2, c) for i, c in enumerate(IN2)] + [(4, w_out2, (0, 512)),
                                                                               (5, w_out2, (512, 512))]:
                if SET1_OF[s] == "gu":
                    sp.wait_ge(ex1["gu"].sem, ex1["gu"].at(n_rounds * (RUNS1 * 2)))
                else:
                    sp.wait_ge(ex1["dn"].sem, ex1["dn"].at(n_rounds * (RUNS1 * 4)))
                load2(s, w, 0, c0, n)

            EXPERT = ((w_gate2, 0), (w_gate2, 512), (w_up2, 0), (w_up2, 512), (w_down2, 0), (w_down2, 512))

            def released(s, e):
                if s < 4:
                    sp.wait_ge(ex2["gu"].sem, ex2["gu"].at((e - 1) * 2 + (s // 2 + 1)))
                else:
                    sp.wait_ge(ex2["dn"].sem, ex2["dn"].at(e))

            def layer(l):
                for s, (w, half) in enumerate(EXPERT):
                    if s < 4:
                        used = 1 + max(i for i, g in enumerate(PROJ2) if g[0] in SLOT_OF2[s])
                        sp.wait_ge(proj2.sem, proj2.at(used, l))
                    else:
                        sp.wait_ge(wo2_mm.sem, wo2_mm.at(2 * T, l))
                    load2(s, w, l * NE2, half)
                with sp.Fori(1, NE2) as e:
                    for s, (w, half) in enumerate(EXPERT):
                        released(s, l * NE2 + e)
                        load2(s, w, l * NE2 + e, half)

            with sp.Fori(0, LAYERS - 1) as l:
                layer(l)
                for s, (c0, n) in enumerate(IN2):
                    released(s, (l + 1) * NE2)
                    load2(s, w_in2, l + 1, c0, n)
                for s in (4, 5):
                    released(s, (l + 1) * NE2)
                    load2(s, w_out2, l + 1, 512 * (s - 4))
            layer(LAYERS - 1)
            for t in range(T):
                sp.wait_ge(fin_ready.sem, t + 1)
                sp.dma_start(out[0, t * P:(t + 1) * P, :], fin_o[:, t, :]).then_inc(stored.sem, 16)
            sp.wait_ge(stored.sem, 16 * T)

        @block.gpsimd
        def _(pool):
            pool.dma_start(pos_i, a["positions"].rearrange("a s -> (a s)").partition_broadcast(P))\
                .then_inc(pos_in.sem, 16)
            pool.dma_start(tables[:, 0:FIRST_N], a["first_const"]).then_inc(first_in.sem, 16)
            pool.dma_start(base[:, :], a["base_const"]).then_inc(base_in.sem, 16)
            for i in range(LAYERS):
                pool.dma_start(all_cols[:, 33 * i:33 * i + 27], a["gains"][i]).then_inc(gains_in.sem, 16)
                pool.dma_start(all_cols[:, 33 * i + 27:33 * i + 33], a["swa_sink_2"][i].partition_broadcast(P))\
                    .then_inc(gains_in.sem, 16)
            for g in range(8):
                pool.dma_start(bsp[HD * (g % 2):HD * (g % 2) + HD, g // 2, :],
                               a["b_spatial"][0, g].partition_broadcast(HD)).then_inc(bsp_in.sem, 16)
            pool.dma_start(bias_r[:, 0:G1], a["b_group"][0].partition_broadcast(P)).then_inc(rt1_in.sem, 16)
            pool.dma_start(bias_r[:, G1:G1 + NE1], a["b_expert"][0].rearrange("g e -> (g e)").partition_broadcast(P))\
                .then_inc(rt1_in.sem, 16)
            pool.wait_ge(qk1_ready.sem, 1)
            pool.memset(mix1[0:HD, 0:4, :], 0.0).then_inc(padded1.sem, 1)
            pool.wait_ge(padded1.sem, 1)
            pool.wait_ge(qk1_ready.sem, 8)
            pool.memset(qk1[HD:P, 4:8, :], 0.0).then_inc(padded1.sem, 1)
            pool.wait_ge(padded1.sem, 2)
            pool.wait_ge(proj1.sem, len(PROJ1))
            pool.dma_start(sgu_g, a["sgu_ln_g"][0].partition_broadcast(P)).then_inc(sgu_in.sem, 16)
            pool.dma_start(sgu_b, a["sgu_ln_b"][0].partition_broadcast(P)).then_inc(sgu_in.sem, 16)
            pool.dma_start(wsT, a["w_spatialT"].rearrange("g s t -> s g t")).then_inc(ws_in.sem, 16)
            pool.wait_ge(ws_in.sem, 16)
            pool.wait_ge(base_in.sem, 16)
            for g in range(8):
                pool.tensor_tensor(wsT[:, g, :], wsT[:, g, :], upto, ALU.mult).then_inc(ws_masked.sem, 1)
            pool.wait_ge(oT_mm.sem, 4)
            pool.dma_start(router1_w, a["w_router1"].rearrange("(k p) e -> p k e", p=P)).then_inc(rt1_in.sem, 16)
            pool.wait_ge(sgu_ok.sem, 4)
            pool.dma_start(ln1g, a["ln1_g"][0].partition_broadcast(P)).then_inc(ln1_in.sem, 16)
            pool.dma_start(ln1b, a["ln1_b"][0].partition_broadcast(P)).then_inc(ln1_in.sem, 16)
            pool.wait_ge(wo1_mm.sem, 2 * T)
            pool.dma_start(ln2g, a["ln2_g"][0].partition_broadcast(P)).then_inc(ln2_in.sem, 16)
            pool.dma_start(ln2b, a["ln2_b"][0].partition_broadcast(P)).then_inc(ln2_in.sem, 16)
            for t in range(T):
                pool.wait_ge(x_rounded.sem, t + 1)
                pool.tensor_tensor(xn[:, t, :], xn[:, t, :], x_part[0][:, t, :], ALU.subtract).then_inc(x_parts.sem, 1)
            pool.wait_ge(x_parts.sem, T)
            for t in range(T):
                pool.wait_ge(x_rounded.sem, T + t + 1)
                pool.tensor_tensor(x_part[2][:, t, :], xn[:, t, :], x_part[1][:, t, :], ALU.subtract)\
                    .then_inc(x_parts.sem, 1)
            pool.wait_ge(layer_done.sem, 1)
            pool.dma_start(tables[:, 0:SECOND_N], a["second_const"]).then_inc(second_in.sem, 16)
            with pool.Fori(0, LAYERS) as l:
                pool.wait_ge(nrm["mm"].sem, nrm["mm"].at(K, l))
                pool.nop(nofuse=True)
                pool.dma_start(wuq, a["mla_w_uq_2"][l].rearrange("(k p) f -> p k f", p=P)).then_inc(ukv_in.sem, 16)
                pool.dma_start(wukv, a["w_ukv"][l]).then_inc(ukv_in.sem, 16)
                pool.wait_ge(kpe_ready.sem, kpe_ready.at(1, l))
                pool.nop(nofuse=True)
                for i in range(MLA_H):
                    pool.tensor_copy(qk2[HD:MLA_D, 14 + i, :], kr_new[HD:MLA_D, :]).then_inc(keys_set.sem, 1)
                pool.wait_ge(keys_set.sem, keys_set.at(MLA_H, l))
                pool.nop(nofuse=True)
                pool.memset(qk2[HD:P, 2:4, :], 0.0).then_inc(keys_set.sem, 1)
                pool.wait_ge(keys_set.sem, keys_set.at(MLA_H + 1, l))
                pool.nop(nofuse=True)
                pool.wait_ge(proj2.sem, proj2.at(1 + last_of(PROJ2, "uv", T - 1), l))
                pool.nop(nofuse=True)
                pool.memset(cq[0:HD, :, :], 0.0).then_inc(keys_set.sem, 1)
                pool.wait_ge(keys_set.sem, keys_set.at(MLA_H + 2, l))
                pool.nop(nofuse=True)
                pool.wait_ge(rope2.sem, rope2.at(rope2.per, l))
                pool.nop(nofuse=True)
                pool.memset(qk2[HD:P, 7, :], 0.0).then_inc(keys_set.sem, 1)
                for i in range(NA_H):
                    if i == 0:
                        pool.wait_ge(took2_a.sem, took2_a.at(took2_a.per, l))
                        pool.wait_ge(took2_v.sem, took2_v.at(took2_v.per, l))
                        pool.wait_ge(rope2.sem, rope2.at(rope2.per, l))
                        pool.nop(nofuse=True)
                    if i >= 2:
                        pool.wait_ge(att2["shifted"].sem, att2["shifted"].at(T * (len(HEADS2) - NA_H + i - 1), l))
                        pool.nop(nofuse=True)
                    for r in range(2):
                        src = bass.AP(a["rpb"].tensor,
                                      l * RPB_LEN + (RPB_PAD + i * RPB_COLS + (1 - r) * RPB_ROW + 15 - (GW - 1)),
                                      [[1, GW], [RPB_ROW, BT_ROWS], [1, GW]])
                        pool.dma_start(split(bt[i % 2][GW * r:GW * r + GW, :], j=BT_ROWS), src)\
                            .then_inc(bias_in[i % 2].sem, 16)
                pool.wait_ge(gnm["mm"].sem, gnm["mm"].at(K, l))
                pool.nop(nofuse=True)
                pool.dma_start(router2_w, a["w_router_2"][l].rearrange("(k p) e -> p k e", p=P))\
                    .then_inc(rt2_in.sem, 16)
                pool.wait_ge(wo2_mm.sem, wo2_mm.at(2 * T, l))
                pool.nop(nofuse=True)
                pool.dma_start(tables[:, 0:SECOND_N], a["second_const"]).then_inc(second_in.sem, 16)
            pool.wait_ge(layer_done.sem, 1 + LAYERS)
            pool.dma_start(fin_g, a["final_norm_2"].partition_broadcast(P)).then_inc(fin_in.sem, 16)

        @block.tensor
        def _(pe):
            def product(o, pairs):
                for i, (lhs, rhs) in enumerate(pairs):
                    mm = pe.matmul(o, lhs, rhs, start=(i == 0), stop=(i == len(pairs) - 1))
                return mm

            def turn(src, chunks, sg, l=0, b0=0):
                for c in range(chunks):
                    for t in range(T):
                        mm = pe.transpose(bank[b0 + c][:, t * P:(t + 1) * P], src[:, t, c * P:(c + 1) * P], ident)
                    mm.then_inc(sg.sem, 1)

            def turn_tiles(src, ready, mm_sg, l=0):
                for t in range(T):
                    pe.wait_ge(ready.sem, ready.at(t + 1, l))
                    for c in range(K):
                        mm = pe.transpose(bank[c][:, t * P:(t + 1) * P], src[:, t, c * P:(c + 1) * P], ident)
                        if t == T - 1:
                            mm.then_inc(mm_sg.sem, 1)

            def first_product(o, pairs, a_sg, v_sg, l=0):
                for k, (lhs, rhs) in enumerate(pairs):
                    if k % 2:
                        pe.wait_ge(v_sg.sem, v_sg.at(k // 2 + 1, l))
                    else:
                        pe.wait_ge(a_sg.sem, a_sg.at(k // 2 + 1, l))
                    mm = pe.matmul(o, lhs, rhs, start=(k == 0), stop=(k == K - 1))
                return mm

            def attention(heads, sg, view, l=0):
                units = [(n, kind, i, t) for n, (kind, i) in enumerate(heads) for t in range(T)]
                for u in range(len(units) + 2):
                    if u < len(units):
                        n, kind, i, t = units[u]
                        q, k, _ = view(kind, i)
                        k0, k1 = first_key(kind, t) * P, end_key(kind, t) * P
                        pe.matmul(bank[u % 2][:, 0:k1 - k0], q[:, t * P:(t + 1) * P], k[:, k0:k1], start=True,
                                  stop=True).then_inc(sg["score"].sem, 1)
                    if 1 <= u <= len(units):
                        n, kind, i, t = units[u - 1]
                        pe.wait_ge(sg["prob"].sem, sg["prob"].at(u, l))
                        for c in range(end_key(kind, t) - first_key(kind, t)):
                            mm = pe.transpose(bank[2 + (u - 1) % 2][:, c * P:(c + 1) * P],
                                              prob[(u - 1) % 2][:, c * P:(c + 1) * P], ident)
                        mm.then_inc(sg["turned"].sem, 1)
                    if u >= 2:
                        w = u - 2
                        n, kind, i, t = units[w]
                        _, _, v = view(kind, i)
                        probT_ok = sg["probT_a" if w % 2 else "probT_v"]
                        pe.wait_ge(probT_ok.sem, probT_ok.at(w // 2 + 1, l))
                        if t == 0 and n >= 2:
                            pe.wait_ge(sg["head_out"].sem, sg["head_out"].at(n - 1, l))
                        k0 = first_key(kind, t)
                        product(bank[4 + n % 2][:, t * P:(t + 1) * P],
                                [(probT[w % 2][:, (c - k0) * P:(c - k0 + 1) * P], v(c))
                                 for c in range(k0, end_key(kind, t))]).then_inc(sg["pv"].sem, 1)

            def columns(o, halves):
                for i in range(len(halves[0])):
                    for n, pairs in enumerate(halves):
                        lhs, rhs = pairs[i]
                        mm = pe.matmul(o[C * n:C * n + C, :], lhs, rhs, start=(i == 0), stop=(i == len(pairs) - 1))
                return mm

            def gather(X, it):
                pe.wait_ge(X["sel"].sem, X["sel"].at(it + 1))
                for c in range(K):
                    mm = product(bank[c // 4][:, c % 4 * P:c % 4 * P + P],
                                 [(xn[:, t, c * P:(c + 1) * P], sel[:, t, :]) for t in range(T)])
                mm.then_inc(X["gath"].sem, 1)

            def turn_hidden(X, n, chunks):
                pe.wait_ge(X["hid"].sem, X["hid"].at(n + 1))
                for c in range(chunks):
                    mm = pe.transpose(bank[2][:, c * P:(c + 1) * P], hid[:, c * P:(c + 1) * P], ident)
                mm.then_inc(X["hT"].sem, 1)

            def turn_gates(X, it):
                pe.wait_ge(X["selg"].sem, X["selg"].at(it + 1))
                for t in range(T):
                    mm = pe.transpose(bank[3][:, t * P:(t + 1) * P], selg[:, t, :], ident)
                mm.then_inc(X["selgT"].sem, 1)

            def scatter(X, it):
                pe.wait_ge(X["selgT_ok"].sem, X["selgT_ok"].at(it + 1))
                pe.wait_ge(X["ys"].sem, X["ys"].at(it * 2 + 2))
                for g in range(2 * T):
                    if g >= 2:
                        pe.wait_ge(X["added"].sem, X["added"].at(it * 8 + g - 1))
                    t, half = divmod(g, 2)
                    pe.matmul(bank[6 + g % 2][:, :], selgT[:, t * P:(t + 1) * P], ys[:, half * 512:(half + 1) * 512],
                              start=True, stop=True).then_inc(X["scat"].sem, 1)

            def places(n, sg):
                mm = pe.matmul(bank[3][:, 0:T * n], upto, mask_s[:, 0:T * n], start=True, stop=False)
                for d in range(1, T):
                    mm = pe.matmul(bank[3][:, d * n:T * n], ones, mask_s[:, 0:(T - d) * n], start=False,
                                   stop=(d == T - 1))
                if n == NE1:
                    mm = product(bank[3][:, T * n:(T + 1) * n], [(ones, mask_of(n)[:, t, :]) for t in range(T)])
                mm.then_inc(sg.sem, 1)

            for n, (w, i) in enumerate(PROJ1):
                b = bank[n % 8][:, :]
                if n >= 8:
                    mine = PROJ1[n - 8][0] in PROJ1_ACT
                    pe.wait_ge((took1_a if mine else took1_v).sem, nth(PROJ1, PROJ1_ACT, n - 8))
                if w == "qk":
                    if n == 0:
                        pe.wait_ge(x_in[0].sem, 32)
                        for k in range(K):
                            if k == K // 2:
                                pe.wait_ge(x_in[1].sem, 32)
                            mm = pe.matmul(b, slot[0][:, k, 0:P], xT[:, k, :], start=(k == 0), stop=(k == K - 1))
                        mm.then_inc(proj1.sem, 1)
                        continue
                    if i >= 4:
                        pe.wait_ge(landed1[1], 16)
                    mm = product(b, [(slot[i // 4][:, k, i % 4 * P:i % 4 * P + P], xT[:, k, :]) for k in range(K)])
                elif w == "rot":
                    pe.wait_ge(first_in.sem, 16)
                    pe.wait_ge(took1_a.sem, nth(PROJ1, PROJ1_ACT, PROJ1.index(("qk", i))))
                    mm = product(b, [(tab(FIRST_AT, "rot"), qk1[:, i, :])])
                elif w == "v":
                    pe.wait_ge(landed1[2], 16)
                    mm = product(b, [(xT[:, k, i * P:(i + 1) * P], slot[2][:, k, :]) for k in range(K)])
                elif w == "u":
                    pe.wait_ge(landed1[3], 16)
                    mm = product(b, [(slot[3][:, k, i * P:(i + 1) * P], xT[:, k, :]) for k in range(K)])
                else:
                    pe.wait_ge(landed1[4], 16)
                    mm = product(b, [(xT[:, k, i * P:(i + 1) * P], slot[4][:, k, :]) for k in range(K)])
                mm.then_inc(proj1.sem, 1)
            pe.wait_ge(took1_a.sem, sum(w in PROJ1_ACT for w, _ in PROJ1))
            pe.wait_ge(took1_v.sem, sum(w not in PROJ1_ACT for w, _ in PROJ1))
            pe.wait_ge(base_in.sem, 16)
            pe.wait_ge(qk1_ready.sem, 8)
            pe.wait_ge(padded1.sem, 2)
            attention(HEADS1, att1, view1)
            pe.wait_ge(att1["head_out"].sem, att1["head_out"].at(H1))
            turn(o1, 4, oT_mm)
            pe.wait_ge(ws_masked.sem, 8)
            pe.wait_ge(g1_ready.sem, T)
            for c in range(4):
                for t in range(T):
                    for g in range(2):
                        mm = pe.matmul(bank[4 + c][HD * g:HD * g + HD, t * P:(t + 1) * P],
                                       g1[:, t, (2 * c + g) * HD:(2 * c + g + 1) * HD], wsT[:, 2 * c + g, :],
                                       start=True, stop=True)
                mm.then_inc(sgu_mm.sem, 1)
            pe.wait_ge(oT_a.sem, 2)
            pe.wait_ge(oT_v.sem, 2)
            pe.wait_ge(sgu_ok.sem, 4)
            pe.wait_ge(landed1[5], 16)
            pe.wait_ge(landed1[0], 16)
            for n in range(2 * T):
                t, half = divmod(n, 2)
                w = slot[5 if half == 0 else 0]
                product(bank[n][:, :], [(mix1[:, k, t * P:(t + 1) * P], w[:, k, :]) for k in range(K)])\
                    .then_inc(wo1_mm.sem, 1)
            pe.wait_ge(h1_sum.sem, 2 * T)
            turn_tiles(xn, h1_ready, r1_mm)
            pe.wait_ge(rt1_in.sem, 48)
            first_product(bank[0][0:NR1, :], [(router1_w[:, k, :], xT[:, k, :]) for k in range(K)], r1_a, r1_v)\
                .then_inc(lgT1_mm.sem, 1)
            pe.wait_ge(r1_a.sem, K // 2)
            pe.wait_ge(r1_v.sem, K // 2)
            pe.wait_ge(lgT1_ok.sem, 1)
            for t in range(T):
                mm = pe.transpose(bank[1][:, t * NR1:(t + 1) * NR1], lgT[0:NR1, t * P:(t + 1) * P], ident[0:NR1, 0:NR1])
            mm.then_inc(lg1_mm.sem, 1)
            pe.wait_ge(mask1.sem, G1)
            places(NE1, cum1_mm)

            def pair1(it, e, q, slots, landed, more, scattering):
                s_gu, s_dn = slots
                X = ex1
                pe.wait_ge(X["xs"].sem, it + 1)
                if scattering:
                    pe.wait_ge(X["selgT_ok"].sem, it)
                for s in s_gu:
                    landed(s)
                columns(bank[2], [[(xs[:, k, C * j:C * j + C], slot[s_gu[j]][:, k, :]) for k in range(K)]
                                  for j in range(2)]).then_inc(X["gu"].sem, 1)
                if more:
                    gather1(it + 1)
                if scattering:
                    scatter1(it - 1)
                pe.wait_ge(X["hid"].sem, it + 1)
                gates = split(gate[:, bass.ds(e * T, 2 * T)], j=2)
                product(bank[2][:, F1:F1 + 2], [(sels[q][:, t, :], gates[:, :, t]) for t in range(T)])
                turn_hidden(X, it, 2)
                if more:
                    turn_tokens(it + 1)
                for t in range(T):
                    mm = pe.transpose(bank[3][:, t * P:(t + 1) * P], sels[q][:, t, :], ident)
                mm.then_inc(X["selgT"].sem, 1)
                landed(s_dn)
                pe.wait_ge(X["hT_ok"].sem, it + 1)
                if scattering:
                    pe.wait_ge(X["added"].sem, it * 8)
                for half in range(2):
                    columns(bank[4 + half], [[(hidT[:, c * P + C * j:c * P + C * j + C],
                                               ring[:, s_dn * SLOT_COLS + (2 * j + c) * D + 512 * half:][:, 0:512])
                                              for c in range(2)] for j in range(2)]).then_inc(X["dn"].sem, 1)

            def scatter1(it):
                X = ex1
                pe.wait_ge(X["selgT_ok"].sem, it + 1)
                for g in range(2 * T):
                    half, t = divmod(g, T)
                    pe.wait_ge(ys_parts.sem, it * 6 + 3 * half + 3)
                    if g == 3:
                        pe.wait_ge(X["ys"].sem, it * 2 + 2)
                    if g >= 4:
                        pe.wait_ge(X["added"].sem, it * 8 + (g - 3))
                    cols = slice(half * 512, half * 512 + 512)
                    product(bank[SCATTER1[g % 4]][:, :], [(selT_b[:, t * P:(t + 1) * P], part[:, cols])
                                                          for part in y_part]).then_inc(X["scat"].sem, 1)

            def gather1(it):
                pe.wait_ge(sel_ok.sem, it + 1)
                for half in range(2):
                    cols = slice(half * 512, half * 512 + 512)
                    product(bank[half][:, :], [(sel_b[:, t, :], part[:, t, cols])
                                               for t in range(T) for part in x_part]).then_inc(ex1["gath"].sem, 1)

            def turn_tokens(it):
                for half in range(2):
                    pe.wait_ge(xg_ready.sem, it * 2 + 2)
                    for c in range(4):
                        k = 4 * half + c
                        mm = pe.transpose(bank[half][:, c * P:(c + 1) * P], xg[:, k * P:(k + 1) * P], ident)
                    mm.then_inc(turned_x.sem, 1)

            def four_experts(run, e4, first=False, last=False):
                def landed(s):
                    pe.wait_ge(landed1[s], (run + (BEFORE1[s] + 1)) * 16)

                for q in range(2):
                    gu0, gu1, dn = (SET1[3 * q + i][0] for i in range(3))
                    pair1(run * 2 + q, e4 * 4 + 2 * q, q, ((gu0, gu1), dn), landed, not (last and q),
                          not first or q == 1)

            def round1(run0):
                gather1(run0 * 2)
                turn_tokens(run0 * 2)
                four_experts(run0, 0, first=True)
                with pe.Fori(1, RUNS1 - 1) as e4:
                    four_experts(run0 + e4, e4)
                four_experts(run0 + (RUNS1 - 1), RUNS1 - 1, last=True)
                scatter1(run0 * 2 + (2 * RUNS1 - 1))

            pe.wait_ge(x_rounded.sem, 2 * T)
            pe.wait_ge(x_parts.sem, 2 * T)
            round1(0)
            pe.wait_ge(places1.sem, 1)
            n_rounds = pe.value_load(rounds_i[0:1, 0:1], min_val=1, max_val=S // C)
            with pe.If(n_rounds > 1):
                with pe.Fori(1, n_rounds) as r:
                    round1(r * RUNS1)

            def rows(w, i):
                return slice(HD, MLA_D) if w in ("kr", "krrot", "uqrot") else slice(0, {"uq": MLA_D}.get(w, P))

            with pe.Fori(0, LAYERS) as l:
                turn_tiles(xn, nrm["x"], nrm["mm"], l)
                pe.wait_ge(second_in.sem, second_in.at(16, l))
                for n, (w, i) in enumerate(PROJ2):
                    b = bank[n % 8]
                    if n >= 8:
                        mine = PROJ2[n - 8][0] in PROJ2_ACT
                        took = took2_a if mine else took2_v
                        pe.wait_ge(took.sem, took.at(nth(PROJ2, PROJ2_ACT, n - 8), l))
                    s = {"cq": 0, "ckv": 0, "kr": 0, "na": 1, "swa": 2, "va": 3}.get(w)
                    if s is not None:
                        pe.wait_ge(landed2[s], l * (16 * PER_SLOT2) + 16)
                    if w in ("cq", "ckv", "kr", "na", "swa"):
                        c0 = {"ckv": 2 * P, "kr": 3 * P}.get(w, i * P)
                        c1 = c0 + (MLA_ROPE if w == "kr" else P)
                        pairs = [(slot[s][:, k, c0:c1], xT[:, k, :]) for k in range(K)]
                        if n < 8:
                            took = nrm["v" if n % 2 else "a"]
                            pe.wait_ge(took.sem, took.at(n // 2 + 1, l))
                        mm = (product(b[rows(w, i), :], pairs) if n else
                              first_product(b[:, :], pairs, nrm["a"], nrm["v"], l))
                    elif w == "va":
                        mm = product(b[:, 0:384], [(xT[:, k, i * P:(i + 1) * P], slot[3][:, k, 0:384])
                                                   for k in range(K)])
                    elif w == "ssq":
                        latent = PROJ2.index(("ckv", 0) if i else ("cq", 1))
                        pe.wait_ge(took2_a.sem, took2_a.at(nth(PROJ2, PROJ2_ACT, latent), l))
                        mm = product(b[:, :], [(ones, sq[:, c, :]) for c in ((2,) if i else (0, 1))])
                    elif w == "krrot":
                        pe.wait_ge(took2_a.sem, took2_a.at(nth(PROJ2, PROJ2_ACT, PROJ2.index(("kr", 0))), l))
                        pe.nop(nofuse=True)
                        mm = product(b[HD:MLA_D, :], [(tab(SECOND_AT, "rot_mla")[HD:MLA_D, :], kr_raw[HD:MLA_D, :])])
                    elif w == "uq":
                        pe.wait_ge(ukv_in.sem, ukv_in.at(32, l))
                        pe.wait_ge(lat_ready.sem, lat_ready.at(2, l))
                        mm = product(b[0:MLA_D, :], [(wuq[:, c, i * MLA_D:(i + 1) * MLA_D], cq[:, c, :])
                                                     for c in range(2)])
                    elif w == "uqrot":
                        pe.wait_ge(took2_a.sem, took2_a.at(nth(PROJ2, PROJ2_ACT, PROJ2.index(("uq", i))), l))
                        pe.nop(nofuse=True)
                        mm = product(b[HD:MLA_D, :], [(tab(SECOND_AT, "rot_mla")[0:MLA_D, :], qk2[0:MLA_D, 8 + i, :])])
                    elif w == "uk":
                        pe.wait_ge(lat_ready.sem, lat_ready.at(3, l))
                        mm = product(b[:, :], [(wukv[:, i * P:(i + 1) * P], cq[:, 2, :])])
                    elif w == "uv":
                        mm = product(b[:, 0:384], [(cq[:, 2, i * P:(i + 1) * P], wukv[:, 384:768])])
                    else:
                        pe.wait_ge(took2_a.sem, took2_a.at(nth(PROJ2, PROJ2_ACT, PROJ2.index(("swa", i))), l))
                        mm = product(b[:, :], [(tab(SECOND_AT, "rot"), qk2[:, 4 + i, :])])
                    mm.then_inc(proj2.sem, 1)
                pe.wait_ge(took2_a.sem, took2_a.at(took2_a.per, l))
                pe.wait_ge(took2_v.sem, took2_v.at(took2_v.per, l))
                pe.wait_ge(rope2.sem, rope2.at(rope2.per, l))
                pe.wait_ge(keys_set.sem, keys_set.at(MLA_H + 3, l))
                attention(HEADS2, att2, view2, l)
                turn_tiles(o2, gnm["x"], gnm["mm"], l)
                pe.wait_ge(landed2[4], l * (16 * PER_SLOT2) + 16)
                pe.wait_ge(landed2[5], l * (16 * PER_SLOT2) + 16)
                for n in range(2 * T):
                    t, half = divmod(n, 2)
                    pairs = [(oT2[:, k, t * P:(t + 1) * P], slot[4 + half][:, k, :]) for k in range(K)]
                    (product(bank[n][:, :], pairs) if n else
                     first_product(bank[n][:, :], pairs, gnm["a"], gnm["v"], l)).then_inc(wo2_mm.sem, 1)
                pe.wait_ge(h2_sum.sem, h2_sum.at(2 * T, l))
                turn_tiles(xn, fnm["x"], fnm["mm"], l)
                pe.wait_ge(rt2_in.sem, rt2_in.at(16, l))
                first_product(bank[0][0:NE2, :], [(router2_w[:, k, :], xT[:, k, :]) for k in range(K)],
                              fnm["a"], fnm["v"], l).then_inc(lgT2_mm.sem, 1)
                pe.wait_ge(fnm["a"].sem, fnm["a"].at(K // 2, l))
                pe.wait_ge(fnm["v"].sem, fnm["v"].at(K // 2, l))
                pe.wait_ge(lgT2_ok.sem, lgT2_ok.at(1, l))
                pe.nop(nofuse=True)
                for t in range(T):
                    mm = pe.transpose(bank[1][:, t * NE2:(t + 1) * NE2], lgT[0:NE2, t * P:(t + 1) * P],
                                      ident[0:NE2, 0:NE2])
                mm.then_inc(lg2_mm.sem, 1)
                pe.wait_ge(aff_ready.sem, aff_ready.at(1, l))
                for t in range(T):
                    mm = pe.transpose(bank[1][0:NE2, t * P:(t + 1) * P], pick[2][:, t * NE2:(t + 1) * NE2], ident)
                mm.then_inc(affT_mm.sem, 1)
                pe.wait_ge(maskT_ready.sem, maskT_ready.at(1, l))
                pe.nop(nofuse=True)
                for t in range(T):
                    mm = pe.transpose(bank[2][:, t * NE2:(t + 1) * NE2], maskT[0:NE2, t * P:(t + 1) * P],
                                      ident[0:NE2, 0:NE2])
                mm.then_inc(mask_mm.sem, 1)
                pe.wait_ge(mask2.sem, mask2.at(1, l))
                places(NE2, cum2_mm)

                def pair2(pair, last):
                    X = ex2
                    it = l * (NE2 // 2) + pair
                    pe.wait_ge(X["xs"].sem, X["xs"].at(it + 1))
                    for j in range(2):
                        def landed(s, j=j):
                            pe.wait_ge(landed2[s], (l * PER_SLOT2 + pair * 2 + (j + 2)) * 16)

                        for which in range(2):
                            landed(2 * which)
                            landed(2 * which + 1)
                            columns(bank[2 + which], [[(xs[:, k, C * j:C * j + C], slot[2 * which + half][:, k, :])
                                                       for k in range(K)] for half in range(2)])\
                                .then_inc(X["gu"].sem, 1)
                        if j and not last:
                            gather(X, it + 1)
                        turn_hidden(X, it * 2 + j, 4)
                        if j:
                            turn_gates(X, it)
                        landed(4)
                        landed(5)
                        pe.wait_ge(X["hT_ok"].sem, X["hT_ok"].at(it * 2 + (j + 1)))
                        columns(bank[4 + j], [[(hidT[:, c * P + C * fh:c * P + C * fh + C],
                                                slot[4 + half][:, 4 * fh + c, :])
                                               for fh in range(2) for c in range(4)] for half in range(2)])\
                            .then_inc(X["dn"].sem, 1)
                    scatter(X, it)

                gather(ex2, l * (NE2 // 2))
                with pe.Fori(0, NE2 // 2 - 1) as pair:
                    pair2(pair, False)
                pair2(NE2 // 2 - 1, True)

        @block.scalar
        def _(act):
            def take_chunks(sg, dst, chunks, gain=None, l=0, b0=0):
                for n, c in enumerate(range(0, chunks, 2)):
                    act.wait_ge(sg["mm"].sem, sg["mm"].at(c + 1, l))
                    act.activation(dst[:, c, :], bank[b0 + c][:, :], ACT.Copy,
                                   scale=1.0 if gain is None else gain[:, c:c + 1]).then_inc(sg["a"].sem, 1)

            def group_square(g, t, l):
                c0, c1 = GROUPS2[g]
                return act.activation(junk[:, t, c0:c1], o2[:, t, c0:c1], ACT.Square,
                                      accum_out=ss[:, g * T + t:g * T + t + 1])

            def attention(heads, sg, l=0, squares_at={}):
                units = [(n, kind, i, t) for n, (kind, i) in enumerate(heads) for t in range(T)]
                for u in range(len(units) + 1):
                    if heads is HEADS1 and u == GATE_STD:
                        act.wait_ge(g1_var.sem, T)
                        act.activation(std[:, 0:T], mv[:, 1:8:2], ACT.Sqrt, bias=eps_ln).then_inc(g1_std.sem, 1)
                    if u in squares_at:
                        g, t, n = squares_at[u]
                        act.wait_ge(sg["head_out"].sem, sg["head_out"].at(n, l))
                        group_square(g, t, l)
                    if u < len(units):
                        n, kind, i, t = units[u]
                        w = (end_key(kind, t) - first_key(kind, t)) * P
                        p = prob[u % 2][:, 0:w]
                        act.wait_ge(sg["shifted"].sem, sg["shifted"].at(u + 1, l))
                        if kind == "mla":
                            if u >= 2:
                                act.wait_ge(sg["turned"].sem, sg["turned"].at(u - 1, l))
                            act.activation(p, bank[u % 2][:, 0:w], ACT.Exp, bias=negmax[:, u:u + 1],
                                           accum_out=total[:, u:u + 1]).then_inc(sg["prob"].sem, 1)
                        else:
                            act.activation(p, p, ACT.Exp, bias=negmax[:, u:u + 1], scale=-1.0,
                                           accum_out=total[:, u:u + 1]).then_inc(sg["prob"].sem, 1)
                        if kind == "swa" and t == T - 1:
                            act.activation(esink, negmax[:, u - T + 1:u + 1], ACT.Exp, bias=sink[:, i:i + 1])\
                               .then_inc(sunk.sem, 1)
                    v = u - 1
                    if v >= 0 and v % 2:
                        n, kind, i, t = units[v]
                        w = (end_key(kind, t) - first_key(kind, t)) * P
                        act.wait_ge(sg["turned"].sem, sg["turned"].at(v + 1, l))
                        if v >= 2:
                            act.wait_ge(sg["pv"].sem, sg["pv"].at(v - 1, l))
                        act.activation(probT[1][:, 0:w], bank[3][:, 0:w], ACT.Copy).then_inc(sg["probT_a"].sem, 1)

            def hidden(X, n, per, w):
                act.wait_ge(X["gu"].sem, X["gu"].at(n * per + 1))
                act.activation(silu[:, 0:w], bank[2][:, 0:w], ACT.Silu).then_inc(X["silu"].sem, 1)
                act.wait_ge(X["hT"].sem, X["hT"].at(n + 1))
                act.activation(hidT[:, 0:w], bank[2][:, 0:w], ACT.Copy).then_inc(X["hT_ok"].sem, 1)

            def gates(X, it):
                act.wait_ge(X["selgT"].sem, X["selgT"].at(it + 1))
                act.activation(selgT, bank[3][:, :], ACT.Copy).then_inc(X["selgT_ok"].sem, 1)

            def tokens1(it, half):
                act.wait_ge(ex1["gath"].sem, it * 2 + (half + 1))
                act.activation(xg[:, half * 512:(half + 1) * 512], bank[half][:, :], ACT.Copy).then_inc(xg_ready.sem, 1)

            def turned1(it):
                for half in range(2):
                    act.wait_ge(turned_x.sem, it * 2 + (half + 1))
                    ins = act.activation(xs[:, 4 * half:4 * half + 4, :], split(bank[half][:, :], k=4), ACT.Copy)
                ins.then_inc(ex1["xs"].sem, 1)

            def pair1(it, more):
                act.wait_ge(ex1["gu"].sem, it + 1)
                act.activation(silu[:, 0:F1], bank[2][:, 0:F1], ACT.Silu).then_inc(ex1["silu"].sem, 1)
                if more:
                    tokens1(it + 1, 0)
                    tokens1(it + 1, 1)
                act.wait_ge(ex1["hT"].sem, it + 1)
                act.activation(hidT[:, 0:F1], bank[2][:, 0:F1], ACT.Copy).then_inc(ex1["hT_ok"].sem, 1)
                if more:
                    turned1(it + 1)
                act.wait_ge(ex1["selgT"].sem, it + 1)
                for j in range(2):
                    own = slice(C * j, C * j + C)
                    act.activation(place_gate[own, :], bank[2][own, F1 + j:F1 + j + 1], ACT.Copy)
                act.activation(selT_b, bank[3][:, :], ACT.Copy).then_inc(ex1["selgT_ok"].sem, 1)
                act.wait_ge(ex1["selgT_ok"].sem, it + 1)
                for half in range(2):
                    act.wait_ge(ex1["dn"].sem, it * 2 + (half + 1))
                    cols = slice(half * 512, half * 512 + 512)
                    act.activation(ys[:, cols], bank[4 + half][:, :], ACT.Copy, scale=place_gate)
                    act.activation(y_part[0][:, cols], bank[4 + half][:, :], ACT.Copy, scale=place_gate)\
                       .then_inc(ex1["ys"].sem, 1)

            def round1(it0):
                tokens1(it0, 0)
                tokens1(it0, 1)
                turned1(it0)
                with act.Fori(0, NE1 // 2 - 1) as pair:
                    pair1(it0 + pair, True)
                pair1(it0 + (NE1 // 2 - 1), False)

            def pair2(it):
                for j in range(2):
                    hidden(ex2, it * 2 + j, 2, 512)
                    if j:
                        gates(ex2, it)
                    act.wait_ge(ex2["dn"].sem, ex2["dn"].at(it * 2 + (j + 1)))
                    for half in range(2):
                        ins = act.activation(ys[C * j:C * j + C, half * 512:(half + 1) * 512],
                                             bank[4 + j][C * half:C * half + C, :], ACT.Copy)
                    ins.then_inc(ex2["ys"].sem, 1)

            def squares(l, came, at):
                for t in range(T):
                    act.wait_ge(came.sem, at(t))
                    ins = act.activation(xn[:, t, :], h[:, t, :], ACT.Square, accum_out=ss[:, t:t + 1])
                ins.then_inc(nrm["ss"].sem, 1)
                act.wait_ge(nrm["ss"].sem, nrm["ss"].at(1, l))
                act.activation(std[:, 0:T], ss[:, 0:T], ACT.Sqrt, bias=eps_rms, scale=1.0 / D)\
                   .then_inc(nrm["std"].sem, 1)

            act.wait_ge(sin_args.sem, 2)
            act.activation(sin1, sin_arg, ACT.Sin).then_inc(rope1.sem, 1)
            act.activation(cos1, cos_arg, ACT.Sin).then_inc(rope1.sem, 1)
            for n, (w, i) in enumerate(PROJ1):
                if w in PROJ1_ACT:
                    act.wait_ge(proj1.sem, n + 1)
                    b = bank[n % 8][:, :]
                    if w == "qk":
                        act.activation(qk1[:, i, :], b, ACT.Copy, scale=-HD ** -0.5 if i < 4 else 1.0)\
                           .then_inc(took1_a.sem, 1)
                    else:
                        act.activation((u1 if w == "u" else g1)[:, i, :], b, ACT.Gelu).then_inc(took1_a.sem, 1)
            attention(HEADS1, att1)
            take_chunks({"mm": oT_mm, "a": oT_a}, mix1, 4)
            for t in range(T):
                act.wait_ge(h1_var.sem, t + 1)
                act.activation(std[:, t:t + 1], mv[:, 2 * t + 1:2 * t + 2], ACT.Sqrt, bias=eps_ln)\
                   .then_inc(h1_std.sem, 1)
            take_chunks({"mm": r1_mm, "a": r1_a}, xT, K)
            act.wait_ge(lg1_mm.sem, 1)
            for t in range(T):
                act.activation(x_part[0][:, t, :], xn[:, t, :], ACT.Copy).then_inc(x_rounded.sem, 1)
            for i, n in enumerate((T * G1, T)):
                act.wait_ge(ex1_in.sem, i + 1)
                act.activation(pick[1][:, 0:n], pick[0][:, 0:n], ACT.Exp).then_inc(ex1_out.sem, 1)
                for t in range(2 * i, 2 * i + 2):
                    act.wait_ge(x_parts.sem, t + 1)
                    act.activation(x_part[1][:, t, :], xn[:, t, :], ACT.Copy).then_inc(x_rounded.sem, 1)
            round1(0)
            act.wait_ge(places1.sem, 1)
            n_rounds = act.value_load(rounds_i[0:1, 0:1], min_val=1, max_val=S // C)
            with act.If(n_rounds > 1):
                with act.Fori(1, n_rounds) as r:
                    round1(r * (NE1 // 2))
            act.wait_ge(h2_var.sem, h2_var.at(T))
            act.activation(std[:, 0:T], mv[:, 1:8:2], ACT.Sqrt, bias=eps_ln).then_inc(h2_std.sem, 1)

            squares(0, h_tiles, lambda t: t + 1)

            with act.Fori(0, LAYERS) as l:
                act.wait_ge(cols_ready.sem, cols_ready.at(1, l))
                take_chunks(nrm, xT, K, gains[:, 0, :], l)
                for n, (w, i) in enumerate(PROJ2):
                    if w not in PROJ2_ACT:
                        continue
                    b = bank[n % 8]
                    act.wait_ge(proj2.sem, proj2.at(n + 1, l))
                    if w in ("cq", "ckv"):
                        c = 2 if w == "ckv" else i
                        act.activation(cq[:, c, :], b[:, :], ACT.Copy)
                        ins = act.activation(sq[:, c, :], b[:, :], ACT.Square)
                    elif w == "kr":
                        ins = act.activation(kr_raw[HD:MLA_D, :], b[HD:MLA_D, :], ACT.Copy)
                    elif w == "na" and i < 2:
                        ins = act.activation(qk2[:, i, :], b[:, :], ACT.Copy, scale=-HD ** -0.5)
                    elif w == "na":
                        act.activation(qk2[0:HD, i, :], b[0:HD, :], ACT.Copy)
                        ins = act.activation(cq[HD:P, i - 2, :], b[HD:P, :], ACT.Copy)
                    elif w == "swa":
                        ins = act.activation(qk2[:, 4 + i, :], b[:, :], ACT.Copy, scale=-HD ** -0.5 if i < 3 else 1.0)
                    elif w == "ssq":
                        ins = act.activation(rs[:, i, :], b[:, :], ACT.Sqrt, bias=eps_rms,
                                             scale=1.0 / (P if i else 2 * P))
                    elif w == "uq":
                        ins = act.activation(qk2[0:MLA_D, 8 + i, :], b[0:MLA_D, :], ACT.Copy, scale=MLA_D ** -0.5)
                    else:
                        ins = act.activation(vm[:, i, :], b[:, 0:384], ACT.Copy)
                    ins.then_inc(took2_a.sem, 1)
                early = {(MLA_H + SWA_H) * T + 2 + t: (1, t, MLA_H) for t in range(T)}
                early.update({(MLA_H + SWA_H + 1) * T + 2 + t: (2, t, MLA_H + SWA_H) for t in range(T)})
                attention(HEADS2, att2, l, early)
                act.wait_ge(att2["head_out"].sem, att2["head_out"].at(len(HEADS2), l))
                for t in range(T):
                    ins = group_square(0, t, l)
                ins.then_inc(gnm["ss"].sem, 1)
                act.wait_ge(gnm["ss"].sem, gnm["ss"].at(1, l))
                act.activation(std[:, 0:T], ss[:, 0:T], ACT.Sqrt, bias=eps_rms, scale=1.0 / 256)
                act.activation(std[:, T:3 * T], ss[:, T:3 * T], ACT.Sqrt, bias=eps_rms, scale=1.0 / 384)\
                   .then_inc(gnm["std"].sem, 1)
                take_chunks(gnm, oT2, K, gains[:, 1, :], l)
                for t in range(T):
                    act.wait_ge(h2_sum.sem, h2_sum.at(2 * t + 2, l))
                    act.activation(junk[:, t, :], h[:, t, :], ACT.Square, accum_out=ss[:, t:t + 1])\
                       .then_inc(fnm_ss.sem, 1)
                    act.wait_ge(fnm_ss.sem, fnm_ss.at(t + 1, l))
                    act.activation(std[:, t:t + 1], ss[:, t:t + 1], ACT.Sqrt, bias=eps_rms, scale=1.0 / D)\
                       .then_inc(fnm_std.sem, 1)
                take_chunks(fnm, xT, K, gains[:, 2, :], l)
                act.wait_ge(ex2_in.sem, ex2_in.at(1, l))
                act.activation(pick[1][:, 0:T * NE2], pick[0][:, 0:T * NE2], ACT.Exp).then_inc(ex2_out.sem, 1)
                with act.Fori(0, NE2 // 2) as pair:
                    pair2(l * (NE2 // 2) + pair)
                squares(l + 1, ex2["added"], lambda t: (l + 1) * (NE2 // 2 * 8) - 2 * (T - 1 - t))

        @block.vector
        def _(dve):
            v = dve

            def take_chunks(sg, dst, chunks, gain=None, l=0, b0=0):
                for c in range(1, chunks, 2):
                    v.wait_ge(sg["mm"].sem, sg["mm"].at(c + 1, l))
                    if gain is None:
                        ins = v.tensor_copy(dst[:, c, :], bank[b0 + c][:, :])
                    else:
                        ins = v.tensor_scalar(dst[:, c, :], bank[b0 + c][:, :], gain[:, c:c + 1], None, ALU.mult)
                    ins.then_inc(sg["v"].sem, 1)

            def attention(heads, sg, table, place_of, chain, l=0, beside=lambda u: None):
                units = [(n, kind, i, t) for n, (kind, i) in enumerate(heads) for t in range(T)]
                for u in range(len(units) + 2):
                    beside(u)
                    if u < len(units):
                        n, kind, i, t = units[u]
                        k0, k1 = first_key(kind, t), end_key(kind, t)
                        w = (k1 - k0) * P
                        if kind == "na" and t == 0:
                            v.wait_ge(bias_in[i % 2].sem, bias_in[i % 2].at(32 * (i // 2 + 1), l))
                            b = split(bt[i % 2], j=BT_ROWS)
                            v.scalar_tensor_tensor(out=b, in0=b, scalar=-1.0,
                                                   in1=spread(tab(SECOND_AT, "window"), 1, BT_ROWS),
                                                   op0=ALU.mult, op1=ALU.add).then_inc(bias_ready.sem, 1)
                            v.wait_ge(bias_ready.sem, bias_ready.at(i + 1, l))
                        v.wait_ge(sg["score"].sem, sg["score"].at(u + 1, l))
                        if kind != "mla":
                            v.nop(nofuse=True)
                        s = bank[u % 2][:, 0:w]
                        if kind == "mla":
                            v.tensor_reduce(negmax[:, u:u + 1], s, AX_X, ALU.max, negate=True)\
                             .then_inc(sg["shifted"].sem, 1)
                        else:
                            if u >= 2:
                                v.wait_ge(sg["turned"].sem, sg["turned"].at(u - 1, l))
                                v.nop(nofuse=True)
                            rows = (lambda x: split(x, r=GH)) if kind == "na" else (lambda x: x)
                            v.tensor_tensor_reduce(out=rows(prob[u % 2][:, 0:w]), in0=rows(s),
                                                   in1=table(kind, i, t), scale=1.0,
                                                   scalar=nsink[:, i:i + 1] if kind == "swa" else HUGE,
                                                   op0=ALU.add, op1=ALU.min, accum_out=negmax[:, u:u + 1])\
                             .then_inc(sg["shifted"].sem, 1)
                    w1 = u - 1
                    if 0 <= w1 < len(units) and w1 % 2 == 0:
                        n, kind, i, t = units[w1]
                        w = (end_key(kind, t) - first_key(kind, t)) * P
                        v.wait_ge(sg["turned"].sem, sg["turned"].at(w1 + 1, l))
                        if w1 >= 2:
                            v.wait_ge(sg["pv"].sem, sg["pv"].at(w1 - 1, l))
                        v.tensor_copy(probT[0][:, 0:w], bank[2][:, 0:w]).then_inc(sg["probT_v"].sem, 1)
                    if u >= 2 and (u - 2) % T == T - 1:
                        n, kind, i, t = units[u - 2]
                        v.wait_ge(sg["pv"].sem, sg["pv"].at(u - 1, l))
                        sums = total[:, n * T:(n + 1) * T]
                        if kind == "swa":
                            v.wait_ge(sunk.sem, sunk.at(i + 1, l))
                            v.tensor_tensor(sums, sums, esink, ALU.add).then_inc(chain.sem, 1)
                            v.wait_ge(chain.sem, chain.next())
                        v.reciprocal(rtotal, sums).then_inc(chain.sem, 1)
                        v.wait_ge(chain.sem, chain.next())
                        own = HD * second_of_two(kind, i)
                        v.tensor_tensor(place_of(kind, i), split(bank[4 + n % 2][:, :], t=T)[:, :, own:own + HD],
                                        spread(rtotal, 2, HD), ALU.mult).then_inc(sg["head_out"].sem, 1)

            def moments(t, width, src, chain):
                m = width // 512
                for i in range(m):
                    ins = v.bn_stats(bn[:, 6 * i:6 * i + 6], src[:, t, 512 * i:512 * (i + 1)])
                ins.then_inc(chain.sem, 1)
                v.wait_ge(chain.sem, chain.next())
                return v.bn_aggr(mv[:, 2 * t:2 * t + 2], bn[:, 0:6 * m])

            def layer_norm(src, dst, g, b, t, chain):
                v.scalar_tensor_tensor(out=src, in0=src, scalar=mv[:, 2 * t:2 * t + 1], in1=g, op0=ALU.subtract,
                                       op1=ALU.mult).then_inc(chain.sem, 1)
                v.wait_ge(chain.sem, chain.next())
                return v.scalar_tensor_tensor(out=dst, in0=src, scalar=rstd[:, t:t + 1], in1=b, op0=ALU.mult,
                                              op1=ALU.add)

            def first_max(values, n, groups, m, eq, chain):
                v.tensor_reduce(m, values, AX_X, ALU.max).then_inc(chain.sem, 1)
                v.wait_ge(chain.sem, chain.next())
                v.tensor_tensor(eq, values, spread(m, 2, n), ALU.is_equal).then_inc(chain.sem, 1)
                v.wait_ge(chain.sem, chain.next())
                v.tensor_tensor(eq, eq, spread(rank[:, 0:n], 1, groups), ALU.mult).then_inc(chain.sem, 1)
                v.wait_ge(chain.sem, chain.next())
                v.tensor_reduce(col[0], eq, AX_X, ALU.max).then_inc(chain.sem, 1)
                v.wait_ge(chain.sem, chain.next())
                v.tensor_tensor(eq, eq, spread(col[0], 2, n), ALU.is_equal).then_inc(chain.sem, 1)
                v.wait_ge(chain.sem, chain.next())

            def set_places(n, mm, l=0):
                v.wait_ge(mm.sem, mm.at(1, l))
                return v.tensor_tensor(place[:, 0:n * T].rearrange("p (e t) -> p t e", t=T), mask_of(n),
                                       split(bank[3][:, 0:n * T], t=T), ALU.mult)

            def by_place(table, e):
                return spread(split(table[:, bass.ds(e * T, 2 * T)], j=2).rearrange("p j t -> p t j"), 3, C)

            def pairs_of(x):
                return x.rearrange("p t (j c) -> p t j c", j=2)

            def scattered1(it):
                for g in range(2 * T):
                    half, t = divmod(g, T)
                    v.wait_ge(ex1["scat"].sem, it * 8 + (g + 1))
                    hs = h[:, t, half * 512:(half + 1) * 512]
                    v.tensor_tensor(hs, hs, bank[SCATTER1[g % 4]][:, :], ALU.add).then_inc(ex1["added"].sem, 1)

            def choose1(it, e, one_hot):
                choose(ex1, it, e, one_hot)
                v.wait_ge(ex1["sel"].sem, it + 1)
                v.tensor_copy(sel_b, one_hot).then_inc(sel_ok.sem, 1)

            def choose(X, it, e, one_hot=sel):
                v.tensor_tensor(pairs_of(one_hot), spread(spread(iota, 1, 2), 1, T), by_place(place, e), ALU.is_equal)\
                 .then_inc(X["sel"].sem, 1)

            def take_tokens(X, it, gain):
                v.wait_ge(X["gath"].sem, X["gath"].at(it + 1))
                for half in range(2):
                    ins = v.tensor_tensor(xs[:, 4 * half:4 * half + 4, :], split(bank[half][:, :], k=4),
                                          spread(gain[:, 4 * half:4 * half + 4], 2, P), ALU.mult)
                ins.then_inc(X["xs"].sem, 1)

            def first_pair(X, it, gain):
                choose(X, it, 0)
                take_tokens(X, it, gain)

            def expert_pair(X, it, e, gain, last):
                v.wait_ge(X["sel"].sem, X["sel"].at(it + 1))
                v.tensor_tensor(pairs_of(selg), pairs_of(sel), by_place(gate, e), ALU.mult).then_inc(X["selg"].sem, 1)
                if not last:
                    v.wait_ge(X["selg"].sem, X["selg"].at(it + 1))
                    choose(X, it + 1, e + 2)
                for n in (it * 2, it * 2 + 1):
                    v.wait_ge(X["gu"].sem, (n + 1) * 2)
                    v.wait_ge(X["silu"].sem, n + 1)
                    v.tensor_tensor(hid, silu, bank[3][:, :], ALU.mult).then_inc(X["hid"].sem, 1)
                if not last:
                    take_tokens(X, it + 1, gain)
                for g in range(2 * T):
                    t, half = divmod(g, 2)
                    v.wait_ge(X["scat"].sem, X["scat"].at(it * 8 + g + 1))
                    hs = h[:, t, half * 512:(half + 1) * 512]
                    v.tensor_tensor(hs, hs, bank[6 + g % 2][:, :], ALU.add).then_inc(X["added"].sem, 1)

            def expert_round(X, it0, pairs, gain):
                first_pair(X, it0, gain)
                with v.Fori(0, pairs - 1) as pair:
                    expert_pair(X, it0 + pair, pair * 2, gain, False)
                expert_pair(X, it0 + (pairs - 1), 2 * (pairs - 1), gain, True)

            def pair1(it, e, q, last, scattering):
                X = ex1
                if not last:
                    v.wait_ge(X["gath"].sem, it * 2 + 2)
                    choose1(it + 1, e + 2, sels[1 - q])
                v.wait_ge(X["silu"].sem, it + 1)
                v.wait_ge(X["gu"].sem, it + 1)
                v.tensor_tensor(hid[:, 0:F1], silu[:, 0:F1], bank[2][:, F1:2 * F1], ALU.mult).then_inc(X["hid"].sem, 1)
                if scattering:
                    scattered1(it - 1)
                for half in range(2):
                    cols = slice(half * 512, half * 512 + 512)
                    v.wait_ge(X["ys"].sem, it * 2 + (half + 1))
                    v.tensor_tensor(ys[:, cols], ys[:, cols], y_part[0][:, cols], ALU.subtract)\
                     .then_inc(ys_parts.sem, 1)
                    v.wait_ge(ys_parts.sem, it * 6 + (3 * half + 1))
                    v.tensor_copy(y_part[1][:, cols], ys[:, cols]).then_inc(ys_parts.sem, 1)
                    v.wait_ge(ys_parts.sem, it * 6 + (3 * half + 2))
                    v.tensor_tensor(y_part[2][:, cols], ys[:, cols], y_part[1][:, cols], ALU.subtract)\
                     .then_inc(ys_parts.sem, 1)

            def four_experts(run, e4, first=False, last=False):
                for q in range(2):
                    pair1(run * 2 + q, e4 * 4 + 2 * q, q, last and q == 1, not first or q == 1)

            def round1(run0):
                choose1(run0 * 2, 0, sels[0])
                four_experts(run0, 0, first=True)
                with v.Fori(1, RUNS1 - 1) as e4:
                    four_experts(run0 + e4, e4)
                four_experts(run0 + (RUNS1 - 1), RUNS1 - 1, last=True)
                scattered1(run0 * 2 + (2 * RUNS1 - 1))

            c1 = Steps(dve1.sem)
            v.memset(eps_ln, LN_EPS).then_inc(c1.sem, 1)
            v.wait_ge(c1.sem, c1.next())
            v.memset(eps_rms, RMS_EPS).then_inc(c1.sem, 1)
            v.wait_ge(c1.sem, c1.next())
            v.wait_ge(pos_in.sem, 16)
            v.wait_ge(first_in.sem, 16)
            v.tensor_copy(ang, pos_i).then_inc(c1.sem, 1)
            v.wait_ge(c1.sem, c1.next())
            v.tensor_scalar(ang, ang, tab(FIRST_AT, "inv"), None, ALU.mult).then_inc(c1.sem, 1)
            v.wait_ge(c1.sem, c1.next())
            v.tensor_scalar(turns, ang, 1.0 / (2 * np.pi), None, ALU.mult).then_inc(c1.sem, 1)
            v.wait_ge(c1.sem, c1.next())
            v.tensor_copy(turns_i, turns).then_inc(c1.sem, 1)
            v.wait_ge(c1.sem, c1.next())
            v.tensor_copy(turns, turns_i).then_inc(c1.sem, 1)
            v.wait_ge(c1.sem, c1.next())
            for n, part in enumerate(TWO_PI_PARTS):
                v.scalar_tensor_tensor(out=sin_arg, in0=turns, scalar=-part, in1=sin_arg if n else ang,
                                       op0=ALU.mult, op1=ALU.add).then_inc(c1.sem, 1)
                v.wait_ge(c1.sem, c1.next())

            def wrap(x, side):
                v.tensor_scalar(over, x, side * np.pi, -side * 2 * np.pi, ALU.is_gt if side > 0 else ALU.is_lt,
                                ALU.mult).then_inc(c1.sem, 1)
                v.wait_ge(c1.sem, c1.next())
                v.tensor_tensor(x, x, over, ALU.add).then_inc(c1.sem, 1)
                v.wait_ge(c1.sem, c1.next())

            wrap(sin_arg, 1)
            wrap(sin_arg, -1)
            v.tensor_scalar(cos_arg, sin_arg, np.pi / 2, None, ALU.add).then_inc(c1.sem, 1)
            v.wait_ge(c1.sem, c1.next())
            wrap(cos_arg, 1)
            for x in (sin_arg, cos_arg):
                v.tensor_scalar(x, x, PI_BELOW, -PI_BELOW, ALU.min, ALU.max).then_inc(sin_args.sem, 1)

            v.wait_ge(rope1.sem, 2)
            for n, (w, i) in enumerate(PROJ1):
                if w in PROJ1_ACT:
                    continue
                v.wait_ge(proj1.sem, n + 1)
                b = bank[n % 8][:, :]
                if w == "v":
                    v.tensor_copy(v1[:, i, :], b).then_inc(took1_v.sem, 1)
                else:
                    v.tensor_tensor(rot_tmp, b, sin1, ALU.mult).then_inc(took1_v.sem, 1)
                    v.tensor_tensor(qk1[:, i, :], qk1[:, i, :], cos1, ALU.mult).then_inc(c1.sem, 1)
                    v.wait_ge(c1.sem, c1.next())
                    v.wait_ge(took1_v.sem, nth(PROJ1, PROJ1_ACT, n))
                    if i >= 4:
                        v.tensor_tensor(mix1[HD:P, i - 4, :], qk1[HD:P, i, :], rot_tmp[HD:P, :], ALU.add)
                    own = slice(0, HD if i >= 4 else P)
                    v.tensor_tensor(qk1[own, i, :], qk1[own, i, :], rot_tmp[own, :], ALU.add)\
                     .then_inc(qk1_ready.sem, 1)
                    v.wait_ge(qk1_ready.sem, i + 1)
            def gate_step(u):
                if u % 2 == 0 and u // 2 < T:
                    t = u // 2
                    v.wait_ge(took1_a.sem, nth(PROJ1, PROJ1_ACT, PROJ1.index(("gate", t))))
                    moments(t, 512, g1, c1).then_inc(g1_var.sem, 1)
                    v.wait_ge(g1_var.sem, t + 1)
                if u == GATE_STD + 2:
                    v.wait_ge(g1_std.sem, 1)
                    v.reciprocal(rstd[:, 0:T], std[:, 0:T]).then_inc(c1.sem, 1)
                    v.wait_ge(c1.sem, c1.next())
                    v.wait_ge(sgu_in.sem, 32)
                if GATE_STD + 4 <= u < GATE_STD + 4 + 2 * T and u % 2 == 0:
                    t = (u - GATE_STD - 4) // 2
                    layer_norm(g1[:, t, :], g1[:, t, :], sgu_g, sgu_b, t, c1).then_inc(g1_ready.sem, 1)
                    v.wait_ge(g1_ready.sem, t + 1)

            attention(HEADS1, att1, table1, lambda kind, i: o1[:, :, i * HD:(i + 1) * HD], c1, 0, gate_step)
            take_chunks({"mm": oT_mm, "v": oT_v}, mix1, 4)
            v.wait_ge(bsp_in.sem, 128)
            for c in range(4):
                v.wait_ge(sgu_mm.sem, c + 1)
                v.tensor_tensor(split(rot_tmp, t=T), split(bank[4 + c][:, :], t=T), spread(bsp[:, c, :], 1, T),
                                ALU.add).then_inc(c1.sem, 1)
                v.wait_ge(c1.sem, c1.next())
                v.tensor_tensor(mix1[:, 4 + c, :], u1[:, c, :], rot_tmp, ALU.mult).then_inc(sgu_ok.sem, 1)
                v.wait_ge(sgu_ok.sem, c + 1)
            v.wait_ge(h_in.sem, 16)
            for n in range(2 * T):
                t, half = divmod(n, 2)
                hs = h[:, t, half * 512:(half + 1) * 512]
                v.wait_ge(wo1_mm.sem, n + 1)
                v.scalar_tensor_tensor(out=hs, in0=hs, scalar=ALPHA, in1=bank[n][:, :], op0=ALU.mult, op1=ALU.add)\
                 .then_inc(h1_sum.sem, 1)
                if half:
                    v.wait_ge(h1_sum.sem, n + 1)
                    moments(t, D, h, c1).then_inc(h1_var.sem, 1)
                    v.wait_ge(h1_std.sem, t + 1)
                    v.reciprocal(rstd[:, t:t + 1], std[:, t:t + 1]).then_inc(c1.sem, 1)
                    v.wait_ge(c1.sem, c1.next())
                    v.wait_ge(ln1_in.sem, 32)
                    layer_norm(h[:, t, :], xn[:, t, :], ln1g, ln1b, t, c1).then_inc(h1_ready.sem, 1)
                    v.wait_ge(h1_ready.sem, t + 1)
                    v.tensor_scalar(h[:, t, :], xn[:, t, :], ALPHA, None, ALU.mult).then_inc(c1.sem, 1)
                    v.wait_ge(c1.sem, c1.next())
            take_chunks({"mm": r1_mm, "v": r1_v}, xT, K)

            v.wait_ge(lgT1_mm.sem, 1)
            v.tensor_copy(lgT[0:NR1, :], bank[0][0:NR1, :]).then_inc(lgT1_ok.sem, 1)
            v.wait_ge(lg1_mm.sem, 1)
            v.wait_ge(rt1_in.sem, 48)
            v.tensor_tensor(logits, split(bank[1][:, 0:T * NR1], t=T), spread(bias_r, 1, T), ALU.add)\
             .then_inc(c1.sem, 1)
            v.wait_ge(c1.sem, c1.next())
            gl, el = logits[:, :, 0:G1], logits[:, :, G1:G1 + NE1]
            gm, psel, e1, e2, w1, w2 = col[1], col[2], col[3], col[4], col[5], col[6]
            gone = split(pick[2][:, 0:T * G1], t=T)
            first_max(gl, G1, T, gm, gone, c1)
            v.tensor_tensor(split(pick[0][:, 0:T * G1], t=T), gl, spread(gm, 2, G1), ALU.subtract)\
             .then_inc(ex1_in.sem, 1)
            v.wait_ge(ex1_out.sem, 1)
            v.tensor_reduce(psel, split(pick[1][:, 0:T * G1], t=T), AX_X, ALU.add).then_inc(c1.sem, 1)
            v.wait_ge(c1.sem, c1.next())
            v.reciprocal(psel, psel).then_inc(c1.sem, 1)
            v.wait_ge(c1.sem, c1.next())
            by_group = mask1_w.rearrange("p (t g e) -> p t g e", t=T, g=G1)
            v.tensor_tensor(by_group, el.rearrange("p t (g e) -> p t g e", g=G1), spread(gone, 3, E1), ALU.mult)\
             .then_inc(c1.sem, 1)
            v.wait_ge(c1.sem, c1.next())
            es = split(pick[0][:, 16:16 + T * E1], t=T)
            v.tensor_reduce(es, by_group.rearrange("p t g e -> p t e g"), AX_X, ALU.add).then_inc(c1.sem, 1)
            v.wait_ge(c1.sem, c1.next())
            one = [split(pick[2][:, 16 + T * E1 * i:16 + T * E1 * (i + 1)], t=T) for i in range(2)]
            first_max(es, E1, T, e1, one[0], c1)
            v.scalar_tensor_tensor(out=es, in0=one[0], scalar=-HUGE, in1=es, op0=ALU.mult, op1=ALU.add)\
             .then_inc(c1.sem, 1)
            v.wait_ge(c1.sem, c1.next())
            first_max(es, E1, T, e2, one[1], c1)
            v.tensor_tensor(pick[0][:, 0:T], e2, e1, ALU.subtract).then_inc(ex1_in.sem, 1)
            v.wait_ge(ex1_out.sem, 2)
            v.tensor_scalar(w1, pick[1][:, 0:T], 1.0, None, ALU.add).then_inc(c1.sem, 1)
            v.wait_ge(c1.sem, c1.next())
            v.reciprocal(w1, w1).then_inc(c1.sem, 1)
            v.wait_ge(c1.sem, c1.next())
            v.tensor_tensor(w2, pick[1][:, 0:T], w1, ALU.mult).then_inc(c1.sem, 1)
            v.wait_ge(c1.sem, c1.next())
            v.tensor_tensor(w1, w1, psel, ALU.mult).then_inc(c1.sem, 1)
            v.wait_ge(c1.sem, c1.next())
            v.tensor_tensor(w2, w2, psel, ALU.mult).then_inc(c1.sem, 1)
            v.wait_ge(c1.sem, c1.next())
            both = split(pick[0][:, 48:48 + T * E1], t=T)
            tmp = split(pick[0][:, 80:80 + T * E1], t=T)
            v.tensor_tensor(both, one[0], one[1], ALU.add).then_inc(c1.sem, 1)
            v.wait_ge(c1.sem, c1.next())
            v.tensor_tensor(one[0], one[0], spread(w1, 2, E1), ALU.mult).then_inc(c1.sem, 1)
            v.wait_ge(c1.sem, c1.next())
            v.tensor_tensor(tmp, one[1], spread(w2, 2, E1), ALU.mult).then_inc(c1.sem, 1)
            v.wait_ge(c1.sem, c1.next())
            v.tensor_tensor(one[0], one[0], tmp, ALU.add).then_inc(c1.sem, 1)
            v.wait_ge(c1.sem, c1.next())
            for g in range(G1):
                v.tensor_tensor(mask_of(NE1)[:, :, g * E1:(g + 1) * E1], both, spread(gone[:, :, g], 2, E1), ALU.mult)\
                 .then_inc(mask1.sem, 1)
                v.tensor_tensor(gate[:, g * E1 * T:(g + 1) * E1 * T].rearrange("p (e t) -> p t e", t=T), one[0],
                                spread(gone[:, :, g], 2, E1), ALU.mult).then_inc(c1.sem, 1)
                v.wait_ge(c1.sem, c1.next())
            v.wait_ge(mask1.sem, G1)
            set_places(NE1, cum1_mm).then_inc(c1.sem, 1)
            v.wait_ge(c1.sem, c1.next())
            most, more = col[7][:, 0:1], small[:, 313:320]
            v.tensor_reduce(most, bank[3][:, T * NE1:(T + 1) * NE1], AX_X, ALU.max).then_inc(c1.sem, 1)
            v.wait_ge(c1.sem, c1.next())
            v.tensor_scalar(more, iota[:, 0:7], float(C), None, ALU.mult).then_inc(c1.sem, 1)
            v.wait_ge(c1.sem, c1.next())
            v.tensor_scalar(more, more, most, None, ALU.is_lt).then_inc(c1.sem, 1)
            v.wait_ge(c1.sem, c1.next())
            v.tensor_reduce(most, more, AX_X, ALU.add).then_inc(c1.sem, 1)
            v.wait_ge(c1.sem, c1.next())
            v.tensor_scalar(rounds_i[:, :], most, 1.0, None, ALU.add).then_inc(places1.sem, 1)
            v.wait_ge(places1.sem, 1)
            round1(0)
            n_rounds = v.value_load(rounds_i[0:1, 0:1], min_val=1, max_val=S // C)
            with v.If(n_rounds > 1):
                with v.Fori(1, n_rounds) as r:
                    v.tensor_scalar(place[:, 0:NE1 * T], place[:, 0:NE1 * T], -float(C), None, ALU.add)\
                     .then_inc(next_round.sem, 1)
                    v.wait_ge(next_round.sem, r)
                    v.nop(nofuse=True)
                    round1(r * RUNS1)
            v.wait_ge(ex1["added"].sem, n_rounds * (NE1 // 2 * 8))
            v.nop(nofuse=True)
            for t in range(T):
                moments(t, D, h, c1).then_inc(h2_var.sem, 1)
                v.wait_ge(h2_var.sem, h2_var.at(t + 1))
            v.wait_ge(h2_std.sem, h2_std.at(1))
            v.reciprocal(rstd[:, 0:T], std[:, 0:T]).then_inc(c1.sem, 1)
            v.wait_ge(c1.sem, c1.next())
            v.wait_ge(ln2_in.sem, 32)
            for t in range(T):
                ins = layer_norm(h[:, t, :], h[:, t, :], ln2g, ln2b, t, c1)
                ins.then_inc(h_tiles.sem, 1)
                v.wait_ge(h_tiles.sem, t + 1)
            v.memset(col[11], 0.0).then_inc(layer_done.sem, 1)

            v.wait_ge(gains_in.sem, 32 * LAYERS)
            with v.Fori(0, LAYERS) as l:
                c = Steps(dve2, l * DVE2)

                def scaled(sg, dst, l=l):
                    v.wait_ge(sg["std"].sem, sg["std"].at(1, l))
                    v.reciprocal(rstd[:, 0:T], std[:, 0:T]).then_inc(c.sem, 1)
                    v.wait_ge(c.sem, c.next())
                    for t in range(T):
                        v.tensor_scalar(dst[:, t, :], h[:, t, :], rstd[:, t:t + 1], None, ALU.mult)\
                         .then_inc(sg["x"].sem, 1)

                v.tensor_copy(layer_cols, all_cols[:, bass.ds(l * 33, 33)]).then_inc(cols_ready.sem, 1)
                v.wait_ge(cols_ready.sem, cols_ready.at(1, l))
                v.tensor_scalar(nsink, sink, -1.0, None, ALU.mult).then_inc(c.sem, 1)
                v.wait_ge(c.sem, c.next())
                scaled(nrm, xn)
                take_chunks(nrm, xT, K, gains[:, 0, :], l)
                v.wait_ge(second_in.sem, second_in.at(16, l))

                def rotate(n, x, dst, cos, sin, done, count, part=slice(0, P), apart=None):
                    v.tensor_tensor(rot_tmp[part, :], bank[n % 8][part, :], tab(SECOND_AT, sin)[part, :], ALU.mult)\
                     .then_inc(took2_v.sem, 1)
                    v.tensor_tensor(dst, x, tab(SECOND_AT, cos)[part, :], ALU.mult).then_inc(c.sem, 1)
                    v.wait_ge(c.sem, c.next())
                    v.wait_ge(took2_v.sem, took2_v.at(nth(PROJ2, PROJ2_ACT, n), l))
                    own = part
                    if apart is not None:
                        v.tensor_tensor(apart, dst[HD:P, :], rot_tmp[HD:P, :], ALU.add)
                        own, dst = slice(0, HD), dst[0:HD, :]
                    v.tensor_tensor(dst, dst, rot_tmp[own, :], ALU.add).then_inc(done.sem, 1)
                    v.wait_ge(done.sem, done.at(count, l))

                low = slice(HD, MLA_D)
                roped = 0
                for n, (w, i) in enumerate(PROJ2):
                    if w == "ssq":
                        v.wait_ge(took2_a.sem, took2_a.at(nth(PROJ2, PROJ2_ACT, n), l))
                        v.reciprocal(rs[:, i, :], rs[:, i, :]).then_inc(c.sem, 1)
                        v.wait_ge(c.sem, c.next())
                        for k in (2,) if i else (0, 1):
                            v.scalar_tensor_tensor(out=cq[:, k, :], in0=cq[:, k, :], scalar=lat_g[:, k:k + 1],
                                                   in1=rs[:, i, :], op0=ALU.mult, op1=ALU.mult)\
                             .then_inc(lat_ready.sem, 1)
                    if w in PROJ2_ACT:
                        continue
                    v.wait_ge(proj2.sem, proj2.at(n + 1, l))
                    b = bank[n % 8]
                    if w == "krrot":
                        rotate(n, kr_raw[low, :], kr_new[low, :], "cos_mla", "sin_mla", kpe_ready, 1, low)
                    elif w in ("uqrot", "swarot"):
                        roped += 1
                        x, names, part = ((qk2[low, 8 + i, :], ("cos_mla", "sin_mla"), low) if w == "uqrot" else
                                          (qk2[:, 4 + i, :], ("cos", "sin"), slice(0, P)))
                        rotate(n, x, x, *names, rope2, roped, part, cq[HD:P, 2, :] if (w, i) == ("swarot", 3) else None)
                    elif w == "uk":
                        v.tensor_copy(qk2[0:HD, 14 + 2 * i, :], b[0:HD, :])
                        v.tensor_copy(qk2[0:HD, 15 + 2 * i, :], b[HD:P, :]).then_inc(took2_v.sem, 1)
                    else:
                        v.tensor_copy(va[:, i, :], b[:, 0:384]).then_inc(took2_v.sem, 1)
                attention(HEADS2, att2, table2, place2, c, l)

                v.wait_ge(gnm["std"].sem, gnm["std"].at(1, l))
                v.reciprocal(rstd, std).then_inc(c.sem, 1)
                v.wait_ge(c.sem, c.next())
                for t in range(T):
                    for g, (c0, c1_) in enumerate(GROUPS2):
                        ins = v.tensor_scalar(o2[:, t, c0:c1_], o2[:, t, c0:c1_],
                                              rstd[:, g * T + t:g * T + t + 1], None,
                                              ALU.mult)
                    ins.then_inc(gnm["x"].sem, 1)
                take_chunks(gnm, oT2, K, gains[:, 1, :], l)
                for n in range(2 * T):
                    t, half = divmod(n, 2)
                    hs = h[:, t, half * 512:(half + 1) * 512]
                    v.wait_ge(wo2_mm.sem, wo2_mm.at(n + 1, l))
                    v.tensor_tensor(hs, hs, bank[n][:, :], ALU.add).then_inc(h2_sum.sem, 1)
                    if half:
                        v.wait_ge(fnm_std.sem, fnm_std.at(t + 1, l))
                        v.reciprocal(rstd[:, t:t + 1], std[:, t:t + 1]).then_inc(c.sem, 1)
                        v.wait_ge(c.sem, c.next())
                        v.wait_ge(h2_sum.sem, h2_sum.at(n + 1, l))
                        v.tensor_scalar(xn[:, t, :], h[:, t, :], rstd[:, t:t + 1], None, ALU.mult)\
                         .then_inc(fnm["x"].sem, 1)
                take_chunks(fnm, xT, K, gains[:, 2, :], l)

                v.wait_ge(lgT2_mm.sem, lgT2_mm.at(1, l))
                v.tensor_copy(lgT[0:NE2, :], bank[0][0:NE2, :]).then_inc(lgT2_ok.sem, 1)
                v.wait_ge(lg2_mm.sem, lg2_mm.at(1, l))
                lg = split(bank[1][:, 0:T * NE2], t=T)
                low_, ex, aff = (split(pick[i][:, 0:T * NE2], t=T) for i in range(3))
                v.tensor_reduce(col[0], lg, AX_X, ALU.max).then_inc(c.sem, 1)
                v.wait_ge(c.sem, c.next())
                v.tensor_tensor(low_, lg, spread(col[0], 2, NE2), ALU.subtract).then_inc(ex2_in.sem, 1)
                v.wait_ge(ex2_out.sem, ex2_out.at(1, l))
                v.tensor_reduce(col[1], ex, AX_X, ALU.add).then_inc(c.sem, 1)
                v.wait_ge(c.sem, c.next())
                v.reciprocal(col[1], col[1]).then_inc(c.sem, 1)
                v.wait_ge(c.sem, c.next())
                v.tensor_tensor(aff, ex, spread(col[1], 2, NE2), ALU.mult).then_inc(aff_ready.sem, 1)
                v.wait_ge(aff_ready.sem, aff_ready.at(1, l))
                v.tensor_copy(gate[:, 0:NE2 * T].rearrange("p (e t) -> p t e", t=T), aff).then_inc(c.sem, 1)
                v.wait_ge(c.sem, c.next())
                v.wait_ge(affT_mm.sem, affT_mm.at(1, l))
                v.tensor_copy(affT[0:NE2, :], bank[1][0:NE2, :]).then_inc(c.sem, 1)
                v.wait_ge(c.sem, c.next())
                v.nop(nofuse=True)
                for i in range(CAP2 // 8):
                    src = workT if i else affT
                    v.max(top8[0:NE2, :], src[0:NE2, :]).then_inc(c.sem, 1)
                    v.wait_ge(c.sem, c.next())
                    v.nop(nofuse=True)
                    v.match_replace(workT[0:NE2, :], top8[0:NE2, :], src[0:NE2, :], -1.0).then_inc(c.sem, 1)
                    v.wait_ge(c.sem, c.next())
                    v.nop(nofuse=True)
                v.tensor_scalar(maskT[0:NE2, :], workT[0:NE2, :], 0.0, None, ALU.is_lt).then_inc(maskT_ready.sem, 1)
                v.wait_ge(mask_mm.sem, mask_mm.at(1, l))
                v.tensor_copy(mask_of(NE2), split(bank[2][:, 0:T * NE2], t=T)).then_inc(mask2.sem, 1)
                set_places(NE2, cum2_mm, l).then_inc(places2.sem, 1)
                v.wait_ge(places2.sem, places2.at(1, l))
                v.nop(nofuse=True)
                expert_round(ex2, l * (NE2 // 2), NE2 // 2, gains[:, 2, :])
                v.wait_ge(ex2["added"].sem, ex2["added"].at((l + 1) * (NE2 // 2 * 8)))
                v.memset(col[11], 0.0).then_inc(layer_done.sem, 1)
            assert c.n == DVE2, c.n

            v.wait_ge(nrm["std"].sem, nrm["std"].at(1, LAYERS))
            c3 = Steps(sem("dve_fin"))
            v.reciprocal(rstd[:, 0:T], std[:, 0:T]).then_inc(c3.sem, 1)
            v.wait_ge(c3.sem, c3.next())
            v.wait_ge(fin_in.sem, 16)
            for t in range(T):
                v.tensor_scalar(fin_o[:, t, :], h[:, t, :], rstd[:, t:t + 1], None, ALU.mult).then_inc(c3.sem, 1)
                v.wait_ge(c3.sem, c3.next())
                v.tensor_tensor(fin_o[:, t, :], fin_o[:, t, :], fin_g, ALU.mult).then_inc(fin_ready.sem, 1)
    return nc


def _laid_out(i):
    np_ = {n: np.asarray(v) for n, v in i.items()}
    same = ("x", "positions", "w_in", "sgu_ln_g", "sgu_ln_b", "b_spatial", "w_out", "ln1_g", "ln1_b", "b_group",
            "b_expert", "w_gate_up", "w_down", "ln2_g", "ln2_b", "mla_w_uq_2", "swa_sink_2", "w_out_2", "w_router_2",
            "w_gate_2", "w_up_2", "w_down_2", "final_norm_2")
    o = {n: np_[n] for n in same}
    o["xT"] = np_["x"][0].T
    o["w_spatialT"] = np_["w_spatial"][0].transpose(0, 2, 1)
    o["w_router1"] = np.concatenate([np_["w_group"][0], np_["w_expert"][0].transpose(1, 0, 2).reshape(D, NE1)], 1)
    w = np_["w_in_2"]
    aq, ak, av, bq, bkv, kr, cq, ck, cv = np.split(w, (256, 512, 768, 1024, 1152, 1184, 1568, 1696), axis=-1)
    cq = cq.reshape(LAYERS, D, 2, 3, HD).transpose(0, 1, 3, 2, 4).reshape(LAYERS, D, 6 * HD)
    o["w_in_2"] = np.concatenate([aq, ak, cq, ck, bq, bkv, kr, av, cv], -1)
    u = np_["mla_w_ukv_2"].reshape(LAYERS, P, MLA_H, 2, HD).transpose(0, 1, 3, 2, 4)
    o["w_ukv"] = u.reshape(LAYERS, P, 2 * MLA_H * HD)
    o["gains"] = np.concatenate([np_[n].reshape(LAYERS, -1, P).transpose(0, 2, 1) for n in (
        "attn_norm_2", "group_norm_2", "ffn_norm_2", "mla_q_norm_2", "mla_kv_norm_2")], -1)
    o["rpb"] = np.pad(np_["na_rpb_2"][..., ::-1].reshape(LAYERS, -1), ((0, 0), (RPB_PAD, RPB_PAD))).reshape(-1)
    o["base_const"], o["first_const"], o["second_const"] = shape_constants()
    return {n: np.ascontiguousarray(v) for n, v in o.items()}


def kernel(**inputs):
    import concourse.bacc as bacc
    from concourse.bass_utils import run_bass_kernel_spmd

    arrays = _laid_out(inputs)
    nc = bacc.Bacc("TRN2", target_bir_lowering=False, num_devices=1)
    aps = {n: nc.dram_tensor(f"in_{n}", v.shape, mybir.dt.from_np(v.dtype), kind="ExternalInput").ap()
           for n, v in arrays.items()}
    out = nc.dram_tensor("out_0", (1, S, D), F32, kind="ExternalOutput").ap()
    build(nc, aps, out)
    r = run_bass_kernel_spmd(nc, [{f"in_{n}": v for n, v in arrays.items()}], core_ids=[0])
    return r.results[0]["out_0"]
```
